# Optimizing a Trainium2 kernel written in Bass

```python
import math
import jax, jax.numpy as jnp
from jax import lax
import numpy as np

D_MODEL = 1024
BATCH = 1
SEQ = 256
DEPTH = 2

HEAD_DIM = 64
RMS_EPS = 1e-6
A_WIDTH = D_MODEL // 2
A_HEADS = A_WIDTH // HEAD_DIM
DECAY_LORA = 64
AAA_LORA = 64
GATE_LORA = 128
GN_EPS = 64e-5
B_WIDTH = D_MODEL // 2
B_GROUPS = 4
B_GROUP_DIM = B_WIDTH // B_GROUPS
CHUNK = 128
LN_EPS = 1e-5
OFF_K = A_WIDTH
OFF_V = 2 * A_WIDTH
OFF_W = 3 * A_WIDTH
OFF_A = OFF_W + DECAY_LORA
OFF_G = OFF_A + AAA_LORA
A_COLS = OFF_G + GATE_LORA
IN_COLS = A_COLS + 2 * B_WIDTH
Q_HEADS = D_MODEL // HEAD_DIM
KV_HEADS = 4
Q_PER_KV = Q_HEADS // KV_HEADS
WINDOW = 128
ROPE_THETA = 10000.0
QKV_COLS = (Q_HEADS + 2 * KV_HEADS) * HEAD_DIM
D_FF = 2816
N_EVEN = (DEPTH + 1) // 2
N_ODD = DEPTH // 2

kernel_name = "hybrid_rwkv7_gmlp_swa_macaron"

def rms_norm(x, gain, eps=RMS_EPS):
    xf = x.astype(jnp.float32)
    y = xf * lax.rsqrt(jnp.mean(xf * xf, axis=-1, keepdims=True) + eps)
    return (y * gain.astype(jnp.float32)).astype(x.dtype)

def layer_norm(x, gain, bias, eps=LN_EPS):
    xf = x.astype(jnp.float32)
    mu = jnp.mean(xf, axis=-1, keepdims=True)
    var = jnp.mean(jnp.square(xf - mu), axis=-1, keepdims=True)
    return ((xf - mu) * lax.rsqrt(var + eps) * gain.astype(jnp.float32) + bias.astype(jnp.float32)).astype(x.dtype)

def swiglu_ffn(x, w_gate, w_up, w_down):
    return (jax.nn.silu(x @ w_gate) * (x @ w_up)) @ w_down

def token_shift(z):
    return jnp.pad(z, ((0, 0), (1, 0), (0, 0)))[:, :-1]

def rope(x, cos, sin):
    x1, x2 = jnp.split(x, 2, axis=-1)
    return jnp.concatenate([x1 * cos - x2 * sin, x2 * cos + x1 * sin], axis=-1).astype(x.dtype)

def rwkv7_scan(r, w, k, v, a, b):
    def step(S, inp):
        r_t, w_t, k_t, v_t, a_t, b_t = inp
        sa = jnp.einsum('bhij,bhj->bhi', S, a_t)
        S = S * w_t[:, :, None, :] + sa[..., None] * b_t[:, :, None, :] + v_t[..., None] * k_t[:, :, None, :]
        return S, jnp.einsum('bhij,bhj->bhi', S, r_t)
    xs = tuple(jnp.moveaxis(t.astype(jnp.float32), 1, 0) for t in (r, w, k, v, a, b))
    bsz, _, heads, dim = r.shape
    s0 = jnp.zeros((bsz, heads, dim, dim), jnp.float32)
    _, y = lax.scan(step, s0, xs)
    return jnp.moveaxis(y, 0, 1)

def rwkv_gmlp_mixer(h, w_in, mu_shift, w0, w_decay_up, a0, w_aaa_up, w_gate_up, k_k, k_a, r_k,
                    gn_gain, gn_bias, sg_ln_gain, sg_ln_bias, w_spatial, b_spatial, w_out):
    bsz, t_len, _ = h.shape
    z = h @ w_in
    z_a, z_b = z[..., :A_COLS], z[..., A_COLS:]

    z_a = z_a + (token_shift(z_a) - z_a) * mu_shift
    r, k, v, xw, xa, xg = jnp.split(z_a, [OFF_K, OFF_V, OFF_W, OFF_A, OFF_G], axis=-1)
    w_log = -jax.nn.softplus(-(w0 + jnp.tanh(xw) @ w_decay_up)) - 0.5
    decay = jnp.exp(-jnp.exp(w_log.astype(jnp.float32)))
    iclr = jax.nn.sigmoid(a0 + xa @ w_aaa_up)
    gate = jax.nn.sigmoid(xg) @ w_gate_up
    heads = lambda t: t.reshape(bsz, t_len, A_HEADS, HEAD_DIM)
    kk = heads(k * k_k).astype(jnp.float32)
    kk = kk / jnp.maximum(jnp.sqrt(jnp.sum(kk * kk, axis=-1, keepdims=True)), 1e-12)
    k = k * (1.0 + (iclr - 1.0) * k_a)
    r_h, k_h, v_h, a_h = heads(r), heads(k), heads(v), heads(iclr)
    y = rwkv7_scan(r_h, heads(decay), k_h, v_h, -kk, kk * a_h.astype(jnp.float32))
    mu = jnp.mean(y, axis=-1, keepdims=True)
    var = jnp.mean(jnp.square(y - mu), axis=-1, keepdims=True)
    y = ((y - mu) * lax.rsqrt(var + GN_EPS)).reshape(bsz, t_len, A_WIDTH)
    y = (y * gn_gain.astype(jnp.float32) + gn_bias.astype(jnp.float32)).astype(h.dtype)
    bonus = (jnp.sum(r_h * k_h * r_k, axis=-1, keepdims=True) * v_h).reshape(bsz, t_len, A_WIDTH)
    y_a = (y + bonus) * gate

    z_b = jax.nn.gelu(z_b, approximate=False)
    u, s = jnp.split(z_b, 2, axis=-1)
    s = layer_norm(s, sg_ln_gain, sg_ln_bias)
    s = s.reshape(bsz, t_len // CHUNK, CHUNK, B_GROUPS, B_GROUP_DIM)
    causal = jnp.tril(jnp.ones((CHUNK, CHUNK), dtype=bool))
    w_s = jnp.where(causal[None], w_spatial, jnp.zeros((), w_spatial.dtype))
    s = jnp.einsum('gts,bcsgd->bctgd', w_s, s) + b_spatial.T[None, None, :, :, None]
    y_b = u * s.reshape(bsz, t_len, B_WIDTH)

    return jnp.concatenate([y_a, y_b], axis=-1) @ w_out

def swa_sink_attention(h, cos, sin, w_qkv, b_qkv, q_norm, k_norm, sinks, w_o, b_o):
    bsz, t_len, _ = h.shape
    nb = t_len // WINDOW
    qkv = h @ w_qkv + b_qkv
    q, k, v = jnp.split(qkv, [Q_HEADS * HEAD_DIM, (Q_HEADS + KV_HEADS) * HEAD_DIM], axis=-1)
    q = rope(rms_norm(q.reshape(bsz, t_len, Q_HEADS, HEAD_DIM), q_norm), cos, sin)
    k = rope(rms_norm(k.reshape(bsz, t_len, KV_HEADS, HEAD_DIM), k_norm), cos, sin)
    v = v.reshape(bsz, t_len, KV_HEADS, HEAD_DIM)

    q_blk = q.reshape(bsz, nb, WINDOW, KV_HEADS, Q_PER_KV, HEAD_DIM).transpose(1, 0, 2, 3, 4, 5)

    def band(t):
        tb = t.reshape(bsz, nb, WINDOW, KV_HEADS, HEAD_DIM)
        prev = jnp.pad(tb, ((0, 0), (1, 0), (0, 0), (0, 0), (0, 0)))[:, :-1]
        return jnp.concatenate([prev, tb], axis=2).transpose(1, 0, 2, 3, 4)

    k_band, v_band = band(k), band(v)
    qi = jnp.arange(WINDOW)[:, None]
    kj = jnp.arange(2 * WINDOW)[None, :]
    dist = qi + WINDOW - kj
    in_window = (dist >= 0) & (dist < WINDOW)
    scale = HEAD_DIM ** -0.5
    sink = sinks.astype(jnp.float32).reshape(KV_HEADS, Q_PER_KV)[None, :, :, None]

    def block(args):
        n, qb, kb, vb = args
        s = jnp.einsum('bqhgd,bkhd->bhgqk', qb, kb, preferred_element_type=jnp.float32) * scale
        valid = in_window & ((n > 0) | (kj >= WINDOW))
        s = jnp.where(valid, s, -jnp.inf)
        m = jnp.maximum(jnp.max(s, axis=-1), sink)
        p = jnp.exp(s - m[..., None])
        denom = jnp.sum(p, axis=-1) + jnp.exp(sink - m)
        o = jnp.einsum('bhgqk,bkhd->bqhgd', p, vb.astype(jnp.float32))
        return (o / denom.transpose(0, 3, 1, 2)[..., None]).astype(qb.dtype)

    o = lax.map(block, (jnp.arange(nb), q_blk, k_band, v_band))
    o = o.transpose(1, 0, 2, 3, 4, 5).reshape(bsz, t_len, Q_HEADS * HEAD_DIM)
    return o @ w_o + b_o

def setup_inputs(seed: int = 0) -> dict:
    key = jax.random.key(seed)
    ks = iter(jax.random.split(key, 40))
    nrm = lambda shape, scale: scale * jax.random.normal(next(ks), shape, jnp.float32)
    d = D_MODEL
    inp = {}
    inp["x"] = nrm((BATCH, SEQ, d), 1.0)
    inp["positions"] = jnp.broadcast_to(jnp.arange(SEQ, dtype=jnp.int32)[None, :], (BATCH, SEQ)).astype(jnp.int32)
    inp["ffn1_norm"] = 1.0 + nrm((DEPTH, d), 0.1)
    inp["ffn1_w_gate"] = nrm((DEPTH, d, D_FF), d ** -0.5)
    inp["ffn1_w_up"] = nrm((DEPTH, d, D_FF), d ** -0.5)
    inp["ffn1_w_down"] = nrm((DEPTH, D_FF, d), D_FF ** -0.5)
    inp["mix_norm"] = 1.0 + nrm((DEPTH, d), 0.1)
    inp["ffn2_norm"] = 1.0 + nrm((DEPTH, d), 0.1)
    inp["ffn2_w_gate"] = nrm((DEPTH, d, D_FF), d ** -0.5)
    inp["ffn2_w_up"] = nrm((DEPTH, d, D_FF), d ** -0.5)
    inp["ffn2_w_down"] = nrm((DEPTH, D_FF, d), D_FF ** -0.5)
    inp["ab_w_in"] = nrm((N_EVEN, d, IN_COLS), d ** -0.5)
    inp["ab_mu_shift"] = jax.random.uniform(next(ks), (N_EVEN, A_COLS), jnp.float32)
    inp["rwkv_w0"] = -2.0 + nrm((N_EVEN, A_WIDTH), 0.7)
    inp["rwkv_w_decay_up"] = nrm((N_EVEN, DECAY_LORA, A_WIDTH), 0.5 * DECAY_LORA ** -0.5)
    inp["rwkv_a0"] = nrm((N_EVEN, A_WIDTH), 0.1)
    inp["rwkv_w_aaa_up"] = nrm((N_EVEN, AAA_LORA, A_WIDTH), 0.5 * AAA_LORA ** -0.5)
    inp["rwkv_w_gate_up"] = nrm((N_EVEN, GATE_LORA, A_WIDTH), GATE_LORA ** -0.5)
    inp["rwkv_k_k"] = 0.85 + nrm((N_EVEN, A_WIDTH), 0.1)
    inp["rwkv_k_a"] = 1.0 + nrm((N_EVEN, A_WIDTH), 0.1)
    inp["rwkv_r_k"] = nrm((N_EVEN, A_HEADS, HEAD_DIM), 0.1)
    inp["rwkv_gn_gain"] = 1.0 + nrm((N_EVEN, A_WIDTH), 0.1)
    inp["rwkv_gn_bias"] = nrm((N_EVEN, A_WIDTH), 0.02)
    inp["sg_ln_gain"] = 1.0 + nrm((N_EVEN, B_WIDTH), 0.1)
    inp["sg_ln_bias"] = nrm((N_EVEN, B_WIDTH), 0.02)
    inp["sg_w_spatial"] = nrm((N_EVEN, B_GROUPS, CHUNK, CHUNK), 0.5 * CHUNK ** -0.5)
    inp["sg_b_spatial"] = 1.0 + nrm((N_EVEN, B_GROUPS, CHUNK), 0.1)
    inp["ab_w_out"] = nrm((N_EVEN, A_WIDTH + B_WIDTH, d), (A_WIDTH + B_WIDTH) ** -0.5)
    inp["attn_w_qkv"] = nrm((N_ODD, d, QKV_COLS), d ** -0.5)
    inp["attn_b_qkv"] = nrm((N_ODD, QKV_COLS), 0.02)
    inp["attn_q_norm"] = 1.0 + nrm((N_ODD, HEAD_DIM), 0.1)
    inp["attn_k_norm"] = 1.0 + nrm((N_ODD, HEAD_DIM), 0.1)
    inp["attn_sinks"] = nrm((N_ODD, Q_HEADS), 1.0)
    inp["attn_w_o"] = nrm((N_ODD, Q_HEADS * HEAD_DIM, d), (Q_HEADS * HEAD_DIM) ** -0.5)
    inp["attn_b_o"] = nrm((N_ODD, d), 0.02)
    return inp

def reference(x, positions, ffn1_norm, ffn1_w_gate, ffn1_w_up, ffn1_w_down, mix_norm,
              ffn2_norm, ffn2_w_gate, ffn2_w_up, ffn2_w_down,
              ab_w_in, ab_mu_shift, rwkv_w0, rwkv_w_decay_up, rwkv_a0, rwkv_w_aaa_up, rwkv_w_gate_up,
              rwkv_k_k, rwkv_k_a, rwkv_r_k, rwkv_gn_gain, rwkv_gn_bias,
              sg_ln_gain, sg_ln_bias, sg_w_spatial, sg_b_spatial, ab_w_out,
              attn_w_qkv, attn_b_qkv, attn_q_norm, attn_k_norm, attn_sinks, attn_w_o, attn_b_o):
    inv_freq = ROPE_THETA ** (-jnp.arange(0, HEAD_DIM, 2, dtype=jnp.float32) / HEAD_DIM)
    ang = positions.astype(jnp.float32)[..., None] * inv_freq
    cos = jnp.cos(ang)[:, :, None, :]
    sin = jnp.sin(ang)[:, :, None, :]
    for l in range(DEPTH):
        h = rms_norm(x, ffn1_norm[l])
        x = x + 0.5 * swiglu_ffn(h, ffn1_w_gate[l], ffn1_w_up[l], ffn1_w_down[l])
        h = rms_norm(x, mix_norm[l])
        i = l // 2
        if l % 2 == 0:
            x = x + rwkv_gmlp_mixer(h, ab_w_in[i], ab_mu_shift[i], rwkv_w0[i], rwkv_w_decay_up[i],
                                    rwkv_a0[i], rwkv_w_aaa_up[i], rwkv_w_gate_up[i], rwkv_k_k[i],
                                    rwkv_k_a[i], rwkv_r_k[i], rwkv_gn_gain[i], rwkv_gn_bias[i],
                                    sg_ln_gain[i], sg_ln_bias[i], sg_w_spatial[i], sg_b_spatial[i],
                                    ab_w_out[i])
        else:
            x = x + swa_sink_attention(h, cos, sin, attn_w_qkv[i], attn_b_qkv[i], attn_q_norm[i],
                                       attn_k_norm[i], attn_sinks[i], attn_w_o[i], attn_b_o[i])
        h = rms_norm(x, ffn2_norm[l])
        x = x + 0.5 * swiglu_ffn(h, ffn2_w_gate[l], ffn2_w_up[l], ffn2_w_down[l])
    return x


_drawn_inputs = setup_inputs


def setup_inputs(seed=0):
    import zlib

    import numpy as np

    out = dict(_drawn_inputs(seed))
    spreads = {}
    factors = {'rwkv_w_decay_up': 3.319,
     'rwkv_a0': 3.249,
     'rwkv_k_k': 4.567,
     'rwkv_gn_bias': 7.501,
     'sg_ln_gain': 3.854,
     'sg_ln_bias': 8.0,
     'attn_b_qkv': 3.706,
     'attn_q_norm': 4.385,
     'attn_k_norm': 3.631,
     'attn_sinks': 16.457,
     'attn_b_o': 3.628}
    for name, (base, spread) in spreads.items():
        noise = np.random.default_rng([zlib.crc32(name.encode()), seed]).standard_normal(out[name].shape)
        drawn = base * np.exp(spread * noise) if base else spread * noise
        out[name] = __import__('jax').numpy.asarray(drawn.astype(out[name].dtype))
    for name, factor in factors.items():
        out[name] = (out[name] * factor).astype(out[name].dtype)
    return out
```

```python
from contextlib import ExitStack

import concourse.bass as bass
from concourse import mybir

F32 = mybir.dt.float32
F32R = mybir.dt.float32r
I32 = mybir.dt.int32
ALU = mybir.AluOpType
ACT = mybir.ActivationFunctionType
AX = mybir.AxisListType.X

P = 128
D = 1024
T = 256
KD = D // P
FF = 2816
KF = FF // P
SUB = KF // 2
HD = 64
AH = 8
AW = 512
CT = AW // P
ZA = 14
ZB = 8
CH = 64
NC = T // CH
QH = 16
RMS_EPS, GN_EPS, LN_EPS = 1e-6, 64e-5, 1e-5
KAPPA = 0.6065306597126334

PCOLS = {}
_at = 0
for _name, _n in (("ffn1_norm0", 8), ("ffn1_norm1", 8), ("mix_norm0", 8), ("mix_norm1", 8), ("ffn2_norm0", 8),
                  ("ffn2_norm1", 8), ("mu", ZA), ("w0", 4), ("a0", 4), ("k_k", 4), ("k_a", 4), ("r_k", 4),
                  ("gn_gain", 4), ("gn_bias", 4), ("ln_gain", 4), ("ln_bias", 4), ("b_qkv", 12), ("q_norm", 1),
                  ("k_norm", 1), ("b_o", 8), ("inv_freq", 1), ("sinks", QH)):
    PCOLS[_name] = (_at, _n)
    _at += _n
NPAR = _at

CCOLS = {}
_at = 0
for _name, _n in (("ident", P), ("head_ones", P), ("rope_swap", P), ("mask_pair", 4 * P), ("mask16", P),
                  ("mask16T", P), ("mask32", P), ("mask64", P), ("causal", P), ("window", 2 * P), ("restart", T),
                  ("pick", 32), ("spread", CT * P)):
    CCOLS[_name] = (_at, _n)
    _at += _n
NCON = _at

LINEARS = (("gu", 22, 8, 0), ("down", 8, SUB, 0), ("w_in", 11, 8, 0), ("w_out", 4, 8, 0), ("gu", 22, 8, 1),
           ("down", 8, SUB, 1), ("gu", 22, 8, 2), ("down", 8, SUB, 2), ("qkv", 6, 8, 0), ("w_o", 4, 8, 0),
           ("gu", 22, 8, 3), ("down", 8, SUB, 3))
FIRST = [sum(x[1] for x in LINEARS[:n]) for n in range(len(LINEARS))]


def build(nc, xT, gu_w, down_w, w_in, w_out, w_qkv, w_o, params, consts, positions, w_lora, w_gate,
          w_spatialT, b_spatial, out):
    with ExitStack() as ctx:
        def sb(name, shape, dt=F32):
            return ctx.enter_context(nc.sbuf_tensor(name, shape, dt))

        def ps(name):
            return ctx.enter_context(nc.psum_tensor(name, [P, 512], F32))

        sems = {}

        def S(name):
            if name not in sems:
                sems[name] = ctx.enter_context(nc.semaphore(name))
            return sems[name]

        raw = sb("raw", [P, 4, 2 * SUB * P])
        w_hi = sb("w_hi", [P, 4, SUB * P], F32R)
        w_lo = sb("w_lo", [P, 4, SUB * P], F32R)
        x = sb("x", [P, KD, T])
        par = sb("par", [P, NPAR])
        con = sb("con", [P, NCON])
        sq = sb("sq", [P, 2, T])
        ssq = sb("ssq", [P, 2, T])
        root = sb("root", [P, T])
        rB = sb("rB", [P, T])
        ones = sb("ones", [P, P])
        eps = sb("eps", [P, 4])
        base = nc.sbuf_base
        base += -base % 32
        room = nc.sbuf_usable_end - base
        arena = sb("arena", [P, room // 4 - 16])

        def at(name, off, shape, dt=F32):
            n = 4
            for s in shape[1:]:
                n *= s
            assert off % 32 == 0 and off + n <= room - 64, (name, off, n, room)
            return nc.alloc_sbuf_tensor_at(name, shape, dt, offset=base + off)

        KB = 1024
        TEMP = 0
        FREE = 8 * KB
        HOFF = FREE + (room - 64 - 8 * KB - 16 * KB - 44 * KB) // 32 * 32
        AHI = HOFF + 16 * KB
        ALO = AHI + 22 * KB
        pre = at("pre", TEMP, [P, 2, 2, T])
        sil = at("sil", TEMP + 4 * KB, [P, 2, T])
        act_f = at("act_f", TEMP + 6 * KB, [P, 2, T])
        h_hi = at("h_hi", HOFF, [P, KD, T], F32R)
        h_lo = at("h_lo", HOFF + 8 * KB, [P, KD, T], F32R)
        a_hi = at("a_hi", AHI, [P, KF, T], F32R)
        a_lo = at("a_lo", ALO, [P, KF, T], F32R)
        y_hi = a_hi[:, KF - KD:KF, :]
        y_lo = a_lo[:, 0:KD, :]

        lin = [ps(f"lin{i}") for i in range(4)]
        mix = [ps(f"mix{i}") for i in range(4)]
        banks = mix + lin

        def pc(name, j=0, n=1, rows=slice(0, P)):
            return par[rows, PCOLS[name][0] + j:PCOLS[name][0] + j + n]

        def cc(name):
            a, n = CCOLS[name]
            return con[:, a:a + n]

        ident = cc("ident")

        zz = at("zz", FREE, [P, ZA + ZB, T + 1])
        ZBYTES = (ZA + ZB) * (T + 1) * 4
        zs = at("zs", ALO + 8 * KB, [P, ZA, T])
        gt = at("gt", AHI, [P, 4, T])
        g_mean = at("g_mean", AHI + 4 * KB, [P, T])
        g_rstd = at("g_rstd", AHI + 5 * KB, [P, T])
        s_tok = at("s_tok", AHI + 6 * KB, [P, 2, AW])
        wsT = at("wsT", AHI + 10 * KB, [P, 4, P])
        bsp = at("bsp", AHI + 12 * KB, [P, 4, P])
        sd = at("sd", HOFF, [P, CT, T])
        cs = at("cs", HOFF + 4 * KB, [P, CT, T])
        ep = at("ep", HOFF + 8 * KB, [P, CT, T])
        ic = at("ic", HOFF + 12 * KB, [P, CT, T])
        kq = at("kq", AHI + 14 * KB, [P, CT, T])
        AR = at("AR", AHI + 4 * KB, [P, CT, 2, 2, P])
        th = at("th", ALO, [P, T])
        sgx = at("sgx", ALO + 3 * KB, [P, T])
        z_b_off = FREE + (ZA * (T + 1) * 4 + 31) // 32 * 32 + 32
        BT = at("BT", z_b_off, [P, CT, T])
        KT = at("KT", z_b_off + 4 * KB, [P, CT, T])
        bonus = at("bonus", z_b_off + 8 * KB, [P, CT, T])
        TM = at("TM", FREE, [P, 4, AW])
        Yc = at("Yc", FREE + 8 * KB, [P, CT, T])
        lora = at("lora", TEMP, [P, AW])
        wgate = at("wgate", TEMP + 2 * KB, [P, AW])
        St = at("St", TEMP + 4 * KB, [P, 3, CT, CH])
        pend = at("pend", TEMP + 7 * KB, [P, CT, NC])
        kfb = at("kfb", TEMP + 7 * KB + 128, [P, 4])
        AM = at("AM", ALO + 8 * KB, [P, 4, 4 * P])
        GH = at("GH", ALO + 8 * KB + 12 * KB, [P, 4, P])
        nb = [at(f"nb{i}", HOFF + 2 * KB * i, [P, 4, P]) for i in range(8)]
        Dm, DmT, M32, M64, D2, D2T, D4, D4T = nb
        Zt = at("Zt", AHI, [P, 4, P])
        Tt = at("Tt", AHI + 2 * KB, [P, 4, P])
        Xa = at("Xa", FREE + 12 * KB, [P, 4, P])
        akv = at("akv", AHI + 22 * KB - 8 * KB + 3 * KB, [P, 4, CH])
        ETs = at("ETs", AHI + 14 * KB, [P, 3, CT, CH])
        Fs = at("Fs", ALO, [P, 3, CT, CH])
        ysum = at("ysum", HOFF, [P, CT, T])
        ysq = at("ysq", HOFF + 4 * KB, [P, CT, T])
        yst = at("yst", HOFF + 8 * KB, [P, 2, T])
        qz = at("qz", FREE, [P, 12, T])
        cosT = at("cosT", FREE + 12 * KB, [P, T])
        sinT = at("sinT", FREE + 13 * KB, [P, T])
        posf = at("posf", FREE + 14 * KB, [P, T])
        posi = at("posi", FREE + 15 * KB, [P, T], I32)
        qr = at("qr", AHI, [P, 10, T])
        qsq = at("qsq", HOFF, [P, 10, T])
        v_tok = at("v_tok", AHI + 10 * KB, [P, 2, T])
        rq = at("rq", AHI + 12 * KB, [P, 2, QH])
        rk = at("rk", AHI + 13 * KB, [P, 2, T])
        trot = at("trot", ALO + 8 * KB, [P, 2, T])
        sc = at("sc", ALO + 10 * KB, [P, 2, 2, T])
        pT = at("pT", ALO + 14 * KB, [P, 2, 2, 2, P])
        sm = at("sm", ALO + 18 * KB, [P, 16, 16])
        att = at("att", TEMP, [P, 2, T])

        YSB = [(lin[0], lin[1]), (lin[2], lin[3]), (mix[0], mix[1])]

        block = ctx.enter_context(nc.Block())

        def rounds(eng, n0, n1, body):
            full = (n1 - n0) // 4
            if full >= 2:
                with eng.Fori(0, full) as i:
                    for q in range(4):
                        body(n0 + q + 4 * i, n0 + q, i)
            else:
                for i in range(full):
                    for q in range(4):
                        body(n0 + q + 4 * i, n0 + q, i)
            for q in range(4 * full, n1 - n0):
                body(n0 + q, n0 + q, 0)

        GAIN_AFTER = {1: "mix_norm0", 3: "ffn2_norm0", 5: "ffn1_norm1", 7: "mix_norm1", 9: "ffn2_norm1"}
        NORM_NO = {-1: 1, 1: 2, 3: 3, 5: 4, 7: 5, 9: 6}
        HBASE = {-1: 0, 1: 8, 3: 16, 5: 24, 7: 32, 9: 40}

        def steps_to(n):
            return 4 + FIRST[n]

        def needed_norm(n):
            return NORM_NO[n - 1]

        @block.sync
        def _(sp):
            sp.dma_start(x[:, :, :], xT).then_inc(S("x_loaded"), 16)
            sp.dma_start(par[:, :], params).then_inc(S("params_loaded"), 16)
            srcs = {"gu": gu_w, "down": down_w, "w_in": w_in, "w_out": w_out, "qkv": w_qkv, "w_o": w_o}
            for n, (name, steps, tiles, inst) in enumerate(LINEARS):
                g0, src = FIRST[n], srcs[name]
                off = inst * steps if name in ("gu", "down") else 0

                def load(j, q, i):
                    slot = (g0 + q) % 4
                    if n > 0 or q >= 4:
                        sp.wait_ge(S("lo_done"), 2 * (g0 + j - 4) + 2)
                    sp.dma_start(raw[:, slot, 0:2 * tiles * P],
                                 src[bass.ds(off + j, 1), :, :].rearrange("a p n -> (a p) n")
                                 ).then_inc(S(f"raw_full{slot}"), 16)

                if n == 0:
                    for j in range(4):
                        load(j, j, 0)
                    sp.dma_start(con[:, :], consts).then_inc(S("consts_loaded"), 16)
                    rounds(sp, 4, steps, load)
                else:
                    rounds(sp, 0, steps, load)
                if name == "w_in":
                    sp.wait_ge(S("evacuated"), steps_to(2))
                    sp.dma_start(wsT[:, :, :], w_spatialT).then_inc(S("spatial_loaded"), 16)
                    sp.dma_start(bsp[:, :, :], b_spatial).then_inc(S("spatial_loaded"), 16)
                    sp.dma_start(lora[:, :], w_lora).then_inc(S("lora_loaded"), 16)
                    sp.dma_start(wgate[:, :], w_gate).then_inc(S("lora_loaded"), 16)
                if name == "qkv":
                    sp.wait_ge(S("evacuated"), steps_to(8))
                    sp.dma_start(posi[:, :], positions).then_inc(S("pos_loaded"), 16)
            sp.wait_ge(S("evacuated"), steps_to(11) + LINEARS[11][1])
            sp.dma_start(out, x[:, :, :]).then_inc(S("stored"), 16)
            sp.wait_ge(S("stored"), 16)

        @block.scalar
        def _(act):
            link_at = [0]

            def link(ins):
                link_at[0] += 1
                ins.then_inc(S("act_link"), 1)
                act.wait_ge(S("act_link"), link_at[0])

            def split_hi(n, j, q, i=0):
                _, _, tiles, _ = LINEARS[n]
                g0 = FIRST[n]
                slot = (g0 + q) % 4
                for s in range(2):
                    if s == 0:
                        act.wait_ge(S(f"raw_full{slot}"), 16 * ((g0 + q) // 4 + 1 + i))
                    if n > 0 or q >= 2:
                        act.wait_ge(S("sub_done"), 2 * (g0 + j - 2) + s + 1)
                    nc.scalar.activation(w_hi[:, (2 * (g0 + q) + s) % 4, 0:tiles * P],
                                         raw[:, slot, s * tiles * P:(s + 1) * tiles * P],
                                         ACT.Copy).then_inc(S("hi_done"), 1)

            def silu(n, j, q):
                m = KF * LINEARS[n][3] + j
                act.wait_ge(S("evacuated"), steps_to(n) + j + 1)
                act.wait_ge(S("act_made"), m + 1)
                nc.scalar.activation(sil[:, q % 2, :], pre[:, q % 2, 0, :], ACT.Silu).then_inc(S("silu_done"), 1)

            def new_h(n, k):
                m = HBASE[n] + k
                nc.scalar.activation(h_hi[:, k, :], x[:, k, :], ACT.Copy,
                                     scale=pc(GAIN_AFTER.get(n, "ffn1_norm0"), k)).then_inc(S("h_hi_done"), 1)
                if m >= 2:
                    act.wait_ge(S("sq_added"), m - 1)
                nc.scalar.activation(sq[:, k % 2, :], x[:, k, :], ACT.Square).then_inc(S("sq_done"), 1)

            def norm_root(no):
                act.wait_ge(S("stats_done"), no)
                if no > 1:
                    act.wait_ge(S("norm_ready"), no - 1)
                nc.scalar.activation(root[:, :], mix[0][:, 0:T], ACT.Sqrt, scale=1.0 / D,
                                     bias=eps[:, 0:1]).then_inc(S("root_done"), 1)

            def late(n, j, q):
                name = LINEARS[n][0]
                if name == "gu":
                    silu(n, j, q)
                elif n in GAIN_AFTER:
                    act.wait_ge(S("evacuated"), steps_to(n) + j + 1)
                    for k in ((j,) if name == "down" else (2 * j, 2 * j + 1)):
                        new_h(n, k)
                elif name == "w_in" and j == 3:
                    act.wait_ge(S("evacuated"), steps_to(n) + 4)
                    nc.scalar.activation(zz[:, 18:22, 1:T + 1], zz[:, 18:22, 1:T + 1], ACT.Gelu).then_inc(S("s_gelu"), 1)
                    nc.scalar.activation(zz[:, 14:18, 1:T + 1], zz[:, 14:18, 1:T + 1], ACT.Gelu).then_inc(S("u_gelu"), 1)
                elif name == "w_in" and j == 6:
                    act.wait_ge(S("s_centred"), 1)
                    nc.scalar.activation(gt[:, :, :], zz[:, 18:22, 1:T + 1], ACT.Square).then_inc(S("s_squared"), 1)
                elif name == "w_in" and j == 10:
                    act.wait_ge(S("s_var"), 1)
                    nc.scalar.activation(g_rstd[:, :], mix[1][:, T:2 * T], ACT.Sqrt, scale=1.0 / AW,
                                         bias=eps[:, 1:2]).then_inc(S("s_root"), 1)
                elif name == "qkv":
                    act.wait_ge(S("evacuated"), steps_to(n) + j + 1)
                    for f in (2 * j, 2 * j + 1):
                        nc.scalar.activation(qz[:, f, :], qz[:, f, :], ACT.Identity,
                                             bias=pc("b_qkv", f)).then_inc(S("qkv_biased"), 1)

            def rwkv_gmlp():
                act.wait_ge(S("s_scaled"), 1)
                for f in range(4):
                    nc.scalar.activation(zz[:, 18 + f, 1:T + 1], zz[:, 18 + f, 1:T + 1], ACT.Identity,
                                         scale=pc("ln_gain", f), bias=pc("ln_bias", f)).then_inc(S("s_normed"), 1)
                act.wait_ge(S("mixed"), ZA)
                nc.scalar.activation(th[0:64, :], zs[0:64, 12, :], ACT.Tanh).then_inc(S("tanh_done"), 1)
                for c in range(CT):
                    nc.scalar.activation(kq[:, c, :], zs[:, 4 + c, :], ACT.Copy, scale=pc("k_k", c)
                                         ).then_inc(S("kq_made"), 1)
                act.wait_ge(S("kq_made"), CT)
                nc.scalar.activation(cs[:, :, :], kq[:, :, :], ACT.Square).then_inc(S("kq_squared"), 1)
                nc.scalar.activation(sgx[:, :], zs[:, 13, :], ACT.Sigmoid).then_inc(S("gate_in"), 1)
                act.wait_ge(S("decay_up"), 1)
                for c in range(CT):
                    nc.scalar.activation(sd[:, c, :], lin[c // 2][:, (c % 2) * T:(c % 2 + 1) * T], ACT.Sigmoid,
                                         bias=pc("w0", c)).then_inc(S("sd_made"), 1)
                act.wait_ge(S("iclr_up"), 1)
                for c in range(CT):
                    nc.scalar.activation(ic[:, c, :], lin[2 + c // 2][:, (c % 2) * T:(c % 2 + 1) * T], ACT.Sigmoid,
                                         bias=pc("a0", c)).then_inc(S("ic_made"), 1)
                act.wait_ge(S("u_used"), 1)
                act.wait_ge(S("kfb_made"), 1)
                act.wait_ge(S("ic_made"), CT)
                for c in range(CT):
                    nc.scalar.activation(BT[:, c, :], ic[:, c, :], ACT.Identity, scale=pc("k_a", c),
                                         bias=kfb[:, c:c + 1]).then_inc(S("kf_made"), 1)
                act.wait_ge(S("kk_sums"), 1)
                nc.scalar.activation(root[:, :], mix[0][:, 0:T], ACT.Sqrt).then_inc(S("kk_root"), 1)
                act.wait_ge(S("cs_made"), 1)
                nc.scalar.activation(ep[:, :, :], cs[:, :, :], ACT.Exp, scale=-KAPPA).then_inc(S("ep_made"), 1)
                act.wait_ge(S("csm_made"), 1)
                nc.scalar.activation(sd[:, :, :], sd[:, :, :], ACT.Exp, scale=-KAPPA).then_inc(S("pprev_made"), 1)
                nc.scalar.activation(cs[:, :, :], cs[:, :, :], ACT.Exp, scale=KAPPA).then_inc(S("en_made"), 1)

                ev = [0]

                def copy(dst, src, wait, value, done):
                    act.wait_ge(S(wait), value)
                    ev[0] += 1
                    nc.scalar.activation(dst, src, ACT.Copy).then_inc(S(done), 1)

                for m in range(2):
                    if m:
                        act.wait_ge(S("y_done"), 2)
                    for kind in range(4):
                        copy(TM[:, kind, :], mix[kind][:, :], "tok_t", 4 * m + kind + 1, "tok_made")
                    for half in range(2):
                        u4 = 2 * m + half
                        copy(D2[:, :, :], v3(mix[1]), "n_sq", 5 * u4 + 1, "sq_made")
                        copy(D2T[:, :, :], v3(mix[2]), "n_sq", 5 * u4 + 2, "sq_made")
                        copy(akv[:, :, :], mix[0][:, 0:4 * CH].rearrange("p (u i) -> p u i", u=4),
                             "akv_t", u4 + 1, "akv_made")
                        copy(D4[:, :, :], v3(lin[0]), "n_sq", 5 * u4 + 3, "sq_made")
                        copy(D4T[:, :, :], v3(lin[1]), "n_sq", 5 * u4 + 4, "sq_made")
                        copy(D2[:, :, :], v3(lin[3]), "n_sq", 5 * u4 + 5, "sq_made")
                        copy(Tt[:, :, :], v3(mix[1]), "t_t", 2 * u4 + 1, "t_made")
                        copy(Tt[:, :, :], v3(lin[0]), "t_t", 2 * u4 + 2, "t_made")
                        copy(GH[:, :, :], v3(mix[0]), "gh_t", u4 + 1, "gh_made")
                        copy(Yc[:, 2 * half:2 * half + 2, m * P:(m + 1) * P],
                             mix[2][:, 0:2 * P].rearrange("p (c t) -> p c t", c=2), "y_t", u4 + 1, "y_done")
                act.wait_ge(S("y_centred"), 1)
                nc.scalar.activation(ysq[:, :, :], Yc[:, :, :], ACT.Square).then_inc(S("y_squared"), 1)
                act.wait_ge(S("y_var"), 1)
                nc.scalar.activation(yst[:, 0, :], mix[0][:, 0:T], ACT.Sqrt, scale=1.0 / HD,
                                     bias=eps[:, 2:3]).then_inc(S("y_root"), 1)
                act.wait_ge(S("y_scaled"), 2)
                for c in range(CT):
                    nc.scalar.activation(Yc[:, c, :], Yc[:, c, :], ACT.Identity, scale=pc("gn_gain", c),
                                         bias=pc("gn_bias", c)).then_inc(S("y_normed"), 1)
                for c in range(2):
                    act.wait_ge(S("y_gated"), c + 1)
                    nc.scalar.activation(y_hi[:, 2 * c:2 * c + 2, :], Yc[:, 2 * c:2 * c + 2, :], ACT.Copy
                                         ).then_inc(S("y_hi_done"), 1)

            def attention():
                act.wait_ge(S("angles"), 1)
                nc.scalar.activation(sinT[:, :], sinT[:, :], ACT.Sin).then_inc(S("rope_tables"), 1)
                nc.scalar.activation(cosT[:, :], cosT[:, :], ACT.Sin).then_inc(S("rope_tables"), 1)
                act.wait_ge(S("qkv_biased"), 12)
                nc.scalar.activation(qsq[:, :, :], qz[:, 0:10, :], ACT.Square).then_inc(S("q_squared"), 1)
                act.wait_ge(S("q_squared"), 1)
                for f in range(10):
                    nc.scalar.activation(qz[:, f, :], qz[:, f, :], ACT.Copy,
                                         scale=pc("q_norm" if f < 8 else "k_norm")).then_inc(S("q_gained"), 1)
                act.wait_ge(S("q_sums"), 2)
                nc.scalar.activation(rq[:, :, :], mix[0][:, 0:2 * QH].rearrange("p (m h) -> p m h", m=2), ACT.Sqrt,
                                     scale=1.0 / HD, bias=eps[:, 0:1]).then_inc(S("rq_root"), 1)
                nc.scalar.activation(rk[0:64, 0, :], mix[1][0:64, 0:T], ACT.Sqrt, scale=1.0 / HD,
                                     bias=eps[0:64, 0:1]).then_inc(S("rk_root"), 1)
                act.wait_ge(S("v_t"), 1)
                nc.scalar.activation(v_tok[:, :, :], mix[3][:, :].rearrange("p (m f) -> p m f", m=2), ACT.Copy
                                     ).then_inc(S("v_tok_made"), 1)
                for f in range(KD):
                    nc.scalar.activation(x[:, f, :], x[:, f, :], ACT.Identity, bias=pc("b_o", f)
                                         ).then_inc(S("b_o_added"), 1)

                def exps(it):
                    n, c, b = it // 8, it % 8, it % 2
                    W = P * (n + 1)
                    act.wait_ge(S("max_made"), it + 1)
                    for p in range(2):
                        nc.scalar.activation(sc[:, b, p, 0:W], sc[:, b, p, 0:W], ACT.Exp,
                                             bias=sm[:, 2, 2 * b + p:2 * b + p + 1],
                                             accum_out=sm[:, 3, 2 * b + p:2 * b + p + 1]).then_inc(S("exp_made"), 1)
                        nc.scalar.activation(sm[:, 4, 2 * b + p:2 * b + p + 1], pc("sinks", 2 * c + p), ACT.Exp,
                                             bias=sm[:, 2, 2 * b + p:2 * b + p + 1]).then_inc(S("exp_made"), 1)

                def probs(it):
                    n, b = it // 8, it % 2
                    act.wait_ge(S("p_t"), it + 1)
                    if it >= 2:
                        act.wait_ge(S("pv"), it - 1)
                    src = lin[b][:, :].rearrange("p (h k q) -> p h k q", h=2, k=2)
                    nc.scalar.activation(pT[:, b, :, 0:n + 1, :], src[:, :, 0:n + 1, :], ACT.Copy
                                         ).then_inc(S("pT_made"), 1)

                def heads(it):
                    n, c, b = it // 8, it % 8, it % 2
                    act.wait_ge(S("pv"), it + 1)
                    nc.scalar.activation(y_hi[:, c, n * P:(n + 1) * P], lin[2 + b][:, 0:P], ACT.Copy
                                         ).then_inc(S("o_hi_done"), 1)

                exps(0)
                for it in range(16):
                    if it + 1 < 16:
                        exps(it + 1)
                    probs(it)
                    if it >= 1:
                        heads(it - 1)
                heads(15)

            act.wait_ge(S("x_loaded"), 16)
            act.wait_ge(S("params_loaded"), 16)
            for k in range(KD):
                new_h(-1, k)
            act.wait_ge(S("setup"), 1)
            for n, (name, steps, tiles, inst) in enumerate(LINEARS):
                if name not in ("w_out", "w_o"):
                    for j in range(2):
                        split_hi(n, j, j)
                        if n:
                            pn = LINEARS[n - 1][1] - 2 + j
                            late(n - 1, pn, pn)
                if n - 1 in NORM_NO:
                    norm_root(NORM_NO[n - 1])
                if name == "gu":
                    def step(j, q, i):
                        split_hi(n, j, q, i)
                        silu(n, j - 2, q - 2)
                    rounds(act, 2, steps, step)
                else:
                    for j in range(2, steps):
                        split_hi(n, j, j)
                        late(n, j - 2, j - 2)
                if name in ("w_in", "qkv"):
                    for j in range(2):
                        late(n, steps - 2 + j, steps - 2 + j)
                    for j in range(2):
                        split_hi(n + 1, j, j)
                    (rwkv_gmlp if name == "w_in" else attention)()

        @block.vector
        def _(dve):
            link_at = [0]

            def link(ins):
                link_at[0] += 1
                ins.then_inc(S("dve_link"), 1)
                dve.wait_ge(S("dve_link"), link_at[0])

            def split_lo(n, j, q, i=0):
                _, _, tiles, _ = LINEARS[n]
                g0 = FIRST[n]
                slot = (g0 + q) % 4
                for s in range(2):
                    dve.wait_ge(S("hi_done"), 2 * (g0 + j) + s + 1)
                    sub = (2 * (g0 + q) + s) % 4
                    nc.vector.tensor_tensor(w_lo[:, sub, 0:tiles * P], raw[:, slot, s * tiles * P:(s + 1) * tiles * P],
                                            w_hi[:, sub, 0:tiles * P].bitcast(F32), ALU.subtract
                                            ).then_inc(S("lo_done"), 1)

            def bank(n, q):
                return lin[(FIRST[n] + q) % 4]

            def scale_gu(n, j, q):
                m = KF * LINEARS[n][3] + j
                dve.wait_ge(S("sub_done"), 2 * (FIRST[n] + j) + 2)
                dve.wait_ge(S("act_made"), m + 1)
                nc.vector.tensor_tensor(pre[:, q % 2, :, :], bank(n, q)[:, :].rearrange("p (a t) -> p a t", a=2),
                                        rB[:, :].unsqueeze(1).to_broadcast([P, 2, T]), ALU.mult
                                        ).then_inc(S("evacuated"), 1)

            def new_h_lo(n, k):
                dve.wait_ge(S("h_hi_done"), HBASE[n] + k + 1)
                nc.vector.scalar_tensor_tensor(out=h_lo[:, k, :], in0=x[:, k, :],
                                               scalar=pc(GAIN_AFTER.get(n, "ffn1_norm0"), k),
                                               in1=h_hi[:, k, :].bitcast(F32), op0=ALU.mult, op1=ALU.subtract
                                               ).then_inc(S("h_ready"), 1)

            def late(n, j, q):
                name = LINEARS[n][0]
                if name == "gu":
                    return scale_gu(n, j, q)
                dve.wait_ge(S("sub_done"), 2 * (FIRST[n] + j) + 2)
                src = bank(n, q)
                if name == "down":
                    nc.vector.scalar_tensor_tensor(out=x[:, j, :], in0=src[:, 0:T], scalar=0.5, in1=x[:, j, :],
                                                   op0=ALU.mult, op1=ALU.add).then_inc(S("evacuated"), 1)
                    if n in GAIN_AFTER:
                        new_h_lo(n, j)
                elif name in ("w_out", "w_o"):
                    if name == "w_o" and j == 0:
                        dve.wait_ge(S("b_o_added"), KD)
                    nc.vector.tensor_tensor(x[:, 2 * j:2 * j + 2, :], src[:, :].rearrange("p (a t) -> p a t", a=2),
                                            x[:, 2 * j:2 * j + 2, :], ALU.add).then_inc(S("evacuated"), 1)
                    new_h_lo(n, 2 * j)
                    new_h_lo(n, 2 * j + 1)
                else:
                    if name == "w_in":
                        f = 14 + 2 * j if j < 4 else 2 * (j - 4)
                        dst = zz[:, f:f + 2, 1:T + 1]
                    else:
                        dst = qz[:, 2 * j:2 * j + 2, :]
                    nc.vector.tensor_tensor(dst, src[:, :].rearrange("p (a t) -> p a t", a=2),
                                            rB[:, :].unsqueeze(1).to_broadcast([P, 2, T]), ALU.mult
                                            ).then_inc(S("evacuated"), 1)
                    if name == "w_in":
                        during_w_in(j)

            def token_mix(j):
                dve.wait_ge(S("shifted"), j - 3)
                for f in (2 * (j - 4), 2 * (j - 4) + 1):
                    nc.vector.scalar_tensor_tensor(out=zs[:, f, :], in0=zs[:, f, :], scalar=pc("mu", f),
                                                   in1=zz[:, f, 1:T + 1], op0=ALU.mult, op1=ALU.add
                                                   ).then_inc(S("mixed"), 1)

            def during_w_in(j):
                if j >= 5:
                    token_mix(j - 1)
                if j == 5:
                    dve.wait_ge(S("s_mean"), 1)
                    link(nc.vector.tensor_scalar(g_mean[:, :], mix[1][:, 0:T], 1.0 / AW, None, ALU.mult))
                    nc.vector.tensor_tensor(zz[:, 18:22, 1:T + 1], zz[:, 18:22, 1:T + 1],
                                            g_mean[:, :].unsqueeze(1).to_broadcast([P, 4, T]), ALU.subtract
                                            ).then_inc(S("s_centred"), 1)

            def norm_factor(no):
                dve.wait_ge(S("root_done"), no)
                nc.vector.reciprocal(rB[:, :], root[:, :]).then_inc(S("norm_ready"), 1)
                dve.wait_ge(S("norm_ready"), no)

            def rwkv_gmlp():
                token_mix(10)
                dve.wait_ge(S("s_root"), 1)
                link(nc.vector.reciprocal(g_rstd[:, :], g_rstd[:, :]))
                nc.vector.tensor_tensor(zz[:, 18:22, 1:T + 1], zz[:, 18:22, 1:T + 1],
                                        g_rstd[:, :].unsqueeze(1).to_broadcast([P, 4, T]), ALU.mult
                                        ).then_inc(S("s_scaled"), 1)
                dve.wait_ge(S("spatial_loaded"), 32)
                nc.vector.tensor_tensor(wsT[:, :, :], wsT[:, :, :], cc("causal").unsqueeze(1).to_broadcast([P, 4, P]),
                                        ALU.mult).then_inc(S("ws_masked"), 1)
                nc.vector.tensor_scalar(kfb[:, :], pc("k_a", 0, 4), -1.0, 1.0, ALU.mult, ALU.add
                                        ).then_inc(S("kfb_made"), 1)
                for m in range(2):
                    dve.wait_ge(S("s_tok_t"), m + 1)
                    nc.vector.tensor_copy(s_tok[:, m, :], mix[2 + m][:, :]).then_inc(S("s_tok_made"), 1)
                for m in range(2):
                    dve.wait_ge(S("spatial_done"), m + 1)
                    link(nc.vector.tensor_tensor(gt[:, :, m * P:(m + 1) * P], v3(mix[2 + m]), bsp[:, :, :], ALU.add))
                dve.wait_ge(S("u_gelu"), 1)
                link(nc.vector.tensor_tensor(gt[:, :, :], gt[:, :, :], zz[:, 14:18, 1:T + 1], ALU.mult))
                link(nc.vector.tensor_copy(y_hi[:, 4:8, :], gt[:, :, :]))
                nc.vector.tensor_tensor(y_lo[:, 4:8, :], gt[:, :, :], y_hi[:, 4:8, :].bitcast(F32), ALU.subtract
                                        ).then_inc(S("u_used"), 1)
                dve.wait_ge(S("u_used"), 1)
                dve.wait_ge(S("kk_sums"), 1)
                dve.wait_ge(S("sd_made"), CT)
                for c in range(CT):
                    i = nc.vector.tensor_tensor_scan(cs[:, c, :], cc("restart"), sd[:, c, :], 0.0, ALU.mult, ALU.add)
                    if c < CT - 1:
                        i.then_inc(S("cs_parts"), 1)
                    else:
                        i.then_inc(S("cs_made"), 1)
                dve.wait_ge(S("cs_made"), 1)
                nc.vector.tensor_tensor(sd[:, :, :], cs[:, :, :], sd[:, :, :], ALU.subtract).then_inc(S("csm_made"), 1)
                dve.wait_ge(S("kk_root"), 1)
                link(nc.vector.tensor_scalar(root[:, :], root[:, :], 1e-12, None, ALU.max))
                nc.vector.reciprocal(rB[:, :], root[:, :]).then_inc(S("kk_inv"), 1)
                dve.wait_ge(S("kf_made"), CT)
                link(nc.vector.tensor_tensor(zs[:, 4:8, :], zs[:, 4:8, :], BT[:, :, :], ALU.mult))
                for c in range(CT):
                    nc.vector.scalar_tensor_tensor(out=bonus[:, c, :], in0=zs[:, c, :], scalar=pc("r_k", c),
                                                   in1=zs[:, 4 + c, :], op0=ALU.mult, op1=ALU.mult
                                                   ).then_inc(S("bonus_in"), 1)
                for c in range(2):
                    dve.wait_ge(S("kk_spread"), c + 1)
                    link(nc.vector.scalar_tensor_tensor(
                        out=kq[:, 2 * c:2 * c + 2, :], in0=mix[2 + c][:, :].rearrange("p (a t) -> p a t", a=2),
                        scalar=-1.0, in1=kq[:, 2 * c:2 * c + 2, :], op0=ALU.mult, op1=ALU.mult))
                dve.wait_ge(S("ep_made"), 1)
                nc.vector.tensor_tensor(tok4(AR, 1), zs[:, 0:4, :].rearrange("p c (m t) -> p c m t", m=2),
                                        ep[:, :, :].rearrange("p c (m t) -> p c m t", m=2), ALU.mult
                                        ).then_inc(S("R_made"), 1)
                link(nc.vector.tensor_copy(pend[:, :, :], ep[:, :, CH - 1:T:CH]))
                dve.wait_ge(S("pprev_made"), 1)
                nc.vector.tensor_tensor(tok4(AR, 0), kq[:, :, :].rearrange("p c (m t) -> p c m t", m=2),
                                        sd[:, :, :].rearrange("p c (m t) -> p c m t", m=2), ALU.mult
                                        ).then_inc(S("A_made"), 1)
                dve.wait_ge(S("en_made"), 1)
                nc.vector.tensor_tensor(KT[:, :, :], zs[:, 4:8, :], cs[:, :, :], ALU.mult).then_inc(S("K_made"), 1)
                link(nc.vector.tensor_tensor(ic[:, :, :], ic[:, :, :], cs[:, :, :], ALU.mult))
                nc.vector.scalar_tensor_tensor(out=BT[:, :, :], in0=kq[:, :, :], scalar=-1.0, in1=ic[:, :, :],
                                               op0=ALU.mult, op1=ALU.mult).then_inc(S("B_made"), 1)
                for c in range(2):
                    dve.wait_ge(S("bonus_sums"), c + 1)
                    link(nc.vector.tensor_tensor(bonus[:, 2 * c:2 * c + 2, :],
                                                 lin[c][:, :].rearrange("p (a t) -> p a t", a=2),
                                                 zs[:, 8 + 2 * c:10 + 2 * c, :], ALU.mult))
                nc.vector.memset(St[:, 0, 0, 0:1], 0.0).then_inc(S("bonus_done"), 1)

                for m in range(2):
                    for half in range(2):
                        u4 = 2 * m + half
                        cs2 = slice(2 * half, 2 * half + 2)
                        if u4:
                            dve.wait_ge(S("y_t"), u4)
                        for u in range(4):
                            dve.wait_ge(S("pairs_t"), 4 * u4 + u + 1)
                            nc.vector.tensor_tensor(AM[:, u, :], lin[u][:, :], cc("mask_pair"), ALU.mult
                                                    ).then_inc(S("AM_made"), 1)
                        dve.wait_ge(S("ab_t"), u4 + 1)
                        for mask, dst in (("mask16", Dm), ("mask32", M32), ("mask64", M64)):
                            for po in range(2):
                                nc.vector.tensor_tensor(
                                    dst[:, po:4:2, :], mix[po][:, 0:2 * P].rearrange("p (a t) -> p a t", a=2),
                                    cc(mask).unsqueeze(1).to_broadcast([P, 2, P]), ALU.mult
                                ).then_inc(S("ab_masked"), 1)
                        dve.wait_ge(S("Z_first"), u4 + 1)
                        for r, b in enumerate((mix[3], lin[2], mix[0])):
                            dve.wait_ge(S("z_t"), 5 * u4 + r + 1)
                            nc.vector.tensor_tensor(Zt[:, :, :], v3(b), Zt[:, :, :], ALU.add).then_inc(S("Z_made"), 1)
                            dve.wait_ge(S("Z_made"), 5 * u4 + r + 1)
                        for r, (bx, bz) in enumerate(((mix[2], mix[3]), (lin[1], lin[2]))):
                            dve.wait_ge(S("x_t"), 2 * u4 + r + 1)
                            nc.vector.tensor_copy(Xa[:, :, :], v3(bx)).then_inc(S("x_made"), 1)
                            dve.wait_ge(S("z_t"), 5 * u4 + 4 + r)
                            nc.vector.tensor_tensor(Zt[:, :, :], v3(bz), Zt[:, :, :], ALU.add).then_inc(S("Z_made"), 1)
                            dve.wait_ge(S("Z_made"), 5 * u4 + 4 + r)
                        dve.wait_ge(S("q_t"), u4 + 1)
                        nc.vector.tensor_tensor(AR[:, cs2, m, 1, :], mix[1][:, 0:2 * P].rearrange("p (c t) -> p c t", c=2),
                                                AR[:, cs2, m, 1, :], ALU.add).then_inc(S("Q_made"), 1)
                        for c2 in range(2):
                            n = 2 * m + c2
                            if n == NC - 1:
                                continue
                            dve.wait_ge(S("e_t"), 4 * m + (c2 + 1 if m == 0 else 1) + half * (2 if m == 0 else 1))
                            for u in range(4):
                                po, c = 64 * (u % 2), 2 * half + u // 2
                                nc.vector.tensor_tensor(
                                    ETs[po:po + 64, n, c, :], (mix[3], lin[0])[c2][po:po + 64, (u // 2) * CH:(u // 2 + 1) * CH],
                                    ident[po:po + 64, po:po + 64], ALU.add).then_inc(S("E_made"), 1)
                            nc.vector.tensor_copy(Fs[:, n, cs2, :],
                                                  (lin[2], lin[1])[c2][:, 0:2 * CH].rearrange("p (c i) -> p c i", c=2)
                                                  ).then_inc(S("F_made"), 1)
                dve.wait_ge(S("F_made"), 6)
                for n in range(3):
                    src = Fs[:, n, :, :]
                    if n:
                        dve.wait_ge(S("s_t"), n)
                        for po in range(2):
                            ins = nc.vector.tensor_tensor(Fs[64 * po:64 * po + 64, n, :, :],
                                                          mix[2 * (n % 2) + po][64 * po:64 * po + 64, 0:4 * CH].rearrange(
                                                              "p (c i) -> p c i", c=4),
                                                          Fs[64 * po:64 * po + 64, n, :, :], ALU.add)
                            link(ins)
                    nc.vector.tensor_tensor(St[:, n, :, :], src, pend[:, :, n:n + 1].to_broadcast([P, CT, CH]), ALU.mult
                                            ).then_inc(S("S_made"), 1)
                for n in range(3):
                    dve.wait_ge(S("ys_t"), n + 1)
                    for po in range(2):
                        r = slice(64 * po, 64 * po + 64)
                        link(nc.vector.tensor_tensor(Yc[r, :, (n + 1) * CH:(n + 2) * CH],
                                                     YSB[n][po][r, 0:4 * CH].rearrange("p (c i) -> p c i", c=4),
                                                     Yc[r, :, (n + 1) * CH:(n + 2) * CH], ALU.add))
                nc.vector.memset(St[:, 0, 0, 0:1], 0.0).then_inc(S("y_complete"), 1)
                for c in range(2):
                    dve.wait_ge(S("y_mean"), c + 1)
                    link(nc.vector.scalar_tensor_tensor(
                        out=Yc[:, 2 * c:2 * c + 2, :], in0=lin[c][:, :].rearrange("p (a t) -> p a t", a=2),
                        scalar=-1.0 / HD, in1=Yc[:, 2 * c:2 * c + 2, :], op0=ALU.mult, op1=ALU.add))
                nc.vector.memset(St[:, 0, 0, 0:1], 0.0).then_inc(S("y_centred"), 1)
                dve.wait_ge(S("y_root"), 1)
                nc.vector.reciprocal(yst[:, 1, :], yst[:, 0, :]).then_inc(S("y_inv"), 1)
                for c in range(2):
                    dve.wait_ge(S("y_spread"), c + 1)
                    nc.vector.tensor_tensor(Yc[:, 2 * c:2 * c + 2, :],
                                            lin[2 + c][:, :].rearrange("p (a t) -> p a t", a=2),
                                            Yc[:, 2 * c:2 * c + 2, :], ALU.mult).then_inc(S("y_scaled"), 1)
                dve.wait_ge(S("y_normed"), CT)
                link(nc.vector.tensor_tensor(Yc[:, :, :], Yc[:, :, :], bonus[:, :, :], ALU.add))
                for c in range(2):
                    dve.wait_ge(S("gate_up"), c + 1)
                    nc.vector.tensor_tensor(Yc[:, 2 * c:2 * c + 2, :],
                                            mix[1 + c][:, :].rearrange("p (a t) -> p a t", a=2),
                                            Yc[:, 2 * c:2 * c + 2, :], ALU.mult).then_inc(S("y_gated"), 1)
                for c in range(2):
                    dve.wait_ge(S("y_hi_done"), c + 1)
                    nc.vector.tensor_tensor(y_lo[:, 2 * c:2 * c + 2, :], Yc[:, 2 * c:2 * c + 2, :],
                                            y_hi[:, 2 * c:2 * c + 2, :].bitcast(F32), ALU.subtract
                                            ).then_inc(S("y_lo_done"), 1)

            def attention():
                C1, C2 = 6.28125, 0.0019350051879882812
                C3 = 6.283185307179586 - C1 - C2
                ROUND = 12582912.0
                PI = 3.14159274101257
                dve.wait_ge(S("pos_loaded"), 16)
                link(nc.vector.tensor_copy(posf[:, :], posi[:, :]))
                link(nc.vector.tensor_scalar(posf[:, :], posf[:, :], pc("inv_freq"), None, ALU.mult))
                turns = posi[:, :].bitcast(F32)
                for dst, quarter in ((sinT, 0.0), (cosT, 0.25)):
                    link(nc.vector.tensor_scalar(turns, posf[:, :], 1.0 / 6.283185307179586, quarter, ALU.mult, ALU.add))
                    link(nc.vector.tensor_scalar(turns, turns, ROUND, -ROUND, ALU.add, ALU.add))
                    link(nc.vector.scalar_tensor_tensor(out=dst[:, :], in0=turns, scalar=-C1, in1=posf[:, :],
                                                        op0=ALU.mult, op1=ALU.add))
                    link(nc.vector.scalar_tensor_tensor(out=dst[:, :], in0=turns, scalar=-C2, in1=dst[:, :],
                                                        op0=ALU.mult, op1=ALU.add))
                    link(nc.vector.scalar_tensor_tensor(out=dst[:, :], in0=turns, scalar=-C3, in1=dst[:, :],
                                                        op0=ALU.mult, op1=ALU.add))
                    if quarter:
                        link(nc.vector.tensor_scalar(dst[:, :], dst[:, :], PI / 2, None, ALU.add))
                    link(nc.vector.tensor_scalar(dst[:, :], dst[:, :], PI, -PI, ALU.min, ALU.max))
                link(nc.vector.tensor_scalar(sm[:, 0, :], pc("sinks", 0, QH), -1.0, None, ALU.mult))
                nc.vector.memset(sm[:, 5, :], 0.0).then_inc(S("angles"), 1)
                dve.wait_ge(S("rq_root"), 1)
                link(nc.vector.reciprocal(rq[:, :, :], rq[:, :, :]))
                link(nc.vector.tensor_scalar(rq[:, :, :], rq[:, :, :], HD ** -0.5, None, ALU.mult))
                dve.wait_ge(S("rk_root"), 1)
                nc.vector.reciprocal(rk[0:64, 1, :], rk[0:64, 0, :]).then_inc(S("rk_made"), 1)
                dve.wait_ge(S("rk_spread"), 1)
                dve.wait_ge(S("q_gained"), 10)
                nc.vector.tensor_tensor(qz[:, 8:10, :], mix[2][:, :].rearrange("p (a t) -> p a t", a=2), qz[:, 8:10, :],
                                        ALU.mult).then_inc(S("k_scaled"), 1)
                dve.wait_ge(S("k_scaled"), 1)
                dve.wait_ge(S("rope_tables"), 2)
                for c in (4, 0, 1, 2, 3):
                    two = slice(2 * c, 2 * c + 2)
                    link(nc.vector.tensor_tensor(qr[:, two, :], qz[:, two, :],
                                                 cosT[:, :].unsqueeze(1).to_broadcast([P, 2, T]), ALU.mult))
                    k = (4, 0, 1, 2, 3).index(c)
                    dve.wait_ge(S("rot_t"), k + 1)
                    nc.vector.tensor_tensor(trot[:, :, :], (lin[0], lin[1])[k % 2][:, :].rearrange("p (a t) -> p a t", a=2),
                                            sinT[:, :].unsqueeze(1).to_broadcast([P, 2, T]), ALU.mult
                                            ).then_inc(S("rot_used"), 1)
                    dve.wait_ge(S("rot_used"), k + 1)
                    nc.vector.tensor_tensor(qr[:, two, :], qr[:, two, :], trot[:, :, :], ALU.add
                                            ).then_inc(S("roped"), 1)
                    dve.wait_ge(S("roped"), k + 1)

                def scores(it):
                    n, c, b = it // 8, it % 8, it % 2
                    W = P * (n + 1)
                    mask = cc("window")[:, 2 * P - W:2 * P]
                    dve.wait_ge(S("scores_t"), it + 1)
                    if it >= 2:
                        dve.wait_ge(S("p_t"), it - 1)
                    for p in range(2):
                        link(nc.vector.scalar_tensor_tensor(out=sc[:, b, p, 0:W], in0=mix[2 * b + p][:, 0:W],
                                                            scalar=rq[:, n, 2 * c + p:2 * c + p + 1], in1=mask,
                                                            op0=ALU.mult, op1=ALU.add))
                    link(nc.vector.tensor_reduce(sm[:, 1, 2 * b:2 * b + 2], sc[:, b, :, 0:W], AX, ALU.max, negate=True))
                    nc.vector.tensor_tensor(sm[:, 2, 2 * b:2 * b + 2], sm[:, 1, 2 * b:2 * b + 2],
                                            sm[:, 0, 2 * c:2 * c + 2], ALU.min).then_inc(S("max_made"), 1)

                def normalise(it):
                    n, c, b = it // 8, it % 8, it % 2
                    W = P * (n + 1)
                    dve.wait_ge(S("exp_made"), 4 * it + 4)
                    link(nc.vector.tensor_tensor(sm[:, 5, 2 * b:2 * b + 2], sm[:, 3, 2 * b:2 * b + 2],
                                                 sm[:, 4, 2 * b:2 * b + 2], ALU.add))
                    link(nc.vector.reciprocal(sm[:, 6, 2 * b:2 * b + 2], sm[:, 5, 2 * b:2 * b + 2]))
                    for p in range(2):
                        nc.vector.tensor_scalar(sc[:, b, p, 0:W], sc[:, b, p, 0:W], sm[:, 6, 2 * b + p:2 * b + p + 1],
                                                None, ALU.mult).then_inc(S("p_made"), 1)

                def heads_lo(it):
                    n, c, b = it // 8, it % 8, it % 2
                    dve.wait_ge(S("o_hi_done"), it + 1)
                    nc.vector.tensor_tensor(y_lo[:, c, n * P:(n + 1) * P], lin[2 + b][:, 0:P],
                                            y_hi[:, c, n * P:(n + 1) * P].bitcast(F32), ALU.subtract
                                            ).then_inc(S("o_lo_done"), 1)

                scores(0)
                for it in range(16):
                    if it + 1 < 16:
                        scores(it + 1)
                    normalise(it)
                    if it >= 2:
                        heads_lo(it - 2)
                heads_lo(14)
                heads_lo(15)

            for i, e in enumerate((RMS_EPS, LN_EPS, GN_EPS, 0.0)):
                nc.vector.memset(eps[:, i:i + 1], e).then_inc(S("setup_parts"), 1)
            nc.vector.memset(ones[:, :], 1.0).then_inc(S("setup"), 1)
            nc.vector.memset(root[:, :], 1.0).then_inc(S("evacuated"), 4)
            dve.wait_ge(S("x_loaded"), 16)
            dve.wait_ge(S("params_loaded"), 16)
            for k in range(KD):
                new_h_lo(-1, k)
            for n, (name, steps, tiles, inst) in enumerate(LINEARS):
                if name not in ("w_out", "w_o"):
                    for j in range(2):
                        split_lo(n, j, j)
                        if n:
                            pn = LINEARS[n - 1][1] - 2 + j
                            late(n - 1, pn, pn)
                if n - 1 in NORM_NO:
                    norm_factor(NORM_NO[n - 1])
                if name == "gu":
                    def step(j, q, i):
                        split_lo(n, j, q, i)
                        scale_gu(n, j - 2, q - 2)
                    rounds(dve, 2, steps, step)
                else:
                    for j in range(2, steps):
                        split_lo(n, j, j)
                        late(n, j - 2, j - 2)
                if name in ("w_in", "qkv"):
                    for j in range(2):
                        late(n, steps - 2 + j, steps - 2 + j)
                    for j in range(2):
                        split_lo(n + 1, j, j)
                    (rwkv_gmlp if name == "w_in" else attention)()
            for j in range(2):
                late(11, LINEARS[11][1] - 2 + j, LINEARS[11][1] - 2 + j)

        @block.gpsimd
        def _(pool):
            nc.gpsimd.memset(zz[:, :, 0:1], 0.0).then_inc(S("zz_zeroed"), 1)
            nc.gpsimd.memset(sil[:, :, :], 0.0).then_inc(S("act_made"), 2)

            def add_square(n, k):
                m = HBASE[n] + k
                pool.wait_ge(S("sq_done"), m + 1)
                if k == 0:
                    if NORM_NO[n] > 1:
                        pool.wait_ge(S("stats_done"), NORM_NO[n] - 1)
                    nc.gpsimd.tensor_copy(ssq[:, 0, :], sq[:, 0, :]).then_inc(S("sq_added"), 1)
                else:
                    pool.wait_ge(S("sq_added"), m)
                    nc.gpsimd.tensor_tensor(ssq[:, 0, :], ssq[:, 0, :], sq[:, k % 2, :], ALU.add
                                            ).then_inc(S("sq_added"), 1)

            def hidden(n, j, q):
                m = KF * LINEARS[n][3] + j
                pool.wait_ge(S("silu_done"), m + 1)
                nc.gpsimd.tensor_tensor(act_f[:, q % 2, :], sil[:, q % 2, :], pre[:, q % 2, 1, :], ALU.mult
                                        ).then_inc(S("act_made"), 1)
                pool.wait_ge(S("act_made"), m + 3)
                if LINEARS[n][3] and isinstance(q, int) and q < 2:
                    pool.wait_ge(S("sub_done"), 2 * FIRST[n])
                nc.gpsimd.tensor_copy(a_hi[:, bass.ds(j, 1), :].rearrange("p a t -> p (a t)"), act_f[:, q % 2, :]
                                      ).then_inc(S("a_hi_done"), 1)
                pool.wait_ge(S("a_hi_done"), m + 1)
                nc.gpsimd.tensor_tensor(a_lo[:, bass.ds(j, 1), :].rearrange("p a t -> p (a t)"), act_f[:, q % 2, :],
                                        a_hi[:, bass.ds(j, 1), :].rearrange("p a t -> p (a t)").bitcast(F32),
                                        ALU.subtract).then_inc(S("a_ready"), 1)

            def rwkv_gmlp():
                for m in range(2):
                    for half in range(2):
                        u4 = 2 * m + half
                        pool.wait_ge(S("AM_made"), 4 * u4 + 4)
                        nc.gpsimd.tensor_tensor(DmT[:, :, :], AM[:, :, 0:P],
                                                cc("mask16T").unsqueeze(1).to_broadcast([P, 4, P]), ALU.mult
                                                ).then_inc(S("DmT_made"), 1)
                        pool.wait_ge(S("DmT_made"), u4 + 1)
                        nc.gpsimd.tensor_tensor(Zt[:, :, :], DmT[:, :, :],
                                                ident.unsqueeze(1).to_broadcast([P, 4, P]), ALU.add
                                                ).then_inc(S("Z_first"), 1)

            for k in range(KD):
                add_square(-1, k)
            for n, (name, steps, tiles, inst) in enumerate(LINEARS):
                if name == "gu":
                    rounds(pool, 0, steps, lambda j, q, i: hidden(n, j, q))
                elif n in GAIN_AFTER:
                    for k in range(KD):
                        add_square(n, k)
                elif name == "w_in":
                    pool.wait_ge(S("zz_zeroed"), 1)
                    for j in range(4, 11):
                        pool.wait_ge(S("evacuated"), steps_to(n) + j + 1)
                        f = 2 * (j - 4)
                        nc.gpsimd.tensor_tensor(zs[:, f:f + 2, :], zz[:, f:f + 2, 0:T], zz[:, f:f + 2, 1:T + 1],
                                                ALU.subtract).then_inc(S("shifted"), 1)
                    rwkv_gmlp()

        @block.tensor
        def _(pe):
            mm = nc.tensor.matmul

            def products(out, sub, w0, tiles, in_hi, in_lo, k0, last_k, first, done):
                for k in range(tiles):
                    wa = w_hi[:, sub, (w0 + k) * P:(w0 + k + 1) * P]
                    wb = w_lo[:, sub, (w0 + k) * P:(w0 + k + 1) * P]
                    a, b = in_hi[:, k0 + k, :], in_lo[:, k0 + k, :]
                    if done is not None:
                        done(k0 + k)
                    mm(out, wa, a, start=first and k == 0, stop=False)
                    mm(out, wa, b, start=False, stop=False)
                    ins = mm(out, wb, a, start=False, stop=last_k and k == tiles - 1)
                ins.then_inc(S("sub_done"), 1)

            def step(n, j, q, i=0):
                name, _, tiles, inst = LINEARS[n]
                g0 = FIRST[n]
                b = lin[(g0 + q) % 4]
                pe.wait_ge(S("evacuated"), g0 + j + 1)
                for s in range(2):
                    pe.wait_ge(S("lo_done"), 2 * (g0 + j) + s + 1)
                    sub = (2 * (g0 + q) + s) % 4
                    if name == "down":
                        ready = (lambda k: pe.wait_ge(S("a_ready"), KF * inst + k + 1)) if q == 0 else None
                        products(b[:, 0:T], sub, 0, tiles, a_hi, a_lo, s * tiles, s == 1, s == 0, ready)
                    elif name in ("w_out", "w_o"):
                        products(b[:, s * T:(s + 1) * T], sub, 0, tiles, y_hi, y_lo, 0, True, True, None)
                    else:
                        ready = (lambda k: pe.wait_ge(S("h_ready"), HBASE[n - 1] + k + 1)) if q == 0 and s == 0 else None
                        products(b[:, s * T:(s + 1) * T], sub, 0, tiles, h_hi, h_lo, 0, True, True, ready)

            def stats(no):
                pe.wait_ge(S("sq_added"), 8 * no)
                pe.wait_ge(S("setup"), 1)
                mm(mix[0][:, 0:T], ones[:, :], ssq[:, 0, :], start=True, stop=True).then_inc(S("stats_done"), 1)

            def during_w_in(j):
                if j == 5:
                    pe.wait_ge(S("s_gelu"), 1)
                    for f in range(4):
                        ins = mm(mix[1][:, 0:T], ones[:, :], zz[:, 18 + f, 1:T + 1], start=f == 0, stop=f == 3)
                    ins.then_inc(S("s_mean"), 1)
                if j == 10:
                    pe.wait_ge(S("s_squared"), 1)
                    for f in range(4):
                        ins = mm(mix[1][:, T:2 * T], ones[:, :], gt[:, f, :], start=f == 0, stop=f == 3)
                    ins.then_inc(S("s_var"), 1)

            def rwkv_gmlp():
                pe.wait_ge(S("consts_loaded"), 16)
                pe.wait_ge(S("evacuated"), steps_to(3))
                pe.wait_ge(S("lora_loaded"), 32)
                pe.wait_ge(S("tanh_done"), 1)
                for c in range(CT):
                    ins = mm(lin[c // 2][:, (c % 2) * T:(c % 2 + 1) * T], lora[0:64, c * P:(c + 1) * P], th[0:64, :],
                             start=True, stop=True)
                ins.then_inc(S("decay_up"), 1)
                for c in range(CT):
                    ins = mm(lin[2 + c // 2][:, (c % 2) * T:(c % 2 + 1) * T], lora[64:128, c * P:(c + 1) * P],
                             zs[64:128, 12, :], start=True, stop=True)
                ins.then_inc(S("iclr_up"), 1)
                pe.wait_ge(S("kq_squared"), 1)
                for c in range(CT):
                    ins = mm(mix[0][32 * c:32 * c + 32, 0:T], cc("pick"), cs[:, c, :], start=True, stop=True)
                ins.then_inc(S("kk_sums"), 1)
                pe.wait_ge(S("s_normed"), 4)
                for m in range(2):
                    for f in range(4):
                        ins = nc.tensor.transpose(mix[2 + m][:, f * P:(f + 1) * P],
                                                  zz[:, 18 + f, 1 + m * P:1 + (m + 1) * P], ident)
                    ins.then_inc(S("s_tok_t"), 1)
                pe.wait_ge(S("ws_masked"), 1)
                for m in range(2):
                    pe.wait_ge(S("s_tok_made"), m + 1)
                    for f in range(4):
                        ins = mm(mix[2 + m][:, f * P:(f + 1) * P], s_tok[:, m, f * P:(f + 1) * P], wsT[:, f, :],
                                 start=True, stop=True)
                    ins.then_inc(S("spatial_done"), 1)
                pe.wait_ge(S("kk_inv"), 1)
                pe.wait_ge(S("u_used"), 1)
                for c in range(CT):
                    ins = mm(mix[2 + c // 2][:, (c % 2) * T:(c % 2 + 1) * T], cc("spread")[:, c * P:(c + 1) * P],
                             rB[:, :], start=True, stop=True)
                    if c % 2:
                        ins.then_inc(S("kk_spread"), 1)
                pe.wait_ge(S("bonus_in"), CT)
                pe.wait_ge(S("sd_made"), CT)
                for c in range(2):
                    mm(lin[c][:, :], cc("head_ones"), bonus[:, 2 * c:2 * c + 2, :], start=True, stop=True
                       ).then_inc(S("bonus_sums"), 1)
                for sem, v in (("A_made", 1), ("R_made", 1), ("K_made", 1), ("B_made", 1), ("bonus_done", 1), ("ic_made", CT)):
                    pe.wait_ge(S(sem), v)
                for m in range(2):
                    tk = slice(m * P, (m + 1) * P)
                    if m:
                        pe.wait_ge(S("F_made"), 4)
                        pe.wait_ge(S("Q_made"), 2)
                        pe.wait_ge(S("E_made"), 16)
                        pe.wait_ge(S("y_done"), 2)
                    for kind in range(4):
                        for c in range(CT):
                            src = (zs[:, 8 + c, tk], BT[:, c, tk], KT[:, c, tk], AR[:, c, m, 0, :])[kind]
                            ins = nc.tensor.transpose(mix[kind][:, c * P:(c + 1) * P], src, ident)
                        ins.then_inc(S("tok_t"), 1)
                    for half in range(2):
                        u4 = 2 * m + half
                        heads = [(u, 2 * half + u // 2, 64 * (u % 2), 4 * half + u) for u in range(4)]
                        if u4:
                            pe.wait_ge(S("F_made"), (0, 2, 4, 5)[u4])
                            pe.wait_ge(S("E_made"), 4 * (0, 2, 4, 5)[u4])
                            pe.wait_ge(S("Q_made"), u4)
                            pe.wait_ge(S("y_done"), u4)
                        for u, c, po, h in heads:
                            r = slice(po, po + 64)
                            mm(lin[u][:, 0:2 * P], BT[r, c, tk], AR[r, c, m, :, :], start=True, stop=True)
                            mm(lin[u][:, 2 * P:4 * P], KT[r, c, tk], AR[r, c, m, :, :], start=True, stop=True
                               ).then_inc(S("pairs_t"), 1)
                        pe.wait_ge(S("tok_made"), 4 * m + 4)
                        for u, c, po, h in heads:
                            r = slice(po, po + 64)
                            ins = mm(mix[u % 2][:, (u // 2) * P:(u // 2 + 1) * P], AR[r, c, m, 0, :], BT[r, c, tk],
                                     start=True, stop=True)
                        ins.then_inc(S("ab_t"), 1)

                        def four(bank_, a, b_, sem):
                            for u in range(4):
                                ins = mm(bank_[:, u * P:(u + 1) * P], a[:, u, :], b_[:, u, :], start=True, stop=True)
                            ins.then_inc(S(sem), 1)

                        pe.wait_ge(S("ab_masked"), 6 * (u4 + 1))
                        pe.wait_ge(S("DmT_made"), u4 + 1)
                        four(mix[1], DmT, Dm, "n_sq")
                        four(mix[2], Dm, DmT, "n_sq")
                        for u, c, po, h in heads:
                            ins = mm(mix[0][:, u * CH:(u + 1) * CH], AM[:, u, 2 * P:3 * P], TM[:, 0, h * HD:(h + 1) * HD],
                                     start=True, stop=True)
                        ins.then_inc(S("akv_t"), 1)
                        pe.wait_ge(S("Z_first"), u4 + 1)
                        pe.wait_ge(S("sq_made"), 5 * u4 + 2)
                        four(lin[0], D2T, D2, "n_sq")
                        four(lin[1], D2, D2T, "n_sq")
                        four(mix[3], D2, Zt, "z_t")
                        pe.wait_ge(S("sq_made"), 5 * u4 + 4)
                        four(lin[3], D4T, D4, "n_sq")
                        pe.wait_ge(S("Z_made"), 5 * u4 + 1)
                        four(lin[2], D4, Zt, "z_t")
                        pe.wait_ge(S("sq_made"), 5 * u4 + 5)
                        pe.wait_ge(S("Z_made"), 5 * u4 + 2)
                        pe.wait_ge(S("akv_made"), u4 + 1)
                        four(mix[0], D2, Zt, "z_t")
                        for r_, (mask, bt, bx, bz) in enumerate(((M32, mix[1], mix[2], mix[3]), (M64, lin[0], lin[1], lin[2]))):
                            pe.wait_ge(S("Z_made"), 5 * u4 + 3 + r_)
                            four(bx, mask, Zt, "x_t")
                            for u in range(4):
                                ins = nc.tensor.transpose(bt[:, u * P:(u + 1) * P], Zt[:, u, :], ident)
                            ins.then_inc(S("t_t"), 1)
                            pe.wait_ge(S("t_made"), 2 * u4 + r_ + 1)
                            pe.wait_ge(S("x_made"), 2 * u4 + r_ + 1)
                            four(bz, Tt, Xa, "z_t")
                        pe.wait_ge(S("Z_made"), 5 * u4 + 5)
                        for u, c, po, h in heads:
                            mm(mix[0][:, u * P:u * P + CH], Zt[:, u, :], akv[:, u, :], start=True, stop=True)
                            ins = mm(mix[0][:, u * P + CH:(u + 1) * P], Zt[:, u, :], TM[:, 3, h * HD:(h + 1) * HD],
                                     start=True, stop=True)
                        ins.then_inc(S("gh_t"), 1)
                        pe.wait_ge(S("gh_made"), u4 + 1)
                        for u, c, po, h in heads:
                            ins = mm(mix[1][po:po + 64, (u // 2) * P:(u // 2 + 1) * P], GH[:, u, CH:2 * CH],
                                     AM[:, u, P:2 * P], start=True, stop=True)
                        ins.then_inc(S("q_t"), 1)
                        for u, c, po, h in heads:
                            o = mix[2][po:po + 64, (u // 2) * P:(u // 2 + 1) * P]
                            mm(o, GH[:, u, 0:CH], AM[:, u, P:2 * P], start=True, stop=False)
                            ins = mm(o, TM[:, 0, h * HD:(h + 1) * HD], AM[:, u, 3 * P:4 * P], start=False, stop=True)
                        ins.then_inc(S("y_t"), 1)
                        for c2 in range(2):
                            n = 2 * m + c2
                            if n == NC - 1:
                                continue
                            r = slice(64 * c2, 64 * c2 + 64)
                            for u, c, po, h in heads:
                                col = slice((u // 2) * CH, (u // 2 + 1) * CH)
                                hc = slice(h * HD, (h + 1) * HD)
                                mm((mix[3], lin[0])[c2][po:po + 64, col], GH[r, u, CH:2 * CH], TM[r, 1, hc],
                                   start=True, stop=True)
                                mm((lin[2], lin[1])[c2][po:po + 64, col], TM[r, 1, hc], GH[r, u, 0:CH],
                                   start=True, stop=False)
                                ins = mm((lin[2], lin[1])[c2][po:po + 64, col], TM[r, 2, hc], TM[r, 0, hc],
                                         start=False, stop=True)
                            ins.then_inc(S("e_t"), 1)
                pe.wait_ge(S("E_made"), 24)
                pe.wait_ge(S("Q_made"), 4)
                pe.wait_ge(S("y_done"), 4)
                for n in range(1, 3):
                    pe.wait_ge(S("S_made"), n)
                    for po in range(2):
                        r = slice(64 * po, 64 * po + 64)
                        for c in range(CT):
                            ins = mm(mix[2 * (n % 2) + po][r, c * CH:(c + 1) * CH], ETs[r, n, c, :], St[r, n - 1, c, :],
                                     start=True, stop=True)
                    ins.then_inc(S("s_t"), 1)
                for n in range(3):
                    pe.wait_ge(S("S_made"), n + 1)
                    for po in range(2):
                        r = slice(64 * po, 64 * po + 64)
                        t0 = (n + 1) * CH
                        for c in range(CT):
                            ins = mm(YSB[n][po][r, c * CH:(c + 1) * CH], St[r, n, c, :],
                                     AR[r, c, t0 // P, 1, t0 % P:t0 % P + CH], start=True, stop=True)
                    ins.then_inc(S("ys_t"), 1)
                pe.wait_ge(S("y_complete"), 1)
                for c in range(2):
                    mm(lin[c][:, :], cc("head_ones"), Yc[:, 2 * c:2 * c + 2, :], start=True, stop=True
                       ).then_inc(S("y_mean"), 1)
                for c in range(2):
                    for a in range(2):
                        ins = mm(mix[1 + c][:, a * T:(a + 1) * T], wgate[:, (2 * c + a) * P:(2 * c + a + 1) * P], sgx[:, :],
                                 start=True, stop=True)
                    ins.then_inc(S("gate_up"), 1)
                pe.wait_ge(S("y_squared"), 1)
                for c in range(CT):
                    ins = mm(mix[0][32 * c:32 * c + 32, 0:T], cc("pick"), ysq[:, c, :], start=True, stop=True)
                ins.then_inc(S("y_var"), 1)
                pe.wait_ge(S("y_inv"), 1)
                for c in range(2):
                    for a in range(2):
                        ins = mm(lin[2 + c][:, a * T:(a + 1) * T], cc("spread")[:, (2 * c + a) * P:(2 * c + a + 1) * P],
                                 yst[:, 1, :], start=True, stop=True)
                    ins.then_inc(S("y_spread"), 1)
                pe.wait_ge(S("y_lo_done"), 2)
                pe.wait_ge(S("u_used"), 1)

            def attention():
                pe.wait_ge(S("q_squared"), 1)
                pe.wait_ge(S("norm_ready"), 5)
                for m in range(2):
                    for c in range(8):
                        ins = mm(mix[0][:, m * QH + 2 * c:m * QH + 2 * c + 2], qsq[:, c, m * P:(m + 1) * P],
                                 cc("pick")[:, 0:2], start=True, stop=True)
                ins.then_inc(S("q_sums"), 1)
                for c in range(2):
                    ins = mm(mix[1][32 * c:32 * c + 32, 0:T], cc("pick"), qsq[:, 8 + c, :], start=True, stop=True)
                ins.then_inc(S("q_sums"), 1)
                for m in range(2):
                    for c in range(2):
                        ins = nc.tensor.transpose(mix[3][:, (2 * m + c) * P:(2 * m + c + 1) * P],
                                                  qz[:, 10 + c, m * P:(m + 1) * P], ident)
                ins.then_inc(S("v_t"), 1)
                pe.wait_ge(S("rk_made"), 1)
                for c in range(2):
                    ins = mm(mix[2][:, c * T:(c + 1) * T], cc("spread")[0:64, c * P:(c + 1) * P], rk[0:64, 1, :],
                             start=True, stop=True)
                ins.then_inc(S("rk_spread"), 1)
                pe.wait_ge(S("k_scaled"), 1)
                pe.wait_ge(S("q_gained"), 10)
                pe.wait_ge(S("evacuated"), steps_to(9))
                for k, c in enumerate((4, 0, 1, 2, 3)):
                    if k >= 2:
                        pe.wait_ge(S("rot_used"), k - 1)
                    mm(lin[k % 2][:, :], cc("rope_swap"), qz[:, 2 * c:2 * c + 2, :], start=True, stop=True
                       ).then_inc(S("rot_t"), 1)
                pe.wait_ge(S("roped"), 5)
                pe.wait_ge(S("v_tok_made"), 1)

                def scores(it):
                    n, c, b = it // 8, it % 8, it % 2
                    if it >= 2:
                        pe.wait_ge(S("max_made"), it - 1)
                    for p in range(2):
                        r = slice(64 * p, 64 * p + 64)
                        ins = mm(mix[2 * b + p][:, 0:P * (n + 1)], qr[r, c, n * P:(n + 1) * P],
                                 qr[r, 8 + c // 4, 0:P * (n + 1)], start=True, stop=True)
                    ins.then_inc(S("scores_t"), 1)

                def transposes(it):
                    n, b = it // 8, it % 2
                    pe.wait_ge(S("p_made"), 2 * it + 2)
                    if it >= 2:
                        pe.wait_ge(S("pT_made"), it - 1)
                    for p in range(2):
                        for k in range(n + 1):
                            ins = nc.tensor.transpose(lin[b][:, (2 * p + k) * P:(2 * p + k + 1) * P],
                                                      sc[:, b, p, k * P:(k + 1) * P], ident)
                    ins.then_inc(S("p_t"), 1)

                def values(it):
                    n, c, b = it // 8, it % 8, it % 2
                    pe.wait_ge(S("pT_made"), it + 1)
                    if it >= 2:
                        pe.wait_ge(S("o_lo_done"), it - 1)
                    for p in range(2):
                        kv = 2 * (c // 4) + p
                        for k in range(n + 1):
                            ins = mm(lin[2 + b][64 * p:64 * p + 64, 0:P], v_tok[:, k, kv * HD:(kv + 1) * HD],
                                     pT[:, b, p, k, :], start=k == 0, stop=k == n)
                    ins.then_inc(S("pv"), 1)

                scores(0)
                for it in range(16):
                    if it + 1 < 16:
                        scores(it + 1)
                    transposes(it)
                    if it >= 1:
                        values(it - 1)
                values(15)
                pe.wait_ge(S("o_lo_done"), 16)

            pe.wait_ge(S("setup"), 1)
            for n, (name, steps, tiles, inst) in enumerate(LINEARS):
                step(n, 0, 0)
                if n - 1 in NORM_NO:
                    stats(NORM_NO[n - 1])
                step(n, 1, 1)
                if name == "w_in":
                    for j in range(2, steps):
                        step(n, j, j)
                        during_w_in(j)
                    rwkv_gmlp()
                elif name == "down":
                    rounds(pe, 2, steps, lambda j, q, i: step(n, j, q, i))
                else:
                    rounds(pe, 2, steps, lambda j, q, i: step(n, j, q, i))
                    if name == "qkv":
                        attention()


def v3(bank):
    return bank[:, :].rearrange("p (u t) -> p u t", u=4)


def tok4(AR, which):
    return AR[:, :, :, which, :]


def constants():
    import numpy as np
    c = np.zeros((P, NCON), np.float32)

    def put(name, a):
        c[:, CCOLS[name][0]:CCOLS[name][0] + CCOLS[name][1]] = a

    i, j = np.arange(P)[:, None], np.arange(P)[None, :]
    put("ident", i == j)
    put("head_ones", i // HD == j // HD)
    swap = np.zeros((P, P))
    for f in range(P):
        if f % HD < HD // 2:
            swap[f + HD // 2, f] = -1
        else:
            swap[f - HD // 2, f] = 1
    put("rope_swap", swap)
    same = i // CH == j // CH
    put("mask_pair", np.concatenate([same & (i < j), same & (i <= j)] * 2, 1))
    put("mask16", (i // 16 == j // 16) & (i > j))
    put("mask16T", (i // 16 == j // 16) & (i < j))
    put("mask32", (i // 32 == j // 32) & (i // 16 > j // 16))
    put("mask64", (i // 64 == j // 64) & (i // 32 > j // 32))
    put("causal", i <= j)
    put("window", np.where(np.concatenate([j > i, j <= i], 1), 0.0, -1e30))
    put("restart", (np.arange(T)[None, :] % CH != 0) * np.ones((P, 1)))
    pick = np.zeros((P, 32))
    pick[:HD, 0] = 1
    pick[HD:, 1] = 1
    put("pick", pick)
    spread = np.zeros((P, CT, P))
    for t in range(CT):
        spread[32 * t, t, :HD] = 1
        spread[32 * t + 1, t, HD:] = 1
    put("spread", spread.reshape(P, CT * P))
    return c


def kernel(x, positions, ffn1_norm, ffn1_w_gate, ffn1_w_up, ffn1_w_down, mix_norm,
           ffn2_norm, ffn2_w_gate, ffn2_w_up, ffn2_w_down,
           ab_w_in, ab_mu_shift, rwkv_w0, rwkv_w_decay_up, rwkv_a0, rwkv_w_aaa_up, rwkv_w_gate_up,
           rwkv_k_k, rwkv_k_a, rwkv_r_k, rwkv_gn_gain, rwkv_gn_bias,
           sg_ln_gain, sg_ln_bias, sg_w_spatial, sg_b_spatial, ab_w_out,
           attn_w_qkv, attn_b_qkv, attn_q_norm, attn_k_norm, attn_sinks, attn_w_o, attn_b_o):
    import numpy as np
    import concourse.bacc as bacc
    from concourse.bass_utils import run_bass_kernel_spmd

    A = np.asarray

    def tiles(w, n_tile):
        w = A(w)
        K, N = w.shape
        return w.reshape(K // P, P, N // n_tile, n_tile).transpose(2, 1, 0, 3)

    def pairs(w):
        t = tiles(w, P)
        n = t.shape[0]
        return t.reshape(n // 2, 2, P, KD, P).transpose(0, 2, 1, 3, 4).reshape(n // 2, P, 2 * KD * P)

    def feature(v):
        return A(v).reshape(-1, P).T

    gu = []
    for wg, wu in ((ffn1_w_gate[0], ffn1_w_up[0]), (ffn2_w_gate[0], ffn2_w_up[0]),
                   (ffn1_w_gate[1], ffn1_w_up[1]), (ffn2_w_gate[1], ffn2_w_up[1])):
        g, u = tiles(wg, P), tiles(wu, P)
        gu.append(np.stack([g, u], 2).reshape(KF, P, 2 * KD * P))
    down = [tiles(w, P).reshape(KD, P, KF * P)
            for w in (ffn1_w_down[0], ffn2_w_down[0], ffn1_w_down[1], ffn2_w_down[1])]
    w_in = A(ab_w_in[0])
    w_in = np.concatenate([w_in[:, ZA * P:], w_in[:, :ZA * P]], 1)
    order = [h for half in range(2) for i in range(4) for h in (8 * half + i, 8 * half + 4 + i)]
    cols = np.concatenate([np.arange(h * HD, (h + 1) * HD) for h in order])
    qcols = np.concatenate([cols, np.arange(QH * HD, 12 * P)])

    par = np.zeros((P, NPAR), np.float32)

    def put(name, a):
        par[:, PCOLS[name][0]:PCOLS[name][0] + PCOLS[name][1]] = a

    for layer in range(2):
        put(f"ffn1_norm{layer}", feature(ffn1_norm[layer]))
        put(f"mix_norm{layer}", feature(mix_norm[layer]))
        put(f"ffn2_norm{layer}", feature(ffn2_norm[layer]))
    for name, v in (("mu", ab_mu_shift), ("w0", rwkv_w0), ("a0", rwkv_a0), ("k_k", rwkv_k_k), ("k_a", rwkv_k_a),
                    ("r_k", rwkv_r_k), ("gn_gain", rwkv_gn_gain), ("gn_bias", rwkv_gn_bias), ("ln_gain", sg_ln_gain),
                    ("ln_bias", sg_ln_bias), ("b_o", attn_b_o)):
        put(name, feature(A(v)[0]))
    put("b_qkv", feature(A(attn_b_qkv)[0][qcols]))
    put("q_norm", np.tile(A(attn_q_norm)[0], 2)[:, None])
    put("k_norm", np.tile(A(attn_k_norm)[0], 2)[:, None])
    put("inv_freq", np.tile((10000.0 ** (-np.arange(0, HD, 2, dtype=np.float32) / np.float32(HD))
                             ).astype(np.float32), 4)[:, None])
    put("sinks", np.broadcast_to(A(attn_sinks)[0][order], (P, QH)))

    arrays = {
        "xT": A(x)[0].T.reshape(KD, P, T).transpose(1, 0, 2),
        "gu_w": np.concatenate(gu, 0),
        "down_w": np.concatenate(down, 0),
        "w_in": pairs(w_in),
        "w_out": pairs(ab_w_out[0]),
        "w_qkv": pairs(A(attn_w_qkv[0])[:, qcols]),
        "w_o": pairs(A(attn_w_o[0])[cols, :]),
        "params": par,
        "consts": constants(),
        "positions": np.broadcast_to(A(positions), (P, T)),
        "w_lora": np.concatenate([A(rwkv_w_decay_up)[0], A(rwkv_w_aaa_up)[0]], 0),
        "w_gate": A(rwkv_w_gate_up)[0],
        "w_spatialT": A(sg_w_spatial)[0].transpose(2, 0, 1),
        "b_spatial": np.broadcast_to(A(sg_b_spatial)[0], (P, 4, P)),
    }
    nc = bacc.Bacc("TRN2", target_bir_lowering=False, num_devices=1)
    args, ins = {}, {}
    for name, a in arrays.items():
        a = np.ascontiguousarray(a)
        ins[f"in_{name}"] = a
        args[name] = nc.dram_tensor(f"in_{name}", a.shape, mybir.dt.from_np(a.dtype), kind="ExternalInput").ap()
    args["out"] = nc.dram_tensor("out_x", (P, KD, T), F32, kind="ExternalOutput").ap()
    build(nc, **args)
    r = run_bass_kernel_spmd(nc, [ins], core_ids=[0])
    got = r.results[0]["out_x"]
    return got.transpose(1, 0, 2).reshape(D, T).T.reshape(1, T, D)
```

```python
from contextlib import ExitStack

import concourse.bass as bass
from concourse import mybir

F32 = mybir.dt.float32
F32R = mybir.dt.float32r
I32 = mybir.dt.int32
ALU = mybir.AluOpType
ACT = mybir.ActivationFunctionType
AX = mybir.AxisListType.X

P = 128
D = 1024
T = 256
KD = D // P
FF = 2816
KF = FF // P
SUB = KF // 2
HD = 64
AH = 8
AW = 512
CT = AW // P
ZA = 14
ZB = 8
CH = 64
NC = T // CH
QH = 16
RMS_EPS, GN_EPS, LN_EPS = 1e-6, 64e-5, 1e-5
KAPPA = 0.6065306597126334

PCOLS = {}
_at = 0
for _name, _n in (("ffn1_norm0", 8), ("ffn1_norm1", 8), ("mix_norm0", 8), ("mix_norm1", 8), ("ffn2_norm0", 8),
                  ("ffn2_norm1", 8), ("mu", ZA), ("w0", 4), ("a0", 4), ("k_k", 4), ("k_a", 4), ("r_k", 4),
                  ("gn_gain", 4), ("gn_bias", 4), ("ln_gain", 4), ("ln_bias", 4), ("b_qkv", 12), ("q_norm", 1),
                  ("k_norm", 1), ("b_o", 8), ("inv_freq", 1), ("sinks", QH)):
    PCOLS[_name] = (_at, _n)
    _at += _n
NPAR = _at

CCOLS = {}
_at = 0
for _name, _n in (("ident", P), ("head_ones", P), ("rope_swap", P), ("mask_pair", 4 * P), ("mask16", P),
                  ("mask16T", P), ("mask32", P), ("mask64", P), ("causal", P), ("window", 2 * P), ("restart", T),
                  ("pick", 32), ("spread", CT * P),
                  ("ident64", CH)):
    CCOLS[_name] = (_at, _n)
    _at += _n
NCON = _at

LINEARS = (("gu", 22, 8, 0), ("down", 8, SUB, 0), ("w_in", 11, 8, 0), ("w_out", 4, 8, 0), ("gu", 22, 8, 1),
           ("down", 8, SUB, 1), ("gu", 22, 8, 2), ("down", 8, SUB, 2), ("qkv", 6, 8, 0), ("w_o", 4, 8, 0),
           ("gu", 22, 8, 3), ("down", 8, SUB, 3))
FIRST = [sum(x[1] for x in LINEARS[:n]) for n in range(len(LINEARS))]


def build(nc, xT, gu_w, down_w, w_in, w_out, w_qkv, w_o, params, consts, positions, w_lora, w_gate,
          w_spatialT, b_spatial, out):
    with ExitStack() as ctx:
        def sb(name, shape, dt=F32):
            return ctx.enter_context(nc.sbuf_tensor(name, shape, dt))

        def ps(name):
            return ctx.enter_context(nc.psum_tensor(name, [P, 512], F32))

        sems = {}

        def S(name):
            if name not in sems:
                sems[name] = ctx.enter_context(nc.semaphore(name))
            return sems[name]

        raw = sb("raw", [P, 4, 2 * SUB * P])
        split_ring = nc.sbuf_base
        w_hi = sb("w_hi", [P, 4, SUB * P], F32R)
        w_lo = sb("w_lo", [P, 4, SUB * P], F32R)
        x = sb("x", [P, KD, T])
        par = sb("par", [P, NPAR])
        con = sb("con", [P, NCON])
        sq = sb("sq", [P, 2, T])
        ssq = sb("ssq", [P, 2, T])
        root = sb("root", [P, T])
        rB = sb("rB", [P, T])
        ones = sb("ones", [P, P])
        eps = sb("eps", [P, 4])
        base = nc.sbuf_base
        base += -base % 32
        room = nc.sbuf_usable_end - base
        arena = sb("arena", [P, room // 4 - 16])

        def at(name, off, shape, dt=F32):
            n = 4
            for s in shape[1:]:
                n *= s
            assert off % 32 == 0 and off + n <= room - 64, (name, off, n, room)
            return nc.alloc_sbuf_tensor_at(name, shape, dt, offset=base + off)

        KB = 1024
        TEMP = 0
        FREE = 8 * KB
        HOFF = FREE + (room - 64 - 8 * KB - 16 * KB - 44 * KB) // 32 * 32
        AHI = HOFF + 16 * KB
        ALO = AHI + 22 * KB
        pre = at("pre", TEMP, [P, 2, 2, T])
        sil = at("sil", TEMP + 4 * KB, [P, 2, T])
        act_f = at("act_f", TEMP + 6 * KB, [P, 2, T])
        h_hi = at("h_hi", HOFF, [P, KD, T], F32R)
        h_lo = at("h_lo", HOFF + 8 * KB, [P, KD, T], F32R)
        a_hi = at("a_hi", AHI, [P, KF, T], F32R)
        a_lo = at("a_lo", ALO, [P, KF, T], F32R)
        y_hi = a_hi[:, KF - KD:KF, :]
        y_lo = a_lo[:, 0:KD, :]

        lin = [ps(f"lin{i}") for i in range(4)]
        mix = [ps(f"mix{i}") for i in range(4)]
        banks = mix + lin

        def pc(name, j=0, n=1, rows=slice(0, P)):
            return par[rows, PCOLS[name][0] + j:PCOLS[name][0] + j + n]

        def cc(name):
            a, n = CCOLS[name]
            return con[:, a:a + n]

        ident = cc("ident")

        zz = at("zz", FREE, [P, ZA + ZB, T + 1])
        ZBYTES = (ZA + ZB) * (T + 1) * 4
        zs = at("zs", ALO + 8 * KB, [P, ZA, T])
        gt = at("gt", AHI, [P, 4, T])
        g_mean = at("g_mean", AHI + 4 * KB, [P, T])
        g_rstd = at("g_rstd", AHI + 5 * KB, [P, T])
        s_tok = at("s_tok", AHI + 6 * KB, [P, 2, AW])
        wsT = at("wsT", AHI + 10 * KB, [P, 4, P])
        bsp = at("bsp", AHI + 12 * KB, [P, 4, P])
        sd = at("sd", HOFF, [P, CT, T])
        cs = at("cs", HOFF + 4 * KB, [P, CT, T])
        ep = at("ep", HOFF + 8 * KB, [P, CT, T])
        ic = at("ic", HOFF + 12 * KB, [P, CT, T])
        kq = at("kq", AHI + 14 * KB, [P, CT, T])
        AR = at("AR", AHI + 4 * KB, [P, CT, 2, 2, P])
        th = at("th", ALO, [P, T])
        sgx = at("sgx", ALO + 3 * KB, [P, T])
        z_b_off = FREE + (ZA * (T + 1) * 4 + 31) // 32 * 32 + 32
        BT = at("BT", z_b_off, [P, CT, T])
        KT = at("KT", z_b_off + 4 * KB, [P, CT, T])
        bonus = at("bonus", z_b_off + 8 * KB, [P, CT, T])
        RING = split_ring - base
        TM = [at("TM0", FREE, [P, 5, AW]), at("TM1", RING + 32 * KB, [P, 5, AW])]
        Yc = at("Yc", FREE + 10 * KB, [P, CT, T])
        lora = at("lora", TEMP, [P, AW])
        wgate = at("wgate", TEMP + 2 * KB, [P, AW])
        St = at("St", TEMP + 4 * KB, [P, 3, CT, CH])
        pend = at("pend", TEMP + 7 * KB, [P, CT, NC])
        kfb = at("kfb", TEMP + 7 * KB + 128, [P, 4])
        AM = [at("AM0", ALO + 8 * KB, [P, 4, 4 * P]), at("AM1", RING, [P, 4, 4 * P])]

        def four_mats(name, off0, off1):
            return [at(f"{name}{i}", off, [P, 4, P]) for i, off in enumerate((off0, off1))]

        Dm, DmT, M32, M64, D2, D2T, D4, D4T = [four_mats(name, HOFF + 2 * KB * i, RING + 8 * KB + 2 * KB * i)
                                               for i, name in enumerate(("Dm", "DmT", "M32", "M64", "D2", "D2T",
                                                                         "D4", "D4T"))]
        Zt = four_mats("Zt", AHI, RING + 24 * KB)
        Tt = four_mats("Tt", AHI + 2 * KB, RING + 26 * KB)
        Xa = four_mats("Xa", AHI + 12 * KB, RING + 28 * KB)
        HG = four_mats("HG", ALO + 20 * KB, RING + 30 * KB)
        ETs = at("ETs", AHI + 14 * KB, [P, 3, CT, CH])
        Fs = at("Fs", ALO, [P, 3, CT, CH])
        ysq = at("ysq", HOFF + 4 * KB, [P, CT, T])
        yst = at("yst", HOFF + 8 * KB, [P, 2, T])
        ROUNDS, NSC = 8, 3
        qz = at("qz", FREE, [P, 12, T])
        cosT = at("cosT", FREE + 12 * KB, [P, T])
        sinT = at("sinT", FREE + 13 * KB, [P, T])
        posf = at("posf", FREE + 14 * KB, [P, T])
        posi = at("posi", FREE + 15 * KB, [P, T], I32)
        swap = at("swap", FREE + 16 * KB, [P, 2, P])
        sm = at("sm", FREE + 17 * KB, [P, NSC, 8, 4])
        nsink = at("nsink", FREE + 17 * KB + 384, [P, QH])
        rq = at("rq", FREE + 17 * KB + 512, [P, 2, QH])
        trot = at("trot", FREE + 18 * KB, [P, 2, 2, T])
        v_tok = at("v_tok", FREE + 22 * KB, [P, 2, T])
        rk = at("rk", FREE + 24 * KB, [P, 2, T])
        qr = at("qr", AHI, [P, 10, T])
        qsq = at("qsq", ALO + 8 * KB, [P, 10, T])
        sc = at("sc", HOFF, [P, NSC, 2, 2, T])
        pT = at("pT", HOFF + 12 * KB, [P, 2, 2, 2, P])

        YSB = [(lin[0], lin[1]), (lin[2], lin[3]), (mix[0], mix[1])]

        block = ctx.enter_context(nc.Block())

        def rounds(eng, n0, n1, body):
            full = (n1 - n0) // 4
            if full >= 2:
                with eng.Fori(0, full) as i:
                    for q in range(4):
                        body(n0 + q + 4 * i, n0 + q, i)
            else:
                for i in range(full):
                    for q in range(4):
                        body(n0 + q + 4 * i, n0 + q, i)
            for q in range(4 * full, n1 - n0):
                body(n0 + q, n0 + q, 0)

        GAIN_AFTER = {1: "mix_norm0", 3: "ffn2_norm0", 5: "ffn1_norm1", 7: "mix_norm1", 9: "ffn2_norm1"}
        NORM_NO = {-1: 1, 1: 2, 3: 3, 5: 4, 7: 5, 9: 6}
        HBASE = {-1: 0, 1: 8, 3: 16, 5: 24, 7: 32, 9: 40}

        def steps_to(n):
            return 4 + FIRST[n]

        def needed_norm(n):
            return NORM_NO[n - 1]

        @block.sync
        def _(sp):
            sp.dma_start(par[:, :], params).then_inc(S("params_loaded"), 16)
            sp.dma_start(x[:, 0:2, :], xT[:, 0:2, :]).then_inc(S("x_first"), 16)
            sp.dma_start(x[:, 2:KD, :], xT[:, 2:KD, :]).then_inc(S("x_loaded"), 16)
            srcs = {"gu": gu_w, "down": down_w, "w_in": w_in, "w_out": w_out, "qkv": w_qkv, "w_o": w_o}
            for n, (name, steps, tiles, inst) in enumerate(LINEARS):
                g0, src = FIRST[n], srcs[name]
                off = inst * steps if name in ("gu", "down") else 0

                def load(j, q, i):
                    slot = (g0 + q) % 4
                    if n > 0 or q >= 4:
                        sp.wait_ge(S("lo_done"), 2 * (g0 + j - 4) + 2)
                    sp.dma_start(raw[:, slot, 0:2 * tiles * P],
                                 src[bass.ds(off + j, 1), :, :].rearrange("a p n -> (a p) n")
                                 ).then_inc(S(f"raw_full{slot}"), 16)

                if n == 0:
                    for j in range(4):
                        load(j, j, 0)
                    sp.dma_start(con[:, :], consts).then_inc(S("consts_loaded"), 16)
                    rounds(sp, 4, steps, load)
                else:
                    rounds(sp, 0, steps, load)
                if name == "w_in":
                    sp.wait_ge(S("evacuated"), steps_to(2))
                    sp.dma_start(wsT[:, :, :], w_spatialT).then_inc(S("spatial_loaded"), 16)
                    sp.dma_start(bsp[:, :, :], b_spatial).then_inc(S("spatial_loaded"), 16)
                    sp.dma_start(lora[:, :], w_lora).then_inc(S("lora_loaded"), 16)
                    sp.dma_start(wgate[:, :], w_gate).then_inc(S("lora_loaded"), 16)
                if n == 6:
                    sp.dma_start(posi[:, :], positions).then_inc(S("pos_loaded"), 16)
            for k0, k1 in ((0, KD - 2), (KD - 2, KD)):
                sp.wait_ge(S("evacuated"), steps_to(11) + k1)
                sp.dma_start(out[:, k0:k1, :], x[:, k0:k1, :]).then_inc(S("stored"), 16)
            sp.wait_ge(S("stored"), 32)

        @block.scalar
        def _(act):
            link_at = [0]

            def link(ins):
                link_at[0] += 1
                ins.then_inc(S("act_link"), 1)
                act.wait_ge(S("act_link"), link_at[0])

            def split_hi(n, j, q, i=0):
                _, _, tiles, _ = LINEARS[n]
                g0 = FIRST[n]
                slot = (g0 + q) % 4
                for s in range(2):
                    if s == 0:
                        act.wait_ge(S(f"raw_full{slot}"), 16 * ((g0 + q) // 4 + 1 + i))
                    if n > 0 or q >= 2:
                        act.wait_ge(S("sub_done"), 2 * (g0 + j - 2) + s + 1)
                    nc.scalar.activation(w_hi[:, (2 * (g0 + q) + s) % 4, 0:tiles * P],
                                         raw[:, slot, s * tiles * P:(s + 1) * tiles * P],
                                         ACT.Copy).then_inc(S("hi_done"), 1)

            def silu(n, j, q):
                m = KF * LINEARS[n][3] + j
                act.wait_ge(S("evacuated"), steps_to(n) + j + 1)
                act.wait_ge(S("act_made"), m + 1)
                nc.scalar.activation(sil[:, q % 2, :], pre[:, q % 2, 0, :], ACT.Silu).then_inc(S("silu_done"), 1)

            def hi_of_h(n, k):
                nc.scalar.activation(h_hi[:, k, :], x[:, k, :], ACT.Copy,
                                     scale=pc(GAIN_AFTER.get(n, "ffn1_norm0"), k)).then_inc(S("h_hi_done"), 1)

            def square(n, k):
                m = HBASE[n] + k
                if m >= 2:
                    act.wait_ge(S("sq_added"), m - 1)
                nc.scalar.activation(sq[:, k % 2, :], x[:, k, :], ACT.Square).then_inc(S("sq_done"), 1)

            def norm_root(no):
                act.wait_ge(S("stats_done"), no)
                if no > 1:
                    act.wait_ge(S("norm_ready"), no - 1)
                nc.scalar.activation(root[:, :], mix[0][:, 0:T], ACT.Sqrt, scale=1.0 / D,
                                     bias=eps[:, 0:1]).then_inc(S("root_done"), 1)

            def late(n, j, q):
                name = LINEARS[n][0]
                if name == "gu":
                    silu(n, j, q)
                elif n in GAIN_AFTER:
                    act.wait_ge(S("evacuated"), steps_to(n) + j + 1)
                    for k in ((j,) if name == "down" else (2 * j, 2 * j + 1)):
                        hi_of_h(n, k)
                        square(n, k)
                elif name == "w_in" and j == 3:
                    act.wait_ge(S("evacuated"), steps_to(n) + 4)
                    nc.scalar.activation(zz[:, 18:22, 1:T + 1], zz[:, 18:22, 1:T + 1], ACT.Gelu).then_inc(S("s_gelu"), 1)
                    nc.scalar.activation(zz[:, 14:18, 1:T + 1], zz[:, 14:18, 1:T + 1], ACT.Gelu).then_inc(S("u_gelu"), 1)
                elif name == "w_in" and j == 6:
                    act.wait_ge(S("s_centred"), 1)
                    nc.scalar.activation(gt[:, :, :], zz[:, 18:22, 1:T + 1], ACT.Square).then_inc(S("s_squared"), 1)
                elif name == "w_in" and j == 10:
                    act.wait_ge(S("s_var"), 1)
                    nc.scalar.activation(g_rstd[:, :], mix[1][:, T:2 * T], ACT.Sqrt, scale=1.0 / AW,
                                         bias=eps[:, 1:2]).then_inc(S("s_root"), 1)
                elif name == "qkv":
                    if j == 4:
                        act.wait_ge(S("k_sums"), 1)
                        nc.scalar.activation(rk[0:64, 0, :], mix[0][0:64, T:2 * T], ACT.Sqrt, scale=1.0 / HD,
                                             bias=eps[0:64, 0:1]).then_inc(S("rk_root"), 1)
                    act.wait_ge(S("evacuated"), steps_to(n) + j + 1)
                    for f in (2 * j, 2 * j + 1):
                        nc.scalar.activation(qz[:, f, :], qz[:, f, :], ACT.Identity,
                                             bias=pc("b_qkv", f)).then_inc(S("qkv_biased"), 1)
                    if j != 1:
                        act.wait_ge(S("qkv_biased"), 2 * j + 2)
                        nc.scalar.activation(qsq[:, max(2 * j - 2, 0):max(2 * j - 2, 0) + 2, :], qz[:, 2 * j:2 * j + 2, :],
                                             ACT.Square).then_inc(S("q_squared"), 1)

            def rwkv_gmlp():
                act.wait_ge(S("s_scaled"), 1)
                for f in range(4):
                    nc.scalar.activation(zz[:, 18 + f, 1:T + 1], zz[:, 18 + f, 1:T + 1], ACT.Identity,
                                         scale=pc("ln_gain", f), bias=pc("ln_bias", f)).then_inc(S("s_normed"), 1)
                act.wait_ge(S("mixed"), ZA)
                nc.scalar.activation(th[0:64, :], zs[0:64, 12, :], ACT.Tanh).then_inc(S("tanh_done"), 1)
                for c in range(CT):
                    nc.scalar.activation(kq[:, c, :], zs[:, 4 + c, :], ACT.Copy, scale=pc("k_k", c)
                                         ).then_inc(S("kq_made"), 1)
                act.wait_ge(S("kq_made"), CT)
                nc.scalar.activation(cs[:, :, :], kq[:, :, :], ACT.Square).then_inc(S("kq_squared"), 1)
                nc.scalar.activation(sgx[:, :], zs[:, 13, :], ACT.Sigmoid).then_inc(S("gate_in"), 1)
                act.wait_ge(S("decay_up"), 1)
                for c in range(CT):
                    nc.scalar.activation(sd[:, c, :], lin[c // 2][:, (c % 2) * T:(c % 2 + 1) * T], ACT.Sigmoid,
                                         bias=pc("w0", c)).then_inc(S("sd_made"), 1)
                act.wait_ge(S("iclr_up"), 1)
                for c in range(CT):
                    nc.scalar.activation(ic[:, c, :], lin[2 + c // 2][:, (c % 2) * T:(c % 2 + 1) * T], ACT.Sigmoid,
                                         bias=pc("a0", c)).then_inc(S("ic_made"), 1)
                act.wait_ge(S("u_used"), 1)
                act.wait_ge(S("kfb_made"), 1)
                act.wait_ge(S("ic_made"), CT)
                for c in range(CT):
                    nc.scalar.activation(BT[:, c, :], ic[:, c, :], ACT.Identity, scale=pc("k_a", c),
                                         bias=kfb[:, c:c + 1]).then_inc(S("kf_made"), 1)
                act.wait_ge(S("kk_sums"), 1)
                nc.scalar.activation(root[:, :], mix[0][:, 0:T], ACT.Sqrt).then_inc(S("kk_root"), 1)
                act.wait_ge(S("cs_made"), 1)
                nc.scalar.activation(ep[:, :, :], cs[:, :, :], ACT.Exp, scale=-KAPPA).then_inc(S("ep_made"), 1)
                act.wait_ge(S("csm_made"), 1)
                nc.scalar.activation(sd[:, :, :], sd[:, :, :], ACT.Exp, scale=-KAPPA).then_inc(S("pprev_made"), 1)
                nc.scalar.activation(cs[:, :, :], cs[:, :, :], ACT.Exp, scale=KAPPA).then_inc(S("en_made"), 1)

                def copy(dst, src, wait, value, done):
                    act.wait_ge(S(wait), value)
                    nc.scalar.activation(dst, src, ACT.Copy).then_inc(S(done), 1)

                for i in range(8):
                    copy(TM[i % 2][:, (0, 3, 2, 1)[i // 2], :], (lin[2], lin[3], mix[0], mix[1])[i % 4][:, :],
                         "tok_t", i + 1, "tok_made")
                for m in range(2):
                    def both(src, wait, value, done, dst):
                        for h in range(2):
                            copy(dst(h), v3(banks[4 * h + src]), wait, of_half(value, h), done)

                    for h in range(2):
                        copy(TM[m][:, 4, 4 * CH * h:4 * CH * (h + 1)], banks[4 * h + 2][:, 0:4 * CH],
                             "akv_t", of_half(m + 1, h), "akv_made")
                    for h in range(2):
                        copy(D2[h][:, :, :], v3(banks[4 * h]), f"n_sq{h}", 5 * m + 1, f"sq_made{h}")
                        copy(D2T[h][:, :, :], v3(banks[4 * h + 1]), f"n_sq{h}", 5 * m + 2, f"sq_made{h}")
                    for h in range(2):
                        copy(D4[h][:, :, :], v3(banks[4 * h + 2]), f"n_sq{h}", 5 * m + 3, f"sq_made{h}")
                        copy(D4T[h][:, :, :], v3(banks[4 * h + 3]), f"n_sq{h}", 5 * m + 4, f"sq_made{h}")
                    for h in range(2):
                        copy(D2[h][:, :, :], v3(banks[4 * h + 1]), f"n_sq{h}", 5 * m + 5, f"sq_made{h}")
                    both(1, "t_t", 2 * m + 1, "t_made", lambda h: Tt[h][:, :, :])
                    both(0, "t_t", 2 * m + 2, "t_made", lambda h: Tt[h][:, :, :])
                    both(2, "hg_t", m + 1, "hg_made", lambda h: HG[h][:, :, :])
                    for h in range(2):
                        copy(Yc[:, 2 * h:2 * h + 2, m * P:(m + 1) * P],
                             banks[4 * h][:, 0:2 * P].rearrange("p (c t) -> p c t", c=2), "y_t", of_half(m + 1, h), "y_done")
                act.wait_ge(S("e_t0"), 3)
                act.wait_ge(S("e_t1"), 3)
                for j in range(2):
                    split_hi(3, j, j)
                act.wait_ge(S("y_centred"), 1)
                nc.scalar.activation(ysq[:, :, :], Yc[:, :, :], ACT.Square).then_inc(S("y_squared"), 1)
                act.wait_ge(S("y_var"), 1)
                nc.scalar.activation(yst[:, 0, :], mix[0][:, 0:T], ACT.Sqrt, scale=1.0 / HD,
                                     bias=eps[:, 2:3]).then_inc(S("y_root"), 1)
                act.wait_ge(S("y_scaled"), 2)
                for c in range(CT):
                    nc.scalar.activation(Yc[:, c, :], Yc[:, c, :], ACT.Identity, scale=pc("gn_gain", c),
                                         bias=pc("gn_bias", c)).then_inc(S("y_normed"), 1)
                for c in range(2):
                    act.wait_ge(S("y_gated"), c + 1)
                    nc.scalar.activation(y_hi[:, 2 * c:2 * c + 2, :], Yc[:, 2 * c:2 * c + 2, :], ACT.Copy
                                         ).then_inc(S("y_hi_done"), 1)

            def attention():
                act.wait_ge(S("q_sums"), 1)
                nc.scalar.activation(rq[:, :, :], mix[0][:, 0:2 * QH].rearrange("p (m h) -> p m h", m=2), ACT.Sqrt,
                                     scale=1.0 / HD, bias=eps[:, 0:1]).then_inc(S("rq_root"), 1)

                def exps(g):
                    n, c, s4 = g // 4, 2 * (g % 4), g % NSC
                    act.wait_ge(S("max_made"), g + 1)
                    for i in range(2):
                        for p in range(2):
                            u = 2 * i + p
                            nc.scalar.activation(sc[:, s4, i, p, 0:P * (n + 1)], sc[:, s4, i, p, 0:P * (n + 1)], ACT.Exp,
                                                 scale=rq[:, n, 2 * c + u:2 * c + u + 1],
                                                 bias=sm[:, s4, 2, u:u + 1], accum_out=sm[:, s4, 4, u:u + 1]
                                                 ).then_inc(S("exp_made"), 1)
                    nc.scalar.activation(sm[:, s4, 5, :], sm[:, s4, 3, :], ACT.Exp).then_inc(S("exp_made"), 1)

                def probs(g):
                    n = g // 4
                    for i in range(2):
                        act.wait_ge(S("p_t"), 2 * g + i + 1)
                        src = lin[i][:, :].rearrange("p (h k q) -> p h k q", h=2, k=2)
                        nc.scalar.activation(pT[:, i, :, 0:n + 1, :], src[:, :, 0:n + 1, :], ACT.Copy
                                             ).then_inc(S("pT_made"), 1)

                def heads(g):
                    n, c = g // 4, 2 * (g % 4)
                    act.wait_ge(S("pv"), g + 1)
                    nc.scalar.activation(y_hi[:, c:c + 2, n * P:(n + 1) * P],
                                         lin[2 + g % 2][:, 0:T].rearrange("p (i q) -> p i q", i=2), ACT.Copy
                                         ).then_inc(S("o_hi_done"), 1)

                act.wait_ge(S("rq_made"), 1)
                exps(0)
                for g in range(ROUNDS):
                    if g + 1 < ROUNDS:
                        exps(g + 1)
                    if g >= 1:
                        act.wait_ge(S("pv"), g)
                    probs(g)
                    if g >= 1:
                        heads(g - 1)
                    nc.scalar.activation(x[:, g, :], x[:, g, :], ACT.Identity, bias=pc("b_o", g)
                                         ).then_inc(S("b_o_added"), 1)
                heads(ROUNDS - 1)

            act.wait_ge(S("setup"), 1)
            nc.scalar.activation(pre[:, 0, 0, 0:4], eps[:, :], ACT.Copy)
            act.wait_ge(S("params_loaded"), 16)
            act.wait_ge(S("x_first"), 16)
            for k in range(KD):
                if k == 2:
                    act.wait_ge(S("x_loaded"), 16)
                hi_of_h(-1, k)
            for j in range(2):
                split_hi(0, j, j)
                for k in range(4 * j, 4 * j + 4):
                    square(-1, k)
            for n, (name, steps, tiles, inst) in enumerate(LINEARS):
                if name not in ("w_out", "w_o"):
                    for j in range(2 if n else 0):
                        pn = LINEARS[n - 1][1] - 2 + j
                        late(n - 1, pn, pn)
                        split_hi(n, j, j)
                if n - 1 in NORM_NO:
                    norm_root(NORM_NO[n - 1])
                if name == "gu":
                    def step(j, q, i):
                        split_hi(n, j, q, i)
                        silu(n, j - 2, q - 2)
                    rounds(act, 2, steps, step)
                else:
                    for j in range(2, steps):
                        split_hi(n, j, j)
                        late(n, j - 2, j - 2)
                        if n == 7 and j == 7:
                            act.wait_ge(S("angles"), 1)
                            nc.scalar.activation(sinT[:, :], sinT[:, :], ACT.Sin).then_inc(S("rope_tables"), 1)
                            nc.scalar.activation(cosT[:, :], cosT[:, :], ACT.Sin).then_inc(S("rope_tables"), 1)
                if name in ("w_in", "qkv"):
                    for j in range(2):
                        late(n, steps - 2 + j, steps - 2 + j)
                    if name == "w_in":
                        rwkv_gmlp()
                    else:
                        for j in range(2):
                            split_hi(n + 1, j, j)
                        attention()

        @block.vector
        def _(dve):
            link_at = [0]

            def link(ins):
                link_at[0] += 1
                ins.then_inc(S("dve_link"), 1)
                dve.wait_ge(S("dve_link"), link_at[0])

            def split_lo(n, j, q, i=0):
                _, _, tiles, _ = LINEARS[n]
                g0 = FIRST[n]
                slot = (g0 + q) % 4
                for s in range(2):
                    dve.wait_ge(S("hi_done"), 2 * (g0 + j) + s + 1)
                    sub = (2 * (g0 + q) + s) % 4
                    nc.vector.tensor_tensor(w_lo[:, sub, 0:tiles * P], raw[:, slot, s * tiles * P:(s + 1) * tiles * P],
                                            w_hi[:, sub, 0:tiles * P].bitcast(F32), ALU.subtract
                                            ).then_inc(S("lo_done"), 1)

            def bank(n, q):
                return lin[(FIRST[n] + q) % 4]

            def scale_gu(n, j, q):
                m = KF * LINEARS[n][3] + j
                dve.wait_ge(S("sub_done"), 2 * (FIRST[n] + j) + 2)
                dve.wait_ge(S("act_made"), m + 1)
                nc.vector.tensor_tensor(pre[:, q % 2, :, :], bank(n, q)[:, :].rearrange("p (a t) -> p a t", a=2),
                                        rB[:, :].unsqueeze(1).to_broadcast([P, 2, T]), ALU.mult
                                        ).then_inc(S("evacuated"), 1)

            def new_h_lo(n, k):
                dve.wait_ge(S("h_hi_done"), HBASE[n] + k + 1)
                nc.vector.scalar_tensor_tensor(out=h_lo[:, k, :], in0=x[:, k, :],
                                               scalar=pc(GAIN_AFTER.get(n, "ffn1_norm0"), k),
                                               in1=h_hi[:, k, :].bitcast(F32), op0=ALU.mult, op1=ALU.subtract
                                               ).then_inc(S("h_ready"), 1)

            def late(n, j, q):
                name = LINEARS[n][0]
                if name == "gu":
                    return scale_gu(n, j, q)
                dve.wait_ge(S("sub_done"), 2 * (FIRST[n] + j) + 2)
                src = bank(n, q)
                if name == "down":
                    nc.vector.scalar_tensor_tensor(out=x[:, j, :], in0=src[:, 0:T], scalar=0.5, in1=x[:, j, :],
                                                   op0=ALU.mult, op1=ALU.add).then_inc(S("evacuated"), 1)
                    if n in GAIN_AFTER:
                        new_h_lo(n, j)
                elif name in ("w_out", "w_o"):
                    if name == "w_o" and j == 0:
                        dve.wait_ge(S("b_o_added"), KD)
                    nc.vector.tensor_tensor(x[:, 2 * j:2 * j + 2, :], src[:, :].rearrange("p (a t) -> p a t", a=2),
                                            x[:, 2 * j:2 * j + 2, :], ALU.add).then_inc(S("evacuated"), 1)
                    new_h_lo(n, 2 * j)
                    new_h_lo(n, 2 * j + 1)
                else:
                    if name == "w_in":
                        f = 14 + 2 * j if j < 4 else 2 * (j - 4)
                        dst = zz[:, f:f + 2, 1:T + 1]
                    else:
                        dst = qz[:, 2 * j:2 * j + 2, :]
                    nc.vector.tensor_tensor(dst, src[:, :].rearrange("p (a t) -> p a t", a=2),
                                            rB[:, :].unsqueeze(1).to_broadcast([P, 2, T]), ALU.mult
                                            ).then_inc(S("evacuated"), 1)
                    if name == "w_in":
                        during_w_in(j)

            def token_mix(j):
                dve.wait_ge(S("shifted"), j - 3)
                for f in (2 * (j - 4), 2 * (j - 4) + 1):
                    nc.vector.scalar_tensor_tensor(out=zs[:, f, :], in0=zs[:, f, :], scalar=pc("mu", f),
                                                   in1=zz[:, f, 1:T + 1], op0=ALU.mult, op1=ALU.add
                                                   ).then_inc(S("mixed"), 1)

            def during_w_in(j):
                if j >= 5:
                    token_mix(j - 1)
                if j == 5:
                    dve.wait_ge(S("s_mean"), 1)
                    link(nc.vector.tensor_scalar(g_mean[:, :], mix[1][:, 0:T], 1.0 / AW, None, ALU.mult))
                    nc.vector.tensor_tensor(zz[:, 18:22, 1:T + 1], zz[:, 18:22, 1:T + 1],
                                            g_mean[:, :].unsqueeze(1).to_broadcast([P, 4, T]), ALU.subtract
                                            ).then_inc(S("s_centred"), 1)

            def norm_factor(no):
                dve.wait_ge(S("root_done"), no)
                nc.vector.reciprocal(rB[:, :], root[:, :]).then_inc(S("norm_ready"), 1)
                dve.wait_ge(S("norm_ready"), no)

            def rwkv_gmlp():
                token_mix(10)
                dve.wait_ge(S("s_root"), 1)
                link(nc.vector.reciprocal(g_rstd[:, :], g_rstd[:, :]))
                nc.vector.tensor_tensor(zz[:, 18:22, 1:T + 1], zz[:, 18:22, 1:T + 1],
                                        g_rstd[:, :].unsqueeze(1).to_broadcast([P, 4, T]), ALU.mult
                                        ).then_inc(S("s_scaled"), 1)
                dve.wait_ge(S("spatial_loaded"), 32)
                nc.vector.tensor_tensor(wsT[:, :, :], wsT[:, :, :], cc("causal").unsqueeze(1).to_broadcast([P, 4, P]),
                                        ALU.mult).then_inc(S("ws_masked"), 1)
                nc.vector.tensor_scalar(kfb[:, :], pc("k_a", 0, 4), -1.0, 1.0, ALU.mult, ALU.add
                                        ).then_inc(S("kfb_made"), 1)
                for m in range(2):
                    dve.wait_ge(S("s_tok_t"), m + 1)
                    nc.vector.tensor_copy(s_tok[:, m, :], mix[2 + m][:, :]).then_inc(S("s_tok_made"), 1)
                for m in range(2):
                    dve.wait_ge(S("spatial_done"), m + 1)
                    link(nc.vector.tensor_tensor(gt[:, :, m * P:(m + 1) * P], v3(mix[2 + m]), bsp[:, :, :], ALU.add))
                dve.wait_ge(S("u_gelu"), 1)
                link(nc.vector.tensor_tensor(gt[:, :, :], gt[:, :, :], zz[:, 14:18, 1:T + 1], ALU.mult))
                link(nc.vector.tensor_copy(y_hi[:, 4:8, :], gt[:, :, :]))
                nc.vector.tensor_tensor(y_lo[:, 4:8, :], gt[:, :, :], y_hi[:, 4:8, :].bitcast(F32), ALU.subtract
                                        ).then_inc(S("u_used"), 1)
                dve.wait_ge(S("u_used"), 1)
                dve.wait_ge(S("kk_sums"), 1)
                dve.wait_ge(S("sd_made"), CT)
                for c in range(CT):
                    i = nc.vector.tensor_tensor_scan(cs[:, c, :], cc("restart"), sd[:, c, :], 0.0, ALU.mult, ALU.add)
                    if c < CT - 1:
                        i.then_inc(S("cs_parts"), 1)
                    else:
                        i.then_inc(S("cs_made"), 1)
                dve.wait_ge(S("cs_made"), 1)
                nc.vector.tensor_tensor(sd[:, :, :], cs[:, :, :], sd[:, :, :], ALU.subtract).then_inc(S("csm_made"), 1)
                dve.wait_ge(S("kk_root"), 1)
                link(nc.vector.tensor_scalar(root[:, :], root[:, :], 1e-12, None, ALU.max))
                nc.vector.reciprocal(rB[:, :], root[:, :]).then_inc(S("kk_inv"), 1)
                dve.wait_ge(S("kf_made"), CT)
                link(nc.vector.tensor_tensor(zs[:, 4:8, :], zs[:, 4:8, :], BT[:, :, :], ALU.mult))
                for c in range(CT):
                    nc.vector.scalar_tensor_tensor(out=bonus[:, c, :], in0=zs[:, c, :], scalar=pc("r_k", c),
                                                   in1=zs[:, 4 + c, :], op0=ALU.mult, op1=ALU.mult
                                                   ).then_inc(S("bonus_in"), 1)
                for c in range(2):
                    dve.wait_ge(S("kk_spread"), c + 1)
                    link(nc.vector.scalar_tensor_tensor(
                        out=kq[:, 2 * c:2 * c + 2, :], in0=mix[2 + c][:, :].rearrange("p (a t) -> p a t", a=2),
                        scalar=-1.0, in1=kq[:, 2 * c:2 * c + 2, :], op0=ALU.mult, op1=ALU.mult))
                dve.wait_ge(S("ep_made"), 1)
                nc.vector.tensor_tensor(tok4(AR, 1), zs[:, 0:4, :].rearrange("p c (m t) -> p c m t", m=2),
                                        ep[:, :, :].rearrange("p c (m t) -> p c m t", m=2), ALU.mult
                                        ).then_inc(S("R_made"), 1)
                link(nc.vector.tensor_copy(pend[:, :, :], ep[:, :, CH - 1:T:CH]))
                dve.wait_ge(S("pprev_made"), 1)
                nc.vector.tensor_tensor(tok4(AR, 0), kq[:, :, :].rearrange("p c (m t) -> p c m t", m=2),
                                        sd[:, :, :].rearrange("p c (m t) -> p c m t", m=2), ALU.mult
                                        ).then_inc(S("A_made"), 1)
                dve.wait_ge(S("en_made"), 1)
                nc.vector.tensor_tensor(KT[:, :, :], zs[:, 4:8, :], cs[:, :, :], ALU.mult).then_inc(S("K_made"), 1)
                link(nc.vector.tensor_tensor(ic[:, :, :], ic[:, :, :], cs[:, :, :], ALU.mult))
                nc.vector.scalar_tensor_tensor(out=BT[:, :, :], in0=kq[:, :, :], scalar=-1.0, in1=ic[:, :, :],
                                               op0=ALU.mult, op1=ALU.mult).then_inc(S("B_made"), 1)
                for c in range(2):
                    dve.wait_ge(S("bonus_sums"), c + 1)
                    link(nc.vector.tensor_tensor(bonus[:, 2 * c:2 * c + 2, :],
                                                 lin[c][:, :].rearrange("p (a t) -> p a t", a=2),
                                                 zs[:, 8 + 2 * c:10 + 2 * c, :], ALU.mult))
                nc.vector.memset(St[:, 0, 0, 0:1], 0.0).then_inc(S("bonus_done"), 1)

                for m in range(2):
                    for h in range(2):
                        if m:
                            dve.wait_ge(S("y_t"), m)
                        for u in range(4):
                            dve.wait_ge(S("pairs_t"), 8 * m + 4 * h + u + 1)
                            nc.vector.tensor_tensor(AM[h][:, u, :], banks[4 * h + u][:, :], cc("mask_pair"), ALU.mult
                                                    ).then_inc(S("AM_made"), 1)
                    for h in range(2):
                        dve.wait_ge(S("ab_t"), of_half(m + 1, h))
                        for mask, dst in (("mask16", Dm), ("mask32", M32), ("mask64", M64)):
                            for po in range(2):
                                nc.vector.tensor_tensor(
                                    dst[h][:, po:4:2, :], banks[4 * h + po][:, 0:2 * P].rearrange("p (a t) -> p a t", a=2),
                                    cc(mask).unsqueeze(1).to_broadcast([P, 2, P]), ALU.mult
                                ).then_inc(S("ab_masked"), 1)

                    def add_to_z(r, b):
                        for h in range(2):
                            dve.wait_ge(S("z_t"), of_half(5 * m + r + 1, h))
                            if r == 0:
                                dve.wait_ge(S("Z_first"), of_half(m + 1, h))
                            else:
                                dve.wait_ge(S("Z_made"), of_half(5 * m + r, h))
                            nc.vector.tensor_tensor(Zt[h][:, :, :], v3(banks[4 * h + b]), Zt[h][:, :, :], ALU.add
                                                    ).then_inc(S("Z_made"), 1)

                    def x_copy(r, b):
                        for h in range(2):
                            dve.wait_ge(S("x_t"), of_half(2 * m + r + 1, h))
                            nc.vector.tensor_copy(Xa[h][:, :, :], v3(banks[4 * h + b])).then_inc(S("x_made"), 1)

                    add_to_z(0, 0)
                    add_to_z(1, 2)
                    add_to_z(2, 3)
                    x_copy(0, 0)
                    add_to_z(3, 2)
                    x_copy(1, 3)
                    add_to_z(4, 1)
                    for h in range(2):
                        cs2 = slice(2 * h, 2 * h + 2)
                        dve.wait_ge(S("q_t"), of_half(m + 1, h))
                        nc.vector.tensor_tensor(AR[:, cs2, m, 1, :],
                                                banks[4 * h + 3][:, 0:2 * P].rearrange("p (c t) -> p c t", c=2),
                                                AR[:, cs2, m, 1, :], ALU.add).then_inc(S("Q_made"), 1)
                        for c2 in range(2):
                            n = 2 * m + c2
                            if n < NC - 1:
                                dve.wait_ge(S(f"e_t{h}"), n + 1)
                                ef = banks[4 * h + 1 + c2][:, :].rearrange("p (k c i) -> p k c i", k=4, c=2)
                                nc.vector.tensor_tensor(ETs[:, n, cs2, :], ef[:, 0, :, :],
                                                        cc("ident64").unsqueeze(1).to_broadcast([P, 2, CH]), ALU.add
                                                        ).then_inc(S(f"EF_made{h}"), 1)
                                nc.vector.tensor_copy(Fs[:, n, cs2, :], ef[:, 1, :, :]).then_inc(S(f"EF_made{h}"), 1)
                dve.wait_ge(S("EF_made0"), 6)
                dve.wait_ge(S("EF_made1"), 6)
                for n in range(3):
                    src = Fs[:, n, :, :]
                    if n:
                        dve.wait_ge(S("s_t"), n)
                        for po in range(2):
                            ins = nc.vector.tensor_tensor(Fs[64 * po:64 * po + 64, n, :, :],
                                                          mix[2 * (n % 2) + po][64 * po:64 * po + 64, 0:4 * CH].rearrange(
                                                              "p (c i) -> p c i", c=4),
                                                          Fs[64 * po:64 * po + 64, n, :, :], ALU.add)
                            link(ins)
                    nc.vector.tensor_tensor(St[:, n, :, :], src, pend[:, :, n:n + 1].to_broadcast([P, CT, CH]), ALU.mult
                                            ).then_inc(S("S_made"), 1)
                for n in range(3):
                    dve.wait_ge(S("ys_t"), n + 1)
                    for po in range(2):
                        r = slice(64 * po, 64 * po + 64)
                        link(nc.vector.tensor_tensor(Yc[r, :, (n + 1) * CH:(n + 2) * CH],
                                                     YSB[n][po][r, 0:4 * CH].rearrange("p (c i) -> p c i", c=4),
                                                     Yc[r, :, (n + 1) * CH:(n + 2) * CH], ALU.add))
                nc.vector.memset(St[:, 0, 0, 0:1], 0.0).then_inc(S("y_complete"), 1)
                for c in range(2):
                    dve.wait_ge(S("y_mean"), c + 1)
                    link(nc.vector.scalar_tensor_tensor(
                        out=Yc[:, 2 * c:2 * c + 2, :], in0=lin[c][:, :].rearrange("p (a t) -> p a t", a=2),
                        scalar=-1.0 / HD, in1=Yc[:, 2 * c:2 * c + 2, :], op0=ALU.mult, op1=ALU.add))
                nc.vector.memset(St[:, 0, 0, 0:1], 0.0).then_inc(S("y_centred"), 1)
                split_lo(3, 0, 0)
                dve.wait_ge(S("y_root"), 1)
                nc.vector.reciprocal(yst[:, 1, :], yst[:, 0, :]).then_inc(S("y_inv"), 1)
                for c in range(2):
                    dve.wait_ge(S("y_spread"), c + 1)
                    nc.vector.tensor_tensor(Yc[:, 2 * c:2 * c + 2, :],
                                            lin[2 + c][:, :].rearrange("p (a t) -> p a t", a=2),
                                            Yc[:, 2 * c:2 * c + 2, :], ALU.mult).then_inc(S("y_scaled"), 1)
                dve.wait_ge(S("y_normed"), CT)
                link(nc.vector.tensor_tensor(Yc[:, :, :], Yc[:, :, :], bonus[:, :, :], ALU.add))
                for c in range(2):
                    dve.wait_ge(S("gate_up"), c + 1)
                    nc.vector.tensor_tensor(Yc[:, 2 * c:2 * c + 2, :],
                                            mix[1 + c][:, :].rearrange("p (a t) -> p a t", a=2),
                                            Yc[:, 2 * c:2 * c + 2, :], ALU.mult).then_inc(S("y_gated"), 1)
                for c in range(2):
                    dve.wait_ge(S("y_hi_done"), c + 1)
                    nc.vector.tensor_tensor(y_lo[:, 2 * c:2 * c + 2, :], Yc[:, 2 * c:2 * c + 2, :],
                                            y_hi[:, 2 * c:2 * c + 2, :].bitcast(F32), ALU.subtract
                                            ).then_inc(S("y_lo_done"), 1)
                split_lo(3, 1, 1)

            def rope_angles(part):
                C1, C2 = 6.28125, 0.0019350051879882812
                C3 = 6.283185307179586 - C1 - C2
                ROUND = 12582912.0
                PI = 3.14159274101257
                if part == 0:
                    dve.wait_ge(S("pos_loaded"), 16)
                    link(nc.vector.tensor_copy(posf[:, :], posi[:, :]))
                    link(nc.vector.tensor_scalar(posf[:, :], posf[:, :], pc("inv_freq"), None, ALU.mult))
                    for which, name in enumerate(("q_norm", "k_norm")):
                        nc.vector.tensor_scalar(swap[:, which, :], cc("rope_swap"), pc(name), None, ALU.mult
                                                ).then_inc(S("swap_made"), 1)
                elif part < 3:
                    dst, quarter = ((sinT, 0.0), (cosT, 0.25))[part - 1]
                    turns = posi[:, :].bitcast(F32)
                    link(nc.vector.tensor_scalar(turns, posf[:, :], 1.0 / 6.283185307179586, quarter, ALU.mult, ALU.add))
                    link(nc.vector.tensor_scalar(turns, turns, ROUND, -ROUND, ALU.add, ALU.add))
                    for first, c in enumerate((C1, C2, C3)):
                        link(nc.vector.scalar_tensor_tensor(out=dst[:, :], in0=turns, scalar=-c,
                                                            in1=(dst if first else posf)[:, :],
                                                            op0=ALU.mult, op1=ALU.add))
                    if quarter:
                        link(nc.vector.tensor_scalar(dst[:, :], dst[:, :], PI / 2, None, ALU.add))
                    link(nc.vector.tensor_scalar(dst[:, :], dst[:, :], PI, -PI, ALU.min, ALU.max))
                else:
                    nc.vector.tensor_scalar(nsink[:, :], pc("sinks", 0, QH), -1.0, None, ALU.mult
                                            ).then_inc(S("angles"), 1)

            def rope(k):
                j = (0, 2, 3, 4, 5)[k]
                f = 2 * j
                dst = qr[:, (8 if j == 0 else f - 4):(8 if j == 0 else f - 4) + 2, :]
                dve.wait_ge(S("qkv_biased"), f + 2)
                dve.wait_ge(S("rope_tables"), 2)
                link(nc.vector.scalar_tensor_tensor(out=dst, in0=qz[:, f:f + 2, :], scalar=pc("k_norm" if j == 0 else "q_norm"),
                                                    in1=cosT[:, :].unsqueeze(1).to_broadcast([P, 2, T]),
                                                    op0=ALU.mult, op1=ALU.mult))
                dve.wait_ge(S("rot_t"), k + 1)
                nc.vector.tensor_tensor(trot[:, k % 2, :, :], mix[1 + k % 2][:, :].rearrange("p (a t) -> p a t", a=2),
                                        sinT[:, :].unsqueeze(1).to_broadcast([P, 2, T]), ALU.mult
                                        ).then_inc(S("rot_used"), 1)
                dve.wait_ge(S("rot_used"), k + 1)
                nc.vector.tensor_tensor(dst, dst, trot[:, k % 2, :, :], ALU.add).then_inc(S("roped"), 1)

            def during_qkv(j):
                if j == 5:
                    dve.wait_ge(S("v_t"), 1)
                    nc.vector.tensor_copy(v_tok[:, :, :], mix[3][:, :].rearrange("p (m f) -> p m f", m=2)
                                          ).then_inc(S("v_tok_made"), 1)
                    rope(0)
                    dve.wait_ge(S("rk_root"), 1)
                    nc.vector.reciprocal(rk[0:64, 1, :], rk[0:64, 0, :]).then_inc(S("rk_made"), 1)

            def attention():
                dve.wait_ge(S("rk_spread"), 1)
                nc.vector.tensor_tensor(qr[:, 8:10, :], mix[3][:, :].rearrange("p (a t) -> p a t", a=2), qr[:, 8:10, :],
                                        ALU.mult).then_inc(S("k_scaled"), 1)
                for k in range(2, 5):
                    rope(k)
                dve.wait_ge(S("rq_root"), 1)
                link(nc.vector.reciprocal(rq[:, :, :], rq[:, :, :]))
                nc.vector.tensor_scalar(rq[:, :, :], rq[:, :, :], HD ** -0.5, None, ALU.mult).then_inc(S("rq_made"), 1)
                dve.wait_ge(S("rq_made"), 1)
                split_lo(9, 0, 0)

                def maxima(g):
                    n, c, s4 = g // 4, 2 * (g % 4), g % NSC
                    W = P * (n + 1)
                    mask = cc("window")[:, 2 * P - W:2 * P].unsqueeze(1).to_broadcast([P, 2, W])
                    if g >= NSC:
                        dve.wait_ge(S("p_t"), 2 * (g - NSC) + 2)
                    for p in range(2):
                        dve.wait_ge(S("scores_t"), 2 * g + p + 1)
                        nc.vector.tensor_tensor(sc[:, s4, :, p, 0:W],
                                                mix[2 * (g % 2) + p][:, :].rearrange("p (i t) -> p i t", i=2)[:, :, 0:W],
                                                mask, ALU.add).then_inc(S("masked"), 1)
                    dve.wait_ge(S("masked"), 2 * g + 2)
                    link(nc.vector.tensor_reduce(sm[:, s4, 0, :].rearrange("p (i h) -> p i h", i=2), sc[:, s4, :, :, 0:W],
                                                 AX, ALU.max, negate=True))
                    link(nc.vector.tensor_tensor(sm[:, s4, 1, :], sm[:, s4, 0, :], rq[:, n, 2 * c:2 * c + 4], ALU.mult))
                    link(nc.vector.tensor_tensor(sm[:, s4, 2, :], sm[:, s4, 1, :], nsink[:, 2 * c:2 * c + 4], ALU.min))
                    nc.vector.tensor_tensor(sm[:, s4, 3, :], sm[:, s4, 2, :], pc("sinks", 2 * c, 4), ALU.add
                                            ).then_inc(S("max_made"), 1)

                def normalise(g):
                    n, s4 = g // 4, g % NSC
                    W = P * (n + 1)
                    dve.wait_ge(S("exp_made"), 5 * g + 5)
                    link(nc.vector.tensor_tensor(sm[:, s4, 6, :], sm[:, s4, 4, :], sm[:, s4, 5, :], ALU.add))
                    link(nc.vector.reciprocal(sm[:, s4, 7, :], sm[:, s4, 6, :]))
                    for i in range(2):
                        nc.vector.tensor_tensor(sc[:, s4, i, :, 0:W], sc[:, s4, i, :, 0:W],
                                                sm[:, s4, 7, 2 * i:2 * i + 2].unsqueeze(2).to_broadcast([P, 2, W]),
                                                ALU.mult).then_inc(S("p_made"), 1)

                def heads_lo(g):
                    n, c = g // 4, 2 * (g % 4)
                    dve.wait_ge(S("o_hi_done"), g + 1)
                    nc.vector.tensor_tensor(y_lo[:, c:c + 2, n * P:(n + 1) * P],
                                            lin[2 + g % 2][:, 0:T].rearrange("p (i q) -> p i q", i=2),
                                            y_hi[:, c:c + 2, n * P:(n + 1) * P].bitcast(F32), ALU.subtract
                                            ).then_inc(S("o_lo_done"), 1)

                maxima(0)
                for g in range(ROUNDS):
                    if g + 1 < ROUNDS:
                        maxima(g + 1)
                    if g == 0:
                        split_lo(9, 1, 1)
                    normalise(g)
                    if g >= 1:
                        heads_lo(g - 1)
                heads_lo(ROUNDS - 1)

            for i, e in enumerate((RMS_EPS, LN_EPS, GN_EPS, 0.0)):
                nc.vector.memset(eps[:, i:i + 1], e).then_inc(S("setup_parts"), 1)
            nc.vector.memset(ones[:, :], 1.0).then_inc(S("setup"), 1)
            nc.vector.memset(root[:, :], 1.0).then_inc(S("evacuated"), 4)
            dve.wait_ge(S("params_loaded"), 16)
            dve.wait_ge(S("x_first"), 16)
            for k in range(KD):
                if k == 2:
                    dve.wait_ge(S("x_loaded"), 16)
                new_h_lo(-1, k)
            for n, (name, steps, tiles, inst) in enumerate(LINEARS):
                if name not in ("w_out", "w_o"):
                    for j in range(2):
                        if n:
                            pn = LINEARS[n - 1][1] - 2 + j
                            late(n - 1, pn, pn)
                        split_lo(n, j, j)
                if n - 1 in NORM_NO:
                    norm_factor(NORM_NO[n - 1])
                if name == "gu":
                    def step(j, q, i):
                        split_lo(n, j, q, i)
                        scale_gu(n, j - 2, q - 2)
                    rounds(dve, 2, steps, step)
                else:
                    for j in range(2, steps):
                        split_lo(n, j, j)
                        late(n, j - 2, j - 2)
                        if name == "qkv":
                            during_qkv(j)
                        if n == 7 and 2 < j < 7:
                            rope_angles(j - 3)
                if name in ("w_in", "qkv"):
                    late(n, steps - 2, steps - 2)
                    if name == "qkv":
                        rope(1)
                    late(n, steps - 1, steps - 1)
                    if name == "w_in":
                        rwkv_gmlp()
                    else:
                        attention()
            for j in range(2):
                late(11, LINEARS[11][1] - 2 + j, LINEARS[11][1] - 2 + j)

        @block.gpsimd
        def _(pool):
            nc.gpsimd.memset(zz[:, :, 0:1], 0.0).then_inc(S("zz_zeroed"), 1)
            nc.gpsimd.memset(sil[:, :, :], 0.0).then_inc(S("act_made"), 2)

            def add_square(n, k):
                m = HBASE[n] + k
                pool.wait_ge(S("sq_done"), m + 1)
                if k == 0:
                    if NORM_NO[n] > 1:
                        pool.wait_ge(S("stats_done"), NORM_NO[n] - 1)
                    nc.gpsimd.tensor_copy(ssq[:, 0, :], sq[:, 0, :]).then_inc(S("sq_added"), 1)
                else:
                    pool.wait_ge(S("sq_added"), m)
                    nc.gpsimd.tensor_tensor(ssq[:, 0, :], ssq[:, 0, :], sq[:, k % 2, :], ALU.add
                                            ).then_inc(S("sq_added"), 1)

            def hidden(n, j, q):
                m = KF * LINEARS[n][3] + j
                pool.wait_ge(S("silu_done"), m + 1)
                nc.gpsimd.tensor_tensor(act_f[:, q % 2, :], sil[:, q % 2, :], pre[:, q % 2, 1, :], ALU.mult
                                        ).then_inc(S("act_made"), 1)
                pool.wait_ge(S("act_made"), m + 3)
                if LINEARS[n][3] and isinstance(q, int) and q < 2:
                    pool.wait_ge(S("sub_done"), 2 * FIRST[n])
                nc.gpsimd.tensor_copy(a_hi[:, bass.ds(j, 1), :].rearrange("p a t -> p (a t)"), act_f[:, q % 2, :]
                                      ).then_inc(S("a_hi_done"), 1)
                pool.wait_ge(S("a_hi_done"), m + 1)
                nc.gpsimd.tensor_tensor(a_lo[:, bass.ds(j, 1), :].rearrange("p a t -> p (a t)"), act_f[:, q % 2, :],
                                        a_hi[:, bass.ds(j, 1), :].rearrange("p a t -> p (a t)").bitcast(F32),
                                        ALU.subtract).then_inc(S("a_ready"), 1)

            def rwkv_gmlp():
                for m in range(2):
                    for h in range(2):
                        pool.wait_ge(S("AM_made"), 8 * m + 4 * h + 4)
                        nc.gpsimd.tensor_tensor(DmT[h][:, :, :], AM[h][:, :, 0:P],
                                                cc("mask16T").unsqueeze(1).to_broadcast([P, 4, P]), ALU.mult
                                                ).then_inc(S("DmT_made"), 1)
                        pool.wait_ge(S("DmT_made"), of_half(m + 1, h))
                        nc.gpsimd.tensor_tensor(Zt[h][:, :, :], DmT[h][:, :, :],
                                                ident.unsqueeze(1).to_broadcast([P, 4, P]), ALU.add
                                                ).then_inc(S("Z_first"), 1)

            for k in range(KD):
                add_square(-1, k)
            for n, (name, steps, tiles, inst) in enumerate(LINEARS):
                if name == "gu":
                    rounds(pool, 0, steps, lambda j, q, i: hidden(n, j, q))
                elif n in GAIN_AFTER:
                    for k in range(KD):
                        add_square(n, k)
                elif name == "w_in":
                    pool.wait_ge(S("zz_zeroed"), 1)
                    for j in range(4, 11):
                        pool.wait_ge(S("evacuated"), steps_to(n) + j + 1)
                        f = 2 * (j - 4)
                        nc.gpsimd.tensor_tensor(zs[:, f:f + 2, :], zz[:, f:f + 2, 0:T], zz[:, f:f + 2, 1:T + 1],
                                                ALU.subtract).then_inc(S("shifted"), 1)
                    rwkv_gmlp()

        @block.tensor
        def _(pe):
            mm = nc.tensor.matmul

            def products(out, sub, w0, tiles, in_hi, in_lo, k0, last_k, first, done):
                for k in range(tiles):
                    wa = w_hi[:, sub, (w0 + k) * P:(w0 + k + 1) * P]
                    wb = w_lo[:, sub, (w0 + k) * P:(w0 + k + 1) * P]
                    a, b = in_hi[:, k0 + k, :], in_lo[:, k0 + k, :]
                    if done is not None:
                        done(k0 + k)
                    mm(out, wa, a, start=first and k == 0, stop=False)
                    mm(out, wa, b, start=False, stop=False)
                    ins = mm(out, wb, a, start=False, stop=last_k and k == tiles - 1)
                ins.then_inc(S("sub_done"), 1)

            def step(n, j, q, i=0):
                name, _, tiles, inst = LINEARS[n]
                g0 = FIRST[n]
                b = lin[(g0 + q) % 4]
                pe.wait_ge(S("evacuated"), g0 + j + 1)
                for s in range(2):
                    pe.wait_ge(S("lo_done"), 2 * (g0 + j) + s + 1)
                    sub = (2 * (g0 + q) + s) % 4
                    if name == "down":
                        ready = (lambda k: pe.wait_ge(S("a_ready"), KF * inst + k + 1)) if q == 0 else None
                        products(b[:, 0:T], sub, 0, tiles, a_hi, a_lo, s * tiles, s == 1, s == 0, ready)
                    elif name in ("w_out", "w_o"):
                        products(b[:, s * T:(s + 1) * T], sub, 0, tiles, y_hi, y_lo, 0, True, True, None)
                    else:
                        ready = (lambda k: pe.wait_ge(S("h_ready"), HBASE[n - 1] + k + 1)) if q == 0 and s == 0 else None
                        products(b[:, s * T:(s + 1) * T], sub, 0, tiles, h_hi, h_lo, 0, True, True, ready)

            def stats(no):
                pe.wait_ge(S("sq_added"), 8 * no)
                pe.wait_ge(S("setup"), 1)
                mm(mix[0][:, 0:T], ones[:, :], ssq[:, 0, :], start=True, stop=True).then_inc(S("stats_done"), 1)

            def during_w_in(j):
                if j == 5:
                    pe.wait_ge(S("s_gelu"), 1)
                    for f in range(4):
                        ins = mm(mix[1][:, 0:T], ones[:, :], zz[:, 18 + f, 1:T + 1], start=f == 0, stop=f == 3)
                    ins.then_inc(S("s_mean"), 1)
                if j == 10:
                    pe.wait_ge(S("s_squared"), 1)
                    for f in range(4):
                        ins = mm(mix[1][:, T:2 * T], ones[:, :], gt[:, f, :], start=f == 0, stop=f == 3)
                    ins.then_inc(S("s_var"), 1)

            def rwkv_gmlp():
                pe.wait_ge(S("consts_loaded"), 16)
                pe.wait_ge(S("evacuated"), steps_to(3))
                pe.wait_ge(S("lora_loaded"), 32)
                pe.wait_ge(S("tanh_done"), 1)
                for c in range(CT):
                    ins = mm(lin[c // 2][:, (c % 2) * T:(c % 2 + 1) * T], lora[0:64, c * P:(c + 1) * P], th[0:64, :],
                             start=True, stop=True)
                ins.then_inc(S("decay_up"), 1)
                for c in range(CT):
                    ins = mm(lin[2 + c // 2][:, (c % 2) * T:(c % 2 + 1) * T], lora[64:128, c * P:(c + 1) * P],
                             zs[64:128, 12, :], start=True, stop=True)
                ins.then_inc(S("iclr_up"), 1)
                pe.wait_ge(S("kq_squared"), 1)
                for c in range(CT):
                    ins = mm(mix[0][32 * c:32 * c + 32, 0:T], cc("pick"), cs[:, c, :], start=True, stop=True)
                ins.then_inc(S("kk_sums"), 1)
                pe.wait_ge(S("s_normed"), 4)
                for m in range(2):
                    for f in range(4):
                        ins = nc.tensor.transpose(mix[2 + m][:, f * P:(f + 1) * P],
                                                  zz[:, 18 + f, 1 + m * P:1 + (m + 1) * P], ident)
                    ins.then_inc(S("s_tok_t"), 1)
                pe.wait_ge(S("ws_masked"), 1)
                for m in range(2):
                    pe.wait_ge(S("s_tok_made"), m + 1)
                    for f in range(4):
                        ins = mm(mix[2 + m][:, f * P:(f + 1) * P], s_tok[:, m, f * P:(f + 1) * P], wsT[:, f, :],
                                 start=True, stop=True)
                    ins.then_inc(S("spatial_done"), 1)
                pe.wait_ge(S("kk_inv"), 1)
                pe.wait_ge(S("u_used"), 1)
                for c in range(CT):
                    ins = mm(mix[2 + c // 2][:, (c % 2) * T:(c % 2 + 1) * T], cc("spread")[:, c * P:(c + 1) * P],
                             rB[:, :], start=True, stop=True)
                    if c % 2:
                        ins.then_inc(S("kk_spread"), 1)
                pe.wait_ge(S("bonus_in"), CT)
                pe.wait_ge(S("sd_made"), CT)
                for c in range(2):
                    mm(lin[c][:, :], cc("head_ones"), bonus[:, 2 * c:2 * c + 2, :], start=True, stop=True
                       ).then_inc(S("bonus_sums"), 1)
                for i in range(8):
                    m, kind = i % 2, i // 2
                    if kind == 0 and m == 0:
                        pe.wait_ge(S("ic_made"), CT)
                    elif m == 0:
                        pe.wait_ge(S(("", "A_made", "K_made", "B_made")[kind]), 1)
                    if i >= 4:
                        pe.wait_ge(S("tok_made"), i - 3)
                    for c in range(CT):
                        tk = slice(m * P, (m + 1) * P)
                        src = (zs[:, 8 + c, tk], AR[:, c, m, 0, :], KT[:, c, tk], BT[:, c, tk])[kind]
                        ins = nc.tensor.transpose((lin[2], lin[3], mix[0], mix[1])[i % 4][:, c * P:(c + 1) * P], src, ident)
                    ins.then_inc(S("tok_t"), 1)
                pe.wait_ge(S("R_made"), 1)
                pe.wait_ge(S("bonus_done"), 1)
                pe.wait_ge(S("tok_made"), 8)

                def heads_of(h):
                    return [(u, 2 * h + u // 2, 64 * (u % 2), 4 * h + u) for u in range(4)]

                def four(bank_, a, b_, sem):
                    for u in range(4):
                        ins = mm(bank_[:, u * P:(u + 1) * P], a[:, u, :], b_[:, u, :], start=True, stop=True)
                    ins.then_inc(S(sem), 1)

                for m in range(2):
                    tk = slice(m * P, (m + 1) * P)
                    for h in range(2):
                        if m:
                            pe.wait_ge(S(f"EF_made{h}"), 4)
                            pe.wait_ge(S("Q_made"), of_half(1, h))
                            pe.wait_ge(S("y_done"), of_half(1, h))
                        for u, c, po, _ in heads_of(h):
                            r = slice(po, po + 64)
                            mm(banks[4 * h + u][:, 0:2 * P], BT[r, c, tk], AR[r, c, m, :, :], start=True, stop=True)
                            mm(banks[4 * h + u][:, 2 * P:4 * P], KT[r, c, tk], AR[r, c, m, :, :], start=True, stop=True
                               ).then_inc(S("pairs_t"), 1)
                    for h in range(2):
                        pe.wait_ge(S("AM_made"), 8 * m + 4 * h + 2)
                        for u, c, po, _ in heads_of(h):
                            r = slice(po, po + 64)
                            ins = mm(banks[4 * h + u % 2][:, (u // 2) * P:(u // 2 + 1) * P], AR[r, c, m, 0, :], BT[r, c, tk],
                                     start=True, stop=True)
                        ins.then_inc(S("ab_t"), 1)
                    for h in range(2):
                        pe.wait_ge(S("AM_made"), 8 * m + 4 * h + 4)
                        for u, c, po, hd in heads_of(h):
                            ins = mm(banks[4 * h + 2][:, u * CH:(u + 1) * CH], AM[h][:, u, 2 * P:3 * P],
                                     TM[m][:, 0, hd * HD:(hd + 1) * HD], start=True, stop=True)
                        ins.then_inc(S("akv_t"), 1)
                    for h in range(2):
                        b = banks[4 * h:4 * h + 4]
                        pe.wait_ge(S("ab_masked"), 12 * m + 6 * h + 6)
                        pe.wait_ge(S("DmT_made"), of_half(m + 1, h))
                        four(b[0], DmT[h], Dm[h], f"n_sq{h}")
                        four(b[1], Dm[h], DmT[h], f"n_sq{h}")
                    for h in range(2):
                        b = banks[4 * h:4 * h + 4]
                        pe.wait_ge(S(f"sq_made{h}"), 5 * m + 2)
                        pe.wait_ge(S("akv_made"), of_half(m + 1, h))
                        four(b[2], D2T[h], D2[h], f"n_sq{h}")
                        four(b[3], D2[h], D2T[h], f"n_sq{h}")
                        pe.wait_ge(S("Z_first"), of_half(m + 1, h))
                        four(b[0], D2[h], Zt[h], "z_t")
                    for h in range(2):
                        b = banks[4 * h:4 * h + 4]
                        pe.wait_ge(S(f"sq_made{h}"), 5 * m + 4)
                        four(b[1], D4T[h], D4[h], f"n_sq{h}")
                        pe.wait_ge(S("Z_made"), of_half(5 * m + 1, h))
                        four(b[2], D4[h], Zt[h], "z_t")
                    for h in range(2):
                        b = banks[4 * h:4 * h + 4]
                        pe.wait_ge(S(f"sq_made{h}"), 5 * m + 5)
                        pe.wait_ge(S("Z_made"), of_half(5 * m + 2, h))
                        four(b[3], D2[h], Zt[h], "z_t")
                    for r_, (mask, bt, bx, bz) in enumerate(((M32, 1, 0, 2), (M64, 0, 3, 1))):
                        for h in range(2):
                            b = banks[4 * h:4 * h + 4]
                            pe.wait_ge(S("Z_made"), of_half(5 * m + 3 + r_, h))
                            four(b[bx], mask[h], Zt[h], "x_t")
                            for u in range(4):
                                ins = nc.tensor.transpose(b[bt][:, u * P:(u + 1) * P], Zt[h][:, u, :], ident)
                            ins.then_inc(S("t_t"), 1)
                        for h in range(2):
                            b = banks[4 * h:4 * h + 4]
                            pe.wait_ge(S("t_made"), of_half(2 * m + r_ + 1, h))
                            pe.wait_ge(S("x_made"), of_half(2 * m + r_ + 1, h))
                            four(b[bz], Tt[h], Xa[h], "z_t")
                    for h in range(2):
                        b = banks[4 * h:4 * h + 4]
                        pe.wait_ge(S("Z_made"), of_half(5 * m + 5, h))
                        for u, c, po, hd in heads_of(h):
                            ins = mm(b[2][:, u * P:(u + 1) * P], Zt[h][:, u, :], TM[m][:, 3:5, hd * HD:(hd + 1) * HD],
                                     start=True, stop=True)
                        ins.then_inc(S("hg_t"), 1)
                    for h in range(2):
                        b = banks[4 * h:4 * h + 4]
                        pe.wait_ge(S("hg_made"), of_half(m + 1, h))
                        for u, c, po, hd in heads_of(h):
                            ins = mm(b[3][po:po + 64, (u // 2) * P:(u // 2 + 1) * P], HG[h][:, u, 0:CH],
                                     AM[h][:, u, P:2 * P], start=True, stop=True)
                        ins.then_inc(S("q_t"), 1)
                        for u, c, po, hd in heads_of(h):
                            o = b[0][po:po + 64, (u // 2) * P:(u // 2 + 1) * P]
                            mm(o, HG[h][:, u, CH:2 * CH], AM[h][:, u, P:2 * P], start=True, stop=False)
                            ins = mm(o, TM[m][:, 0, hd * HD:(hd + 1) * HD], AM[h][:, u, 3 * P:4 * P], start=False, stop=True)
                        ins.then_inc(S("y_t"), 1)
                        for c2 in range(2):
                            if 2 * m + c2 == NC - 1:
                                continue
                            r = slice(64 * c2, 64 * c2 + 64)
                            for u, c, po, hd in heads_of(h):
                                col = (u // 2) * CH
                                hc = slice(hd * HD, (hd + 1) * HD)
                                mm(b[1 + c2][po:po + 64, col:col + CH], HG[h][r, u, 0:CH], TM[m][r, 1, hc],
                                   start=True, stop=True)
                                o = b[1 + c2][po:po + 64, P + col:P + col + CH]
                                mm(o, TM[m][r, 1, hc], HG[h][r, u, CH:2 * CH], start=True, stop=False)
                                ins = mm(o, TM[m][r, 2, hc], TM[m][r, 0, hc], start=False, stop=True)
                            ins.then_inc(S(f"e_t{h}"), 1)
                for h in range(2):
                    pe.wait_ge(S(f"EF_made{h}"), 6)
                    pe.wait_ge(S("Q_made"), of_half(2, h))
                    pe.wait_ge(S("y_done"), of_half(2, h))
                for n in range(1, 3):
                    pe.wait_ge(S("S_made"), n)
                    for po in range(2):
                        r = slice(64 * po, 64 * po + 64)
                        for c in range(CT):
                            ins = mm(mix[2 * (n % 2) + po][r, c * CH:(c + 1) * CH], ETs[r, n, c, :], St[r, n - 1, c, :],
                                     start=True, stop=True)
                    ins.then_inc(S("s_t"), 1)
                for n in range(3):
                    pe.wait_ge(S("S_made"), n + 1)
                    for po in range(2):
                        r = slice(64 * po, 64 * po + 64)
                        t0 = (n + 1) * CH
                        for c in range(CT):
                            ins = mm(YSB[n][po][r, c * CH:(c + 1) * CH], St[r, n, c, :],
                                     AR[r, c, t0 // P, 1, t0 % P:t0 % P + CH], start=True, stop=True)
                    ins.then_inc(S("ys_t"), 1)
                pe.wait_ge(S("y_complete"), 1)
                for c in range(2):
                    mm(lin[c][:, :], cc("head_ones"), Yc[:, 2 * c:2 * c + 2, :], start=True, stop=True
                       ).then_inc(S("y_mean"), 1)
                for c in range(2):
                    for a in range(2):
                        ins = mm(mix[1 + c][:, a * T:(a + 1) * T], wgate[:, (2 * c + a) * P:(2 * c + a + 1) * P], sgx[:, :],
                                 start=True, stop=True)
                    ins.then_inc(S("gate_up"), 1)
                pe.wait_ge(S("y_squared"), 1)
                for c in range(CT):
                    ins = mm(mix[0][32 * c:32 * c + 32, 0:T], cc("pick"), ysq[:, c, :], start=True, stop=True)
                ins.then_inc(S("y_var"), 1)
                pe.wait_ge(S("y_inv"), 1)
                for c in range(2):
                    for a in range(2):
                        ins = mm(lin[2 + c][:, a * T:(a + 1) * T], cc("spread")[:, (2 * c + a) * P:(2 * c + a + 1) * P],
                                 yst[:, 1, :], start=True, stop=True)
                    ins.then_inc(S("y_spread"), 1)
                pe.wait_ge(S("y_lo_done"), 2)
                pe.wait_ge(S("u_used"), 1)

            def rot(k):
                f = 2 * (0, 2, 3, 4, 5)[k]
                pe.wait_ge(S("swap_made"), 2)
                pe.wait_ge(S("qkv_biased"), f + 2)
                if k >= 2:
                    pe.wait_ge(S("rot_used"), k - 1)
                mm(mix[1 + k % 2][:, :], swap[:, 1 if k == 0 else 0, :], qz[:, f:f + 2, :], start=True, stop=True
                   ).then_inc(S("rot_t"), 1)

            def q_sums(c):
                for m in range(2):
                    ins = mm(mix[0][:, m * QH + 2 * c:m * QH + 2 * c + 2], qsq[:, 2 + c, m * P:(m + 1) * P],
                             cc("pick")[:, 0:2], start=True, stop=True)
                return ins

            def during_qkv(j):
                if j == 3:
                    pe.wait_ge(S("qkv_biased"), 4)
                    for m in range(2):
                        for c in range(2):
                            ins = nc.tensor.transpose(mix[3][:, (2 * m + c) * P:(2 * m + c + 1) * P],
                                                      qz[:, 2 + c, m * P:(m + 1) * P], ident)
                    ins.then_inc(S("v_t"), 1)
                    rot(0)
                    for c in range(2):
                        ins = mm(mix[0][32 * c:32 * c + 32, T:2 * T], cc("pick"), qsq[:, c, :], start=True, stop=True)
                    ins.then_inc(S("k_sums"), 1)
                if j == 5:
                    rot(1)

            def attention():
                pe.wait_ge(S("rk_made"), 1)
                pe.wait_ge(S("v_tok_made"), 1)
                for c in range(2):
                    ins = mm(mix[3][:, c * T:(c + 1) * T], cc("spread")[0:64, c * P:(c + 1) * P], rk[0:64, 1, :],
                             start=True, stop=True)
                ins.then_inc(S("rk_spread"), 1)
                for k in range(1, 5):
                    if k > 1:
                        rot(k)
                    pe.wait_ge(S("q_squared"), k + 1)
                    q_sums(2 * k - 2)
                    ins = q_sums(2 * k - 1)
                ins.then_inc(S("q_sums"), 1)
                pe.wait_ge(S("k_scaled"), 1)
                pe.wait_ge(S("roped"), 5)
                pe.wait_ge(S("rot_used"), 5)
                pe.wait_ge(S("rq_root"), 1)
                pe.wait_ge(S("evacuated"), steps_to(9))

                def scores(g):
                    n, c = g // 4, 2 * (g % 4)
                    if g >= 2:
                        pe.wait_ge(S("masked"), 2 * g - 2)
                    for p in range(2):
                        r = slice(64 * p, 64 * p + 64)
                        for i in range(2):
                            ins = mm(mix[2 * (g % 2) + p][:, i * T:i * T + P * (n + 1)], qr[r, c + i, n * P:(n + 1) * P],
                                     qr[r, 8 + c // 4, 0:P * (n + 1)], start=True, stop=True)
                        ins.then_inc(S("scores_t"), 1)

                def transposes(g):
                    n, s4 = g // 4, g % NSC
                    for i in range(2):
                        pe.wait_ge(S("p_made"), 2 * g + i + 1)
                        for p in range(2):
                            for k in range(n + 1):
                                ins = nc.tensor.transpose(lin[i][:, (2 * p + k) * P:(2 * p + k + 1) * P],
                                                          sc[:, s4, i, p, k * P:(k + 1) * P], ident)
                        ins.then_inc(S("p_t"), 1)

                def values(g):
                    n, c = g // 4, 2 * (g % 4)
                    if g >= 2:
                        pe.wait_ge(S("o_lo_done"), g - 1)
                    for i in range(2):
                        pe.wait_ge(S("pT_made"), 2 * g + i + 1)
                        for p in range(2):
                            kv = 2 * (c // 4) + p
                            for k in range(n + 1):
                                ins = mm(lin[2 + g % 2][64 * p:64 * p + 64, i * P:(i + 1) * P],
                                         v_tok[:, k, kv * HD:(kv + 1) * HD],
                                         pT[:, i, p, k, :], start=k == 0, stop=k == n)
                    ins.then_inc(S("pv"), 1)

                scores(0)
                scores(1)
                for g in range(ROUNDS):
                    if g + 2 < ROUNDS:
                        scores(g + 2)
                    transposes(g)
                    values(g)
                pe.wait_ge(S("o_lo_done"), ROUNDS)

            pe.wait_ge(S("setup"), 1)
            for n, (name, steps, tiles, inst) in enumerate(LINEARS):
                step(n, 0, 0)
                if n - 1 in NORM_NO:
                    stats(NORM_NO[n - 1])
                step(n, 1, 1)
                if name == "w_in":
                    for j in range(2, steps):
                        step(n, j, j)
                        during_w_in(j)
                    rwkv_gmlp()
                elif name == "down":
                    rounds(pe, 2, steps, lambda j, q, i: step(n, j, q, i))
                elif name == "qkv":
                    for j in range(2, steps):
                        step(n, j, j)
                        during_qkv(j)
                    attention()
                else:
                    rounds(pe, 2, steps, lambda j, q, i: step(n, j, q, i))


def v3(bank):
    return bank[:, :].rearrange("p (u t) -> p u t", u=4)


def of_half(v, h):
    return 2 * v - 1 + h


def tok4(AR, which):
    return AR[:, :, :, which, :]


def constants():
    import numpy as np
    c = np.zeros((P, NCON), np.float32)

    def put(name, a):
        c[:, CCOLS[name][0]:CCOLS[name][0] + CCOLS[name][1]] = a

    i, j = np.arange(P)[:, None], np.arange(P)[None, :]
    put("ident", i == j)
    put("head_ones", i // HD == j // HD)
    swap = np.zeros((P, P))
    for f in range(P):
        if f % HD < HD // 2:
            swap[f + HD // 2, f] = -1
        else:
            swap[f - HD // 2, f] = 1
    put("rope_swap", swap)
    same = i // CH == j // CH
    put("mask_pair", np.concatenate([same & (i < j), same & (i <= j)] * 2, 1))
    put("mask16", (i // 16 == j // 16) & (i > j))
    put("mask16T", (i // 16 == j // 16) & (i < j))
    put("mask32", (i // 32 == j // 32) & (i // 16 > j // 16))
    put("mask64", (i // 64 == j // 64) & (i // 32 > j // 32))
    put("causal", i <= j)
    put("window", np.where(np.concatenate([j > i, j <= i], 1), 0.0, -1e30))
    put("restart", (np.arange(T)[None, :] % CH != 0) * np.ones((P, 1)))
    put("ident64", i % CH == np.arange(CH)[None, :])
    pick = np.zeros((P, 32))
    pick[:HD, 0] = 1
    pick[HD:, 1] = 1
    put("pick", pick)
    spread = np.zeros((P, CT, P))
    for t in range(CT):
        spread[32 * t, t, :HD] = 1
        spread[32 * t + 1, t, HD:] = 1
    put("spread", spread.reshape(P, CT * P))
    return c


def kernel(x, positions, ffn1_norm, ffn1_w_gate, ffn1_w_up, ffn1_w_down, mix_norm,
           ffn2_norm, ffn2_w_gate, ffn2_w_up, ffn2_w_down,
           ab_w_in, ab_mu_shift, rwkv_w0, rwkv_w_decay_up, rwkv_a0, rwkv_w_aaa_up, rwkv_w_gate_up,
           rwkv_k_k, rwkv_k_a, rwkv_r_k, rwkv_gn_gain, rwkv_gn_bias,
           sg_ln_gain, sg_ln_bias, sg_w_spatial, sg_b_spatial, ab_w_out,
           attn_w_qkv, attn_b_qkv, attn_q_norm, attn_k_norm, attn_sinks, attn_w_o, attn_b_o):
    import numpy as np
    import concourse.bacc as bacc
    from concourse.bass_utils import run_bass_kernel_spmd

    A = np.asarray

    def tiles(w, n_tile):
        w = A(w)
        K, N = w.shape
        return w.reshape(K // P, P, N // n_tile, n_tile).transpose(2, 1, 0, 3)

    def pairs(w):
        t = tiles(w, P)
        n = t.shape[0]
        return t.reshape(n // 2, 2, P, KD, P).transpose(0, 2, 1, 3, 4).reshape(n // 2, P, 2 * KD * P)

    def feature(v):
        return A(v).reshape(-1, P).T

    gu = []
    for wg, wu in ((ffn1_w_gate[0], ffn1_w_up[0]), (ffn2_w_gate[0], ffn2_w_up[0]),
                   (ffn1_w_gate[1], ffn1_w_up[1]), (ffn2_w_gate[1], ffn2_w_up[1])):
        g, u = tiles(wg, P), tiles(wu, P)
        gu.append(np.stack([g, u], 2).reshape(KF, P, 2 * KD * P))
    down = [tiles(w, P).reshape(KD, P, KF * P)
            for w in (ffn1_w_down[0], ffn2_w_down[0], ffn1_w_down[1], ffn2_w_down[1])]
    w_in = A(ab_w_in[0])
    w_in = np.concatenate([w_in[:, ZA * P:], w_in[:, :ZA * P]], 1)
    order = [h for half in range(2) for i in range(4) for h in (8 * half + i, 8 * half + 4 + i)]
    cols = np.concatenate([np.arange(h * HD, (h + 1) * HD) for h in order])
    qcols = np.concatenate([np.arange(QH * HD, 12 * P), cols])

    par = np.zeros((P, NPAR), np.float32)

    def put(name, a):
        par[:, PCOLS[name][0]:PCOLS[name][0] + PCOLS[name][1]] = a

    for layer in range(2):
        put(f"ffn1_norm{layer}", feature(ffn1_norm[layer]))
        put(f"mix_norm{layer}", feature(mix_norm[layer]))
        put(f"ffn2_norm{layer}", feature(ffn2_norm[layer]))
    for name, v in (("mu", ab_mu_shift), ("w0", rwkv_w0), ("a0", rwkv_a0), ("k_k", rwkv_k_k), ("k_a", rwkv_k_a),
                    ("r_k", rwkv_r_k), ("gn_gain", rwkv_gn_gain), ("gn_bias", rwkv_gn_bias), ("ln_gain", sg_ln_gain),
                    ("ln_bias", sg_ln_bias), ("b_o", attn_b_o)):
        put(name, feature(A(v)[0]))
    put("b_qkv", feature(A(attn_b_qkv)[0][qcols]))
    put("q_norm", np.tile(A(attn_q_norm)[0], 2)[:, None])
    put("k_norm", np.tile(A(attn_k_norm)[0], 2)[:, None])
    put("inv_freq", np.tile((10000.0 ** (-np.arange(0, HD, 2, dtype=np.float32) / np.float32(HD))
                             ).astype(np.float32), 4)[:, None])
    put("sinks", np.broadcast_to(A(attn_sinks)[0][order], (P, QH)))

    arrays = {
        "xT": A(x)[0].T.reshape(KD, P, T).transpose(1, 0, 2),
        "gu_w": np.concatenate(gu, 0),
        "down_w": np.concatenate(down, 0),
        "w_in": pairs(w_in),
        "w_out": pairs(ab_w_out[0]),
        "w_qkv": pairs(A(attn_w_qkv[0])[:, qcols]),
        "w_o": pairs(A(attn_w_o[0])[cols, :]),
        "params": par,
        "consts": constants(),
        "positions": np.broadcast_to(A(positions), (P, T)),
        "w_lora": np.concatenate([A(rwkv_w_decay_up)[0], A(rwkv_w_aaa_up)[0]], 0),
        "w_gate": A(rwkv_w_gate_up)[0],
        "w_spatialT": A(sg_w_spatial)[0].transpose(2, 0, 1),
        "b_spatial": np.broadcast_to(A(sg_b_spatial)[0], (P, 4, P)),
    }
    nc = bacc.Bacc("TRN2", target_bir_lowering=False, num_devices=1)
    args, ins = {}, {}
    for name, a in arrays.items():
        a = np.ascontiguousarray(a)
        ins[f"in_{name}"] = a
        args[name] = nc.dram_tensor(f"in_{name}", a.shape, mybir.dt.from_np(a.dtype), kind="ExternalInput").ap()
    args["out"] = nc.dram_tensor("out_x", (P, KD, T), F32, kind="ExternalOutput").ap()
    build(nc, **args)
    r = run_bass_kernel_spmd(nc, [ins], core_ids=[0])
    got = r.results[0]["out_x"]
    return got.transpose(1, 0, 2).reshape(D, T).T.reshape(1, T, D)
```

```python
from contextlib import ExitStack

import concourse.bass as bass
from concourse import mybir

F32 = mybir.dt.float32
F32R = mybir.dt.float32r
I32 = mybir.dt.int32
ALU = mybir.AluOpType
ACT = mybir.ActivationFunctionType
AX = mybir.AxisListType.X

P = 128
D = 1024
T = 256
KD = D // P
FF = 2816
KF = FF // P
SUB = KF // 2
HD = 64
AH = 8
AW = 512
CT = AW // P
ZA = 14
ZB = 8
W_IN_TILE = (12, 4, 6, 0, 2, 8, 10, 18, 20, 14, 16)
CH = 64
NC = T // CH
QH = 16
RMS_EPS, GN_EPS, LN_EPS = 1e-6, 64e-5, 1e-5
KAPPA = 0.6065306597126334

PCOLS = {}
_at = 0
for _name, _n in (("ffn1_norm0", 8), ("ffn1_norm1", 8), ("mix_norm0", 8), ("mix_norm1", 8), ("ffn2_norm0", 8),
                  ("ffn2_norm1", 8), ("mu", ZA), ("w0", 4), ("a0", 4), ("k_k", 4), ("k_a", 4), ("r_k", 4),
                  ("gn_gain", 4), ("gn_bias", 4), ("ln_gain", 4), ("ln_bias", 4), ("b_qkv", 12), ("q_norm", 1),
                  ("k_norm", 1), ("b_o", 8), ("inv_freq", 1), ("sinks", QH)):
    PCOLS[_name] = (_at, _n)
    _at += _n
NPAR = _at

CCOLS = {}
_at = 0
for _name, _n in (("ident", P), ("head_ones", P), ("rope_swap", P), ("mask_pair", 4 * P), ("mask16", P),
                  ("mask16T", P), ("mask32", P), ("mask64", P), ("causal", P), ("window", 2 * P), ("restart", T),
                  ("pick", 32), ("spread", CT * P),
                  ("ident64", CH)):
    CCOLS[_name] = (_at, _n)
    _at += _n
NCON = _at

LINEARS = (("gu", 22, 8, 0), ("down", 8, SUB, 0), ("w_in", 11, 8, 0), ("w_out", 4, 8, 0), ("gu", 22, 8, 1),
           ("down", 8, SUB, 1), ("gu", 22, 8, 2), ("down", 8, SUB, 2), ("qkv", 6, 8, 0), ("w_o", 4, 8, 0),
           ("gu", 22, 8, 3), ("down", 8, SUB, 3))
FIRST = [sum(x[1] for x in LINEARS[:n]) for n in range(len(LINEARS))]


def build(nc, xT, gu_w, down_w, w_in, w_out, w_qkv, w_o, params, consts, positions, w_lora, w_gate,
          w_spatialT, b_spatial, out):
    with ExitStack() as ctx:
        def sb(name, shape, dt=F32):
            return ctx.enter_context(nc.sbuf_tensor(name, shape, dt))

        def ps(name):
            return ctx.enter_context(nc.psum_tensor(name, [P, 512], F32))

        sems = {}

        def S(name):
            if name not in sems:
                sems[name] = ctx.enter_context(nc.semaphore(name))
            return sems[name]

        raw = sb("raw", [P, 4, 2 * SUB * P])
        split_ring = nc.sbuf_base
        w_hi = sb("w_hi", [P, 4, SUB * P], F32R)
        w_lo = sb("w_lo", [P, 4, SUB * P], F32R)
        x = sb("x", [P, KD, T])
        par = sb("par", [P, NPAR])
        con = sb("con", [P, NCON])
        sq = sb("sq", [P, 2, T])
        ssq = sb("ssq", [P, 2, T])
        root = sb("root", [P, T])
        rB = sb("rB", [P, T])
        ones = sb("ones", [P, P])
        eps = sb("eps", [P, 4])
        base = nc.sbuf_base
        base += -base % 32
        room = nc.sbuf_usable_end - base
        arena = sb("arena", [P, room // 4 - 16])

        def at(name, off, shape, dt=F32):
            n = 4
            for s in shape[1:]:
                n *= s
            assert off % 32 == 0 and off + n <= room - 64, (name, off, n, room)
            return nc.alloc_sbuf_tensor_at(name, shape, dt, offset=base + off)

        KB = 1024
        TEMP = 0
        FREE = 8 * KB
        HOFF = FREE + (room - 64 - 8 * KB - 16 * KB - 44 * KB) // 32 * 32
        AHI = HOFF + 16 * KB
        ALO = AHI + 22 * KB
        pre = at("pre", TEMP, [P, 2, 2, T])
        sil = at("sil", TEMP + 4 * KB, [P, 2, T])
        act_f = at("act_f", TEMP + 6 * KB, [P, 2, T])
        h_hi = at("h_hi", HOFF, [P, KD, T], F32R)
        h_lo = at("h_lo", HOFF + 8 * KB, [P, KD, T], F32R)
        a_hi = at("a_hi", AHI, [P, KF, T], F32R)
        a_lo = at("a_lo", ALO, [P, KF, T], F32R)
        y_hi = a_hi[:, KF - KD:KF, :]
        y_lo = a_lo[:, 0:KD, :]

        lin = [ps(f"lin{i}") for i in range(4)]
        mix = [ps(f"mix{i}") for i in range(4)]
        banks = mix + lin

        def pc(name, j=0, n=1, rows=slice(0, P)):
            return par[rows, PCOLS[name][0] + j:PCOLS[name][0] + j + n]

        def cc(name):
            a, n = CCOLS[name]
            return con[:, a:a + n]

        ident = cc("ident")

        zz = at("zz", FREE, [P, ZA + ZB, T + 1])
        ZBYTES = (ZA + ZB) * (T + 1) * 4
        zs = at("zs", ALO + 8 * KB, [P, ZA, T])
        RING = split_ring - base
        zz_end = FREE + (ZBYTES + 31) // 32 * 32
        s_tok = at("s_tok", zz_end, [P, 2, AW])
        s_sq = s_tok[:, :, :].rearrange("p a t -> p (a t)").rearrange("p (f t) -> p f t", f=4)
        g_mean, g_rstd = sq[:, 0, :], sq[:, 1, :]
        wsT = at("wsT", RING + 42 * KB, [P, 4, P])
        bsp = ssq[:, :, :].rearrange("p a t -> p (a t)").rearrange("p (f t) -> p f t", f=4)
        sd = at("sd", AHI, [P, CT, T])
        cs = at("cs", ALO + 4 * KB, [P, CT, T])
        ep = at("ep", FREE + (4 * (T + 1) * 4 + 31) // 32 * 32, [P, CT, T])
        ic = at("ic", AHI + 18 * KB, [P, CT, T])
        kq = at("kq", AHI + 14 * KB, [P, CT, T])
        ksq = at("ksq", AHI + 4 * KB, [P, CT, T])
        kf = at("kf", AHI + 8 * KB, [P, CT, T])
        AR = at("AR", AHI + 4 * KB, [P, CT, 2, 2, P])
        th = at("th", ALO, [P, T])
        sgx = at("sgx", ALO + 3 * KB, [P, T])
        kinv = sq[:, 1, :]
        KT, BT = cs, ic
        bonus_in = at("bonus_in", FREE, [P, CT, T])
        bonus = kq
        TM = [at("TM0", FREE, [P, 5, AW]), at("TM1", RING + 32 * KB, [P, 5, AW])]
        Yc = at("Yc", FREE + 10 * KB, [P, CT, T])
        lora = at("lora", TEMP, [P, AW])
        wgate = at("wgate", TEMP + 2 * KB, [P, AW])
        St = at("St", TEMP + 4 * KB, [P, 3, CT, CH])
        pend = at("pend", TEMP + 7 * KB, [P, CT, NC])
        kfb = at("kfb", TEMP + 7 * KB + 128, [P, 4])
        AM = [at("AM0", ALO + 8 * KB, [P, 4, 4 * P]), at("AM1", RING, [P, 4, 4 * P])]

        def four_mats(name, off0, off1):
            return [at(f"{name}{i}", off, [P, 4, P]) for i, off in enumerate((off0, off1))]

        Dm, DmT, M32, M64, D2, D2T, D4, D4T = [four_mats(name, HOFF + 2 * KB * i, RING + 8 * KB + 2 * KB * i)
                                               for i, name in enumerate(("Dm", "DmT", "M32", "M64", "D2", "D2T",
                                                                         "D4", "D4T"))]
        Zt = four_mats("Zt", AHI, RING + 24 * KB)
        Tt = four_mats("Tt", AHI + 2 * KB, RING + 26 * KB)
        Xa = four_mats("Xa", AHI + 12 * KB, RING + 28 * KB)
        HG = four_mats("HG", ALO + 20 * KB, RING + 30 * KB)
        ETs = at("ETs", ALO + 16 * KB, [P, 3, CT, CH])
        Fs = at("Fs", ALO, [P, 3, CT, CH])
        ysq = at("ysq", HOFF + 4 * KB, [P, CT, T])
        yst = at("yst", HOFF + 8 * KB, [P, 2, T])
        ROUNDS, NSC = 8, 3

        def round_of(g):
            return g % 2, 2 * (g // 2)

        qz = at("qz", FREE, [P, 12, T])
        cosT = at("cosT", FREE + 12 * KB, [P, T])
        sinT = at("sinT", FREE + 13 * KB, [P, T])
        cosg = at("cosg", FREE + 14 * KB, [P, 2, T])
        posf = at("posf", FREE + 14 * KB, [P, T])
        posi = at("posi", FREE + 15 * KB, [P, T], I32)
        swap = at("swap", FREE + 16 * KB, [P, 2, P])
        sm = at("sm", FREE + 17 * KB, [P, NSC, 8, 4])
        nsink = at("nsink", FREE + 17 * KB + 384, [P, QH])
        rq = at("rq", FREE + 17 * KB + 512, [P, 2, QH])
        trot = at("trot", FREE + 18 * KB, [P, 2, 2, T])
        v_tok = at("v_tok", FREE + 22 * KB, [P, 2, T])
        rk = at("rk", FREE + 24 * KB, [P, 2, T])
        qr = at("qr", AHI, [P, 10, T])
        qsq = at("qsq", ALO + 8 * KB, [P, 10, T])
        sc = at("sc", HOFF, [P, NSC, 2, 2, T])
        pT = at("pT", HOFF + 12 * KB, [P, 2, 2, 2, P])

        YSB = [(lin[0], lin[1]), (lin[2], lin[3]), (mix[0], mix[1])]

        ROT_BANK = [mix[1], mix[2], lin[(FIRST[8] + 2) % 4], lin[(FIRST[8] + 3) % 4], mix[1]]

        PART = {3: (CT, KD), 9: (0, CT)}
        W_O_BANK = [(mix[0], mix[1]), (mix[2], mix[3])]
        W_OUT_BANK = [(lin[1], lin[2]), (lin[3], lin[0]), (mix[1], mix[1]), (mix[2], mix[2])]

        block = ctx.enter_context(nc.Block())

        def rounds(eng, n0, n1, body):
            full = (n1 - n0) // 4
            if full >= 2:
                with eng.Fori(0, full) as i:
                    for q in range(4):
                        body(n0 + q + 4 * i, n0 + q, i)
            else:
                for i in range(full):
                    for q in range(4):
                        body(n0 + q + 4 * i, n0 + q, i)
            for q in range(4 * full, n1 - n0):
                body(n0 + q, n0 + q, 0)

        GAIN_AFTER = {1: "mix_norm0", 3: "ffn2_norm0", 5: "ffn1_norm1", 7: "mix_norm1", 9: "ffn2_norm1"}
        NORM_NO = {-1: 1, 1: 2, 3: 3, 5: 4, 7: 5, 9: 6}
        HBASE = {-1: 0, 1: 8, 3: 16, 5: 24, 7: 32, 9: 40}

        def steps_to(n):
            return 4 + FIRST[n]

        def needed_norm(n):
            return NORM_NO[n - 1]

        @block.sync
        def _(sp):
            sp.dma_start(par[:, :], params).then_inc(S("params_loaded"), 16)
            sp.dma_start(x[:, 0:2, :], xT[:, 0:2, :]).then_inc(S("x_first"), 16)
            sp.dma_start(x[:, 2:KD, :], xT[:, 2:KD, :]).then_inc(S("x_loaded"), 16)
            srcs = {"gu": gu_w, "down": down_w, "w_in": w_in, "w_out": w_out, "qkv": w_qkv, "w_o": w_o}
            for n, (name, steps, tiles, inst) in enumerate(LINEARS):
                g0, src = FIRST[n], srcs[name]
                off = inst * steps if name in ("gu", "down") else 0

                def load(j, q, i):
                    slot = (g0 + q) % 4
                    if n > 0 or q >= 4:
                        sp.wait_ge(S("lo_done"), 2 * (g0 + j - 4) + 2)
                    sp.dma_start(raw[:, slot, 0:2 * tiles * P],
                                 src[bass.ds(off + j, 1), :, :].rearrange("a p n -> (a p) n")
                                 ).then_inc(S(f"raw_full{slot}"), 16)

                if n == 0:
                    half = tiles * P
                    sp.dma_start(raw[:, 0, 0:half], gu_w[0, :, 0:half]).then_inc(S("raw_first"), 16)
                    sp.dma_start(raw[:, 0, half:2 * half], gu_w[0, :, half:2 * half]).then_inc(S("raw_full0"), 16)
                    for j in range(1, 4):
                        load(j, j, 0)
                    sp.dma_start(con[:, :], consts).then_inc(S("consts_loaded"), 16)
                    rounds(sp, 4, steps, load)
                elif name == "w_in":
                    for j in range(steps):
                        load(j, j, 0)
                        if j == 3:
                            sp.wait_ge(S("evacuated"), steps_to(2))
                            sp.dma_start(lora[:, :], w_lora).then_inc(S("lora_loaded"), 16)
                            sp.dma_start(wgate[:, :], w_gate).then_inc(S("lora_loaded"), 16)
                else:
                    rounds(sp, 0, steps, load)
                if n == 3:
                    sp.wait_ge(S("sub_done"), 2 * FIRST[3])
                    sp.wait_ge(S("norm_ready"), 2)
                    sp.dma_start(wsT[:, :, :], w_spatialT).then_inc(S("spatial_loaded"), 16)
                    sp.dma_start(bsp, b_spatial).then_inc(S("spatial_loaded"), 16)
                if n == 6:
                    sp.dma_start(posi[:, :], positions).then_inc(S("pos_loaded"), 16)
            for k0, k1 in ((0, KD - 2), (KD - 2, KD)):
                sp.wait_ge(S("evacuated"), steps_to(11) + k1)
                sp.dma_start(out[:, k0:k1, :], x[:, k0:k1, :]).then_inc(S("stored"), 16)
            sp.wait_ge(S("stored"), 32)

        @block.scalar
        def _(act):
            link_at = [0]

            def link(ins):
                link_at[0] += 1
                ins.then_inc(S("act_link"), 1)
                act.wait_ge(S("act_link"), link_at[0])

            def split_hi(n, j, q, i=0):
                _, _, tiles, _ = LINEARS[n]
                g0 = FIRST[n]
                slot = (g0 + q) % 4
                for s in range(2):
                    first = n == 0 and q == 0
                    if first and s == 0:
                        act.wait_ge(S("raw_first"), 16)
                    elif s == first:
                        act.wait_ge(S(f"raw_full{slot}"), 16 * ((g0 + q) // 4 + 1 + i))
                    if n > 0 or q >= 2:
                        act.wait_ge(S("sub_done"), 2 * (g0 + j - 2) + s + 1)
                    nc.scalar.activation(w_hi[:, (2 * (g0 + q) + s) % 4, 0:tiles * P],
                                         raw[:, slot, s * tiles * P:(s + 1) * tiles * P],
                                         ACT.Copy).then_inc(S("hi_done"), 1)

            def silu(n, j, q):
                m = KF * LINEARS[n][3] + j
                act.wait_ge(S("evacuated"), steps_to(n) + j + 1)
                act.wait_ge(S("act_made"), m + 1)
                nc.scalar.activation(sil[:, q % 2, :], pre[:, q % 2, 0, :], ACT.Silu).then_inc(S("silu_done"), 1)

            def hi_of_h(n, k):
                nc.scalar.activation(h_hi[:, k, :], x[:, k, :], ACT.Copy,
                                     scale=pc(GAIN_AFTER.get(n, "ffn1_norm0"), k)).then_inc(S("h_hi_done"), 1)

            def square(n, k):
                m = HBASE[n] + k
                if m >= 2:
                    act.wait_ge(S("sq_added"), m - 1)
                nc.scalar.activation(sq[:, k % 2, :], x[:, k, :], ACT.Square).then_inc(S("sq_done"), 1)

            def norm_root(no):
                act.wait_ge(S("stats_done"), no)
                if no > 1:
                    act.wait_ge(S("norm_ready"), no - 1)
                nc.scalar.activation(root[:, :], mix[0][:, 0:T], ACT.Sqrt, scale=1.0 / D,
                                     bias=eps[:, 0:1]).then_inc(S("root_done"), 1)

            def late(n, j, q):
                name = LINEARS[n][0]
                if name == "gu":
                    silu(n, j, q)
                elif n in GAIN_AFTER:
                    act.wait_ge(S("evacuated"), steps_to(n) + j + 1)
                    for k in ((j,) if name == "down" else (2 * j, 2 * j + 1)):
                        hi_of_h(n, k)
                        square(n, k)
                elif name == "w_in":
                    during_w_in(j + 2)
                elif name == "qkv":
                    if j == 4:
                        act.wait_ge(S("k_sums"), 1)
                        nc.scalar.activation(rk[0:64, 0, :], mix[0][0:64, T:2 * T], ACT.Sqrt, scale=1.0 / HD,
                                             bias=eps[0:64, 0:1]).then_inc(S("rk_root"), 1)
                    act.wait_ge(S("evacuated"), steps_to(n) + j + 1)
                    for f in (2 * j, 2 * j + 1):
                        nc.scalar.activation(qz[:, f, :], qz[:, f, :], ACT.Identity,
                                             bias=pc("b_qkv", f)).then_inc(S("qkv_biased"), 1)
                    if j != 1:
                        act.wait_ge(S("qkv_biased"), 2 * j + 2)
                        nc.scalar.activation(qsq[:, max(2 * j - 2, 0):max(2 * j - 2, 0) + 2, :], qz[:, 2 * j:2 * j + 2, :],
                                             ACT.Square).then_inc(S("q_squared"), 1)

            def during_w_in(j):
                if j == 4:
                    act.wait_ge(S("mixed"), 2)
                    nc.scalar.activation(th[0:64, :], zs[0:64, 12, :], ACT.Tanh).then_inc(S("tanh_done"), 1)
                    nc.scalar.activation(sgx[:, :], zs[:, 13, :], ACT.Sigmoid).then_inc(S("gate_in"), 1)
                if j in (5, 6):
                    act.wait_ge(S("mixed"), 2 * j - 6)
                    for c in (2 * j - 10, 2 * j - 9):
                        nc.scalar.activation(kq[:, c, :], zs[:, 4 + c, :], ACT.Copy, scale=pc("k_k", c)
                                             ).then_inc(S("kq_made"), 1)
                if j == 6:
                    act.wait_ge(S("decay_up"), 1)
                    for c in range(CT):
                        nc.scalar.activation(sd[:, c, :], mix[2 + c // 2][:, (c % 2) * T:(c % 2 + 1) * T], ACT.Sigmoid,
                                             bias=pc("w0", c)).then_inc(S("sd_made"), 1)
                if j == 7:
                    act.wait_ge(S("kq_made"), CT)
                    nc.scalar.activation(ksq[:, :, :], kq[:, :, :], ACT.Square).then_inc(S("kq_squared"), 1)
                    act.wait_ge(S("iclr_up"), 1)
                    for c in range(CT):
                        nc.scalar.activation(ic[:, c, :], mix[c // 2][:, (c % 2) * T:(c % 2 + 1) * T], ACT.Sigmoid,
                                             bias=pc("a0", c)).then_inc(S("ic_made"), 1)
                if j == 8:
                    act.wait_ge(S("kfb_made"), 1)
                    act.wait_ge(S("ic_made"), CT)
                    for c in range(CT):
                        nc.scalar.activation(kf[:, c, :], ic[:, c, :], ACT.Identity, scale=pc("k_a", c),
                                             bias=kfb[:, c:c + 1]).then_inc(S("kf_made"), 1)
                if j == 9:
                    act.wait_ge(S("kk_sums"), 1)
                    nc.scalar.activation(root[:, :], mix[2][:, 0:T], ACT.Sqrt).then_inc(S("kk_root"), 1)
                if j == 10:
                    act.wait_ge(S("cs_made"), 1)
                    nc.scalar.activation(ep[:, :, :], cs[:, :, :], ACT.Exp, scale=-KAPPA).then_inc(S("ep_made"), 1)
                    act.wait_ge(S("csm_made"), 1)
                    nc.scalar.activation(cs[:, :, :], cs[:, :, :], ACT.Exp, scale=KAPPA).then_inc(S("en_made"), 1)
                    nc.scalar.activation(sd[:, :, :], sd[:, :, :], ACT.Exp, scale=-KAPPA).then_inc(S("pprev_made"), 1)
                if j == 11:
                    act.wait_ge(S("evacuated"), steps_to(2) + 9)
                    nc.scalar.activation(zz[:, 18:22, 1:T + 1], zz[:, 18:22, 1:T + 1], ACT.Gelu).then_inc(S("s_gelu"), 1)

            def rwkv_gmlp():
                def copy(dst, src, wait, value, done):
                    act.wait_ge(S(wait), value)
                    nc.scalar.activation(dst, src, ACT.Copy).then_inc(S(done), 1)

                for i in range(8):
                    copy(TM[i % 2][:, (0, 3, 2, 1)[i // 2], :], (lin[2], lin[3], mix[0], mix[1])[i % 4][:, :],
                         "tok_t", i + 1, "tok_made")
                act.wait_ge(S("evacuated"), steps_to(3))
                nc.scalar.activation(zz[:, 14:18, 1:T + 1], zz[:, 14:18, 1:T + 1], ACT.Gelu).then_inc(S("u_gelu"), 1)
                for m in range(2):
                    def both(src, wait, value, done, dst):
                        for h in range(2):
                            copy(dst(h), v3(banks[4 * h + src]), wait, of_half(value, h), done)

                    for h in range(2):
                        copy(TM[m][:, 4, 4 * CH * h:4 * CH * (h + 1)], banks[4 * h + 2][:, 0:4 * CH],
                             "akv_t", of_half(m + 1, h), "akv_made")
                    for h in range(2):
                        copy(D2[h][:, :, :], v3(banks[4 * h]), f"n_sq{h}", 5 * m + 1, f"sq_made{h}")
                        copy(D2T[h][:, :, :], v3(banks[4 * h + 1]), f"n_sq{h}", 5 * m + 2, f"sq_made{h}")
                    for h in range(2):
                        copy(D4[h][:, :, :], v3(banks[4 * h + 2]), f"n_sq{h}", 5 * m + 3, f"sq_made{h}")
                        copy(D4T[h][:, :, :], v3(banks[4 * h + 3]), f"n_sq{h}", 5 * m + 4, f"sq_made{h}")
                    if m == 0:
                        act.wait_ge(S("s_centred"), 1)
                        nc.scalar.activation(s_sq, zz[:, 18:22, 1:T + 1], ACT.Square).then_inc(S("s_squared"), 1)
                    for h in range(2):
                        copy(D2[h][:, :, :], v3(banks[4 * h + 1]), f"n_sq{h}", 5 * m + 5, f"sq_made{h}")
                    if m == 0:
                        act.wait_ge(S("s_var"), 1)
                        nc.scalar.activation(g_rstd, banks[0][:, 0:T], ACT.Sqrt, scale=1.0 / AW,
                                             bias=eps[:, 1:2]).then_inc(S("s_root"), 1)
                    both(1, "t_t", 2 * m + 1, "t_made", lambda h: Tt[h][:, :, :])
                    if m == 0:
                        act.wait_ge(S("s_scaled"), 1)
                        for f in range(4):
                            nc.scalar.activation(zz[:, 18 + f, 1:T + 1], zz[:, 18 + f, 1:T + 1], ACT.Identity,
                                                 scale=pc("ln_gain", f), bias=pc("ln_bias", f)).then_inc(S("s_normed"), 1)
                    both(0, "t_t", 2 * m + 2, "t_made", lambda h: Tt[h][:, :, :])
                    both(2, "hg_t", m + 1, "hg_made", lambda h: HG[h][:, :, :])
                    for h in range(2):
                        copy(Yc[:, 2 * h:2 * h + 2, m * P:(m + 1) * P],
                             banks[4 * h][:, 0:2 * P].rearrange("p (c t) -> p c t", c=2), "y_t", of_half(m + 1, h), "y_done")
                act.wait_ge(S("e_t0"), 3)
                act.wait_ge(S("e_t1"), 3)
                for j in range(2):
                    split_hi(3, j, j)
                act.wait_ge(S("y_centred"), 1)
                nc.scalar.activation(ysq[:, :, :], Yc[:, :, :], ACT.Square).then_inc(S("y_squared"), 1)
                act.wait_ge(S("y_var"), 1)
                nc.scalar.activation(yst[:, 0, :], mix[0][:, 0:T], ACT.Sqrt, scale=1.0 / HD,
                                     bias=eps[:, 2:3]).then_inc(S("y_root"), 1)
                for c in range(CT):
                    act.wait_ge(S("y_scaled"), c // 2 + 1)
                    nc.scalar.activation(Yc[:, c, :], Yc[:, c, :], ACT.Identity, scale=pc("gn_gain", c),
                                         bias=pc("gn_bias", c)).then_inc(S("y_normed"), 1)
                for c in range(2):
                    act.wait_ge(S("y_gated"), c + 1)
                    nc.scalar.activation(y_hi[:, 2 * c:2 * c + 2, :], Yc[:, 2 * c:2 * c + 2, :], ACT.Copy
                                         ).then_inc(S("y_hi_done"), 1)

            def attention():
                act.wait_ge(S("q_sums"), 1)
                nc.scalar.activation(rq[:, :, :], mix[0][:, 0:2 * QH].rearrange("p (m h) -> p m h", m=2), ACT.Sqrt,
                                     scale=1.0 / HD, bias=eps[:, 0:1]).then_inc(S("rq_root"), 1)
                split_hi(9, 1, 1)
                act.wait_ge(S("rk_made"), 1)
                nc.scalar.activation(rk[0:64, 0, 0:4], rk[0:64, 0, 0:4], ACT.Exp)

                def exps(g):
                    (n, c), s4 = round_of(g), g % NSC
                    act.wait_ge(S("max_made"), g + 1)
                    for i in range(2):
                        for p in range(2):
                            u = 2 * i + p
                            nc.scalar.activation(sc[:, s4, i, p, 0:P * (n + 1)], sc[:, s4, i, p, 0:P * (n + 1)], ACT.Exp,
                                                 scale=rq[:, n, 2 * c + u:2 * c + u + 1],
                                                 bias=sm[:, s4, 2, u:u + 1], accum_out=sm[:, s4, 4, u:u + 1]
                                                 ).then_inc(S("exp_made"), 1)
                    nc.scalar.activation(sm[:, s4, 5, :], sm[:, s4, 3, :], ACT.Exp).then_inc(S("exp_made"), 1)

                def probs(g):
                    n, _ = round_of(g)
                    for i in range(2):
                        act.wait_ge(S("p_t"), 2 * g + i + 1)
                        src = lin[i][:, :].rearrange("p (h k q) -> p h k q", h=2, k=2)
                        nc.scalar.activation(pT[:, i, :, 0:n + 1, :], src[:, :, 0:n + 1, :], ACT.Copy
                                             ).then_inc(S("pT_made"), 1)

                def heads(g):
                    n, c = round_of(g)
                    act.wait_ge(S("pv"), g + 1)
                    nc.scalar.activation(y_hi[:, c:c + 2, n * P:(n + 1) * P],
                                         lin[2 + g % 2][:, 0:T].rearrange("p (i q) -> p i q", i=2), ACT.Copy
                                         ).then_inc(S("o_hi_done"), 1)

                act.wait_ge(S("rq_made"), 1)
                exps(0)
                for g in range(ROUNDS):
                    if g + 1 < ROUNDS:
                        exps(g + 1)
                    if g >= 1:
                        heads(g - 1)
                    nc.scalar.activation(x[:, g, :], x[:, g, :], ACT.Identity, bias=pc("b_o", g)
                                         ).then_inc(S("b_o_added"), 1)
                    probs(g)
                heads(ROUNDS - 1)

            act.wait_ge(S("setup"), 1)
            nc.scalar.activation(pre[:, 0, 0, 0:4], eps[:, :], ACT.Copy)
            act.wait_ge(S("params_loaded"), 16)
            act.wait_ge(S("x_first"), 16)
            for k in range(KD):
                if k == 2:
                    act.wait_ge(S("x_loaded"), 16)
                hi_of_h(-1, k)
            for j in range(2):
                split_hi(0, j, j)
                for k in range(4 * j, 4 * j + 4):
                    square(-1, k)
            for n, (name, steps, tiles, inst) in enumerate(LINEARS):
                if name not in ("w_out", "w_o"):
                    for j in range(2 if n else 0):
                        pn = LINEARS[n - 1][1] - 2 + j
                        late(n - 1, pn, pn)
                        split_hi(n, j, j)
                if n - 1 in NORM_NO:
                    norm_root(NORM_NO[n - 1])
                if name == "gu":
                    def step(j, q, i):
                        split_hi(n, j, q, i)
                        silu(n, j - 2, q - 2)
                    rounds(act, 2, steps, step)
                elif n in PART:
                    for j in range(2, steps):
                        split_hi(n, j, j)
                    for j in range(2, steps):
                        late(n, j - 2, j - 2)
                else:
                    for j in range(2, steps):
                        split_hi(n, j, j)
                        late(n, j - 2, j - 2)
                        if n == 7 and j == 7:
                            act.wait_ge(S("angles"), 1)
                            nc.scalar.activation(sinT[:, :], sinT[:, :], ACT.Sin).then_inc(S("rope_tables"), 1)
                            nc.scalar.activation(cosT[:, :], cosT[:, :], ACT.Sin).then_inc(S("rope_tables"), 1)
                if name in ("w_in", "qkv"):
                    for j in range(2):
                        late(n, steps - 2 + j, steps - 2 + j)
                    if name == "w_in":
                        rwkv_gmlp()
                    else:
                        split_hi(9, 0, 0)
                        attention()

        @block.vector
        def _(dve):
            link_at = [0]

            def link(ins):
                link_at[0] += 1
                ins.then_inc(S("dve_link"), 1)
                dve.wait_ge(S("dve_link"), link_at[0])

            def split_lo(n, j, q, i=0):
                _, _, tiles, _ = LINEARS[n]
                g0 = FIRST[n]
                slot = (g0 + q) % 4
                for s in range(2):
                    dve.wait_ge(S("hi_done"), 2 * (g0 + j) + s + 1)
                    sub = (2 * (g0 + q) + s) % 4
                    nc.vector.tensor_tensor(w_lo[:, sub, 0:tiles * P], raw[:, slot, s * tiles * P:(s + 1) * tiles * P],
                                            w_hi[:, sub, 0:tiles * P].bitcast(F32), ALU.subtract
                                            ).then_inc(S("lo_done"), 1)

            def bank(n, q):
                return lin[(FIRST[n] + q) % 4]

            def scale_gu(n, j, q):
                m = KF * LINEARS[n][3] + j
                dve.wait_ge(S("sub_done"), 2 * (FIRST[n] + j) + 2)
                dve.wait_ge(S("act_made"), m + 1)
                nc.vector.tensor_tensor(pre[:, q % 2, :, :], bank(n, q)[:, :].rearrange("p (a t) -> p a t", a=2),
                                        rB[:, :].unsqueeze(1).to_broadcast([P, 2, T]), ALU.mult
                                        ).then_inc(S("evacuated"), 1)

            def new_h_lo(n, k):
                dve.wait_ge(S("h_hi_done"), HBASE[n] + k + 1)
                nc.vector.scalar_tensor_tensor(out=h_lo[:, k, :], in0=x[:, k, :],
                                               scalar=pc(GAIN_AFTER.get(n, "ffn1_norm0"), k),
                                               in1=h_hi[:, k, :].bitcast(F32), op0=ALU.mult, op1=ALU.subtract
                                               ).then_inc(S("h_ready"), 1)

            def late(n, j, q):
                name = LINEARS[n][0]
                if name == "gu":
                    return scale_gu(n, j, q)
                dve.wait_ge(S("sub_done"), 2 * (FIRST[n] + j) + 2)
                src = bank(n, q)
                if name == "down":
                    nc.vector.scalar_tensor_tensor(out=x[:, j, :], in0=src[:, 0:T], scalar=0.5, in1=x[:, j, :],
                                                   op0=ALU.mult, op1=ALU.add).then_inc(S("evacuated"), 1)
                    if n in GAIN_AFTER:
                        new_h_lo(n, j)
                elif name in ("w_out", "w_o"):
                    if name == "w_o" and j == 0:
                        dve.wait_ge(S("b_o_added"), KD)
                    if name == "w_out":
                        src = W_OUT_BANK[j][1]
                    if j < 2:
                        first, src = (W_OUT_BANK if name == "w_out" else W_O_BANK)[j]
                        nc.vector.tensor_tensor(x[:, 2 * j, :], first[:, 0:T], x[:, 2 * j, :], ALU.add
                                                ).then_inc(S("first_half_added"), 1)
                        nc.vector.tensor_tensor(x[:, 2 * j + 1, :], src[:, T:2 * T], x[:, 2 * j + 1, :], ALU.add
                                                ).then_inc(S("evacuated"), 1)
                    else:
                        nc.vector.tensor_tensor(x[:, 2 * j:2 * j + 2, :], src[:, :].rearrange("p (a t) -> p a t", a=2),
                                                x[:, 2 * j:2 * j + 2, :], ALU.add).then_inc(S("evacuated"), 1)
                    new_h_lo(n, 2 * j)
                    new_h_lo(n, 2 * j + 1)
                else:
                    if name == "w_in":
                        f = W_IN_TILE[j]
                        dst = zz[:, f:f + 2, 1:T + 1]
                    else:
                        dst = qz[:, 2 * j:2 * j + 2, :]
                    nc.vector.tensor_tensor(dst, src[:, :].rearrange("p (a t) -> p a t", a=2),
                                            rB[:, :].unsqueeze(1).to_broadcast([P, 2, T]), ALU.mult
                                            ).then_inc(S("evacuated"), 1)
                    if name == "w_in":
                        during_w_in(j + 2)

            def token_mix(j):
                dve.wait_ge(S("shifted"), j + 1)
                for f in (W_IN_TILE[j], W_IN_TILE[j] + 1):
                    nc.vector.scalar_tensor_tensor(out=zs[:, f, :], in0=zs[:, f, :], scalar=pc("mu", f),
                                                   in1=zz[:, f, 1:T + 1], op0=ALU.mult, op1=ALU.add
                                                   ).then_inc(S("mixed"), 1)

            def during_w_in(j):
                if 3 <= j < 10:
                    token_mix(j - 3)
                if j == 2:
                    nc.vector.tensor_scalar(kfb[:, :], pc("k_a", 0, 4), -1.0, 1.0, ALU.mult, ALU.add
                                            ).then_inc(S("kfb_made"), 1)
                if j == 7:
                    dve.wait_ge(S("sd_made"), CT)
                    dve.wait_ge(S("consts_loaded"), 16)
                    for c in range(CT):
                        i = nc.vector.tensor_tensor_scan(cs[:, c, :], cc("restart"), sd[:, c, :], 0.0, ALU.mult, ALU.add)
                        if c < CT - 1:
                            i.then_inc(S("cs_parts"), 1)
                        else:
                            i.then_inc(S("cs_made"), 1)
                if j == 9:
                    dve.wait_ge(S("kk_root"), 1)
                    link(nc.vector.tensor_scalar(root[:, :], root[:, :], 1e-12, None, ALU.max))
                    nc.vector.reciprocal(kinv, root[:, :]).then_inc(S("kk_inv"), 1)
                if j == 10:
                    for c in range(2):
                        dve.wait_ge(S("kk_spread"), c + 1)
                        link(nc.vector.scalar_tensor_tensor(
                            out=kq[:, 2 * c:2 * c + 2, :], in0=mix[c][:, :].rearrange("p (a t) -> p a t", a=2),
                            scalar=-1.0, in1=kq[:, 2 * c:2 * c + 2, :], op0=ALU.mult, op1=ALU.mult))
                    dve.wait_ge(S("k_factored"), 1)
                    for c in range(CT):
                        nc.vector.scalar_tensor_tensor(out=bonus_in[:, c, :], in0=zs[:, c, :], scalar=pc("r_k", c),
                                                       in1=zs[:, 4 + c, :], op0=ALU.mult, op1=ALU.mult
                                                       ).then_inc(S("bonus_in"), 1)
                if j == 11:
                    dve.wait_ge(S("ep_made"), 1)
                    nc.vector.tensor_tensor(tok4(AR, 1), zs[:, 0:4, :].rearrange("p c (m t) -> p c m t", m=2),
                                            ep[:, :, :].rearrange("p c (m t) -> p c m t", m=2), ALU.mult
                                            ).then_inc(S("R_made"), 1)
                    link(nc.vector.tensor_copy(pend[:, :, :], ep[:, :, CH - 1:T:CH]))
                if j == 12:
                    dve.wait_ge(S("pprev_made"), 1)
                    nc.vector.tensor_tensor(tok4(AR, 0), kq[:, :, :].rearrange("p c (m t) -> p c m t", m=2),
                                            sd[:, :, :].rearrange("p c (m t) -> p c m t", m=2), ALU.mult
                                            ).then_inc(S("A_made"), 1)

            def norm_factor(no):
                dve.wait_ge(S("root_done"), no)
                nc.vector.reciprocal(rB[:, :], root[:, :]).then_inc(S("norm_ready"), 1)
                dve.wait_ge(S("norm_ready"), no)

            def rwkv_gmlp():
                dve.wait_ge(S("ic_scaled"), 1)
                nc.vector.tensor_tensor(KT[:, :, :], zs[:, 4:8, :], cs[:, :, :], ALU.mult).then_inc(S("K_made"), 1)
                nc.vector.scalar_tensor_tensor(out=BT[:, :, :], in0=kq[:, :, :], scalar=-1.0, in1=ic[:, :, :],
                                               op0=ALU.mult, op1=ALU.mult).then_inc(S("B_made"), 1)
                dve.wait_ge(S("A_made"), 1)
                dve.wait_ge(S("B_made"), 1)
                for c in range(2):
                    dve.wait_ge(S("bonus_sums"), c + 1)
                    nc.vector.tensor_tensor(bonus[:, 2 * c:2 * c + 2, :],
                                            mix[2 + c][:, :].rearrange("p (a t) -> p a t", a=2),
                                            zs[:, 8 + 2 * c:10 + 2 * c, :], ALU.mult).then_inc(S("bonus_done"), 1)
                dve.wait_ge(S("s_mean"), 1)
                nc.vector.tensor_scalar(g_mean, lin[0][:, 0:T], 1.0 / AW, None, ALU.mult).then_inc(S("mean_made"), 1)
                dve.wait_ge(S("spatial_loaded"), 32)
                nc.vector.tensor_tensor(wsT[:, :, :], wsT[:, :, :], cc("causal").unsqueeze(1).to_broadcast([P, 4, P]),
                                        ALU.mult).then_inc(S("ws_masked"), 1)

                def state(n, b):
                    if n:
                        dve.wait_ge(S("s_t"), n)
                        for po in range(2):
                            r = slice(64 * po, 64 * po + 64)
                            link(nc.vector.tensor_tensor(Fs[r, n, :, :],
                                                         b[po][r, 0:4 * CH].rearrange("p (c i) -> p c i", c=4),
                                                         Fs[r, n, :, :], ALU.add))
                    nc.vector.tensor_tensor(St[:, n, :, :], Fs[:, n, :, :],
                                            pend[:, :, n:n + 1].to_broadcast([P, CT, CH]), ALU.mult
                                            ).then_inc(S("S_made"), 1)

                for m in range(2):
                    for h in range(2):
                        if m:
                            if h == 0:
                                dve.wait_ge(S("EF_made0"), 4)
                                dve.wait_ge(S("EF_made1"), 4)
                                state(0, None)
                            dve.wait_ge(S("y_t"), of_half(m, h))
                        for u in range(4):
                            dve.wait_ge(S("pairs_t"), 8 * m + 4 * h + u + 1)
                            nc.vector.tensor_tensor(AM[h][:, u, :], banks[4 * h + u][:, :], cc("mask_pair"), ALU.mult
                                                    ).then_inc(S("AM_made"), 1)
                    for h in range(2):
                        dve.wait_ge(S("ab_t"), of_half(m + 1, h))
                        for mask, dst in (("mask16", Dm), ("mask32", M32), ("mask64", M64)):
                            for po in range(2):
                                nc.vector.tensor_tensor(
                                    dst[h][:, po:4:2, :], banks[4 * h + po][:, 0:2 * P].rearrange("p (a t) -> p a t", a=2),
                                    cc(mask).unsqueeze(1).to_broadcast([P, 2, P]), ALU.mult
                                ).then_inc(S("ab_masked"), 1)

                    def add_to_z(r, b):
                        for h in range(2):
                            dve.wait_ge(S("z_t"), of_half(5 * m + r + 1, h))
                            if r == 0:
                                dve.wait_ge(S("Z_first"), of_half(m + 1, h))
                            else:
                                dve.wait_ge(S("Z_made"), of_half(5 * m + r, h))
                            nc.vector.tensor_tensor(Zt[h][:, :, :], v3(banks[4 * h + b]), Zt[h][:, :, :], ALU.add
                                                    ).then_inc(S("Z_made"), 1)

                    def x_copy(r, b):
                        for h in range(2):
                            dve.wait_ge(S("x_t"), of_half(2 * m + r + 1, h))
                            nc.vector.tensor_copy(Xa[h][:, :, :], v3(banks[4 * h + b])).then_inc(S("x_made"), 1)

                    if m == 0:
                        dve.wait_ge(S("mean_made"), 1)
                        nc.vector.tensor_tensor(zz[:, 18:22, 1:T + 1], zz[:, 18:22, 1:T + 1],
                                                g_mean.unsqueeze(1).to_broadcast([P, 4, T]), ALU.subtract
                                                ).then_inc(S("s_centred"), 1)
                    else:
                        for i in range(2):
                            dve.wait_ge(S("spatial_done"), i + 1)
                            nc.vector.tensor_tensor(zz[:, 18:22, 1 + i * P:1 + (i + 1) * P], v3(banks[4 * i + 3]), bsp,
                                                    ALU.add).then_inc(S("s_mixed"), 1)
                    add_to_z(0, 0)
                    add_to_z(1, 2)
                    if m == 1:
                        state(1, (banks[0], banks[4]))
                    add_to_z(2, 3)
                    if m == 1:
                        dve.wait_ge(S("s_mixed"), 2)
                        dve.wait_ge(S("u_gelu"), 1)
                        link(nc.vector.tensor_tensor(zz[:, 18:22, 1:T + 1], zz[:, 18:22, 1:T + 1],
                                                     zz[:, 14:18, 1:T + 1], ALU.mult))
                        link(nc.vector.tensor_copy(y_hi[:, 4:8, :], zz[:, 18:22, 1:T + 1]))
                    x_copy(0, 0)
                    if m == 0:
                        dve.wait_ge(S("s_root"), 1)
                        link(nc.vector.reciprocal(g_rstd, g_rstd))
                    add_to_z(3, 2)
                    if m == 0:
                        nc.vector.tensor_tensor(zz[:, 18:22, 1:T + 1], zz[:, 18:22, 1:T + 1],
                                                g_rstd.unsqueeze(1).to_broadcast([P, 4, T]), ALU.mult
                                                ).then_inc(S("s_scaled"), 1)
                    else:
                        nc.vector.tensor_tensor(y_lo[:, 4:8, :], zz[:, 18:22, 1:T + 1], y_hi[:, 4:8, :].bitcast(F32),
                                                ALU.subtract).then_inc(S("u_used"), 1)
                    x_copy(1, 3)
                    add_to_z(4, 1)
                    if m == 0:
                        for i in range(2):
                            dve.wait_ge(S("s_tok_t"), i + 1)
                            nc.vector.tensor_copy(s_tok[:, i, :], banks[4 * i + 2][:, :]).then_inc(S("s_tok_made"), 1)
                    for h in range(2):
                        cs2 = slice(2 * h, 2 * h + 2)
                        dve.wait_ge(S("q_t"), of_half(m + 1, h))
                        nc.vector.tensor_tensor(AR[:, cs2, m, 1, :],
                                                banks[4 * h + 3][:, 0:2 * P].rearrange("p (c t) -> p c t", c=2),
                                                AR[:, cs2, m, 1, :], ALU.add).then_inc(S("Q_made"), 1)
                        for c2 in range(2):
                            n = 2 * m + c2
                            if n < NC - 1:
                                dve.wait_ge(S(f"e_t{h}"), n + 1)
                                ef = banks[4 * h + 1 + c2][:, :].rearrange("p (k c i) -> p k c i", k=4, c=2)
                                nc.vector.tensor_tensor(ETs[:, n, cs2, :], ef[:, 0, :, :],
                                                        cc("ident64").unsqueeze(1).to_broadcast([P, 2, CH]), ALU.add
                                                        ).then_inc(S(f"EF_made{h}"), 1)
                                nc.vector.tensor_copy(Fs[:, n, cs2, :], ef[:, 1, :, :]).then_inc(S(f"EF_made{h}"), 1)
                dve.wait_ge(S("EF_made0"), 6)
                dve.wait_ge(S("EF_made1"), 6)
                state(2, mix[0:2])
                for n in range(3):
                    dve.wait_ge(S("ys_t"), n + 1)
                    for po in range(2):
                        r = slice(64 * po, 64 * po + 64)
                        link(nc.vector.tensor_tensor(Yc[r, :, (n + 1) * CH:(n + 2) * CH],
                                                     YSB[n][po][r, 0:4 * CH].rearrange("p (c i) -> p c i", c=4),
                                                     Yc[r, :, (n + 1) * CH:(n + 2) * CH], ALU.add))
                nc.vector.memset(St[:, 0, 0, 0:1], 0.0).then_inc(S("y_complete"), 1)
                split_lo(3, 0, 0)
                for c in range(2):
                    dve.wait_ge(S("y_mean"), c + 1)
                    link(nc.vector.scalar_tensor_tensor(
                        out=Yc[:, 2 * c:2 * c + 2, :], in0=mix[3 * c][:, :].rearrange("p (a t) -> p a t", a=2),
                        scalar=-1.0 / HD, in1=Yc[:, 2 * c:2 * c + 2, :], op0=ALU.mult, op1=ALU.add))
                nc.vector.memset(St[:, 0, 0, 0:1], 0.0).then_inc(S("y_centred"), 1)
                split_lo(3, 1, 1)
                dve.wait_ge(S("y_root"), 1)
                nc.vector.reciprocal(yst[:, 1, :], yst[:, 0, :]).then_inc(S("y_inv"), 1)
                for c in range(2):
                    dve.wait_ge(S("y_spread"), c + 1)
                    nc.vector.tensor_tensor(Yc[:, 2 * c:2 * c + 2, :],
                                            mix[3 * c][:, :].rearrange("p (a t) -> p a t", a=2),
                                            Yc[:, 2 * c:2 * c + 2, :], ALU.mult).then_inc(S("y_scaled"), 1)
                for c in range(2):
                    half = Yc[:, 2 * c:2 * c + 2, :]
                    dve.wait_ge(S("y_normed"), 2 * c + 2)
                    link(nc.vector.tensor_tensor(half, half, bonus[:, 2 * c:2 * c + 2, :], ALU.add))
                    dve.wait_ge(S("gate_up"), c + 1)
                    nc.vector.tensor_tensor(half, mix[1 + c][:, :].rearrange("p (a t) -> p a t", a=2), half, ALU.mult
                                            ).then_inc(S("y_gated"), 1)
                for c in range(2):
                    dve.wait_ge(S("y_hi_done"), c + 1)
                    nc.vector.tensor_tensor(y_lo[:, 2 * c:2 * c + 2, :], Yc[:, 2 * c:2 * c + 2, :],
                                            y_hi[:, 2 * c:2 * c + 2, :].bitcast(F32), ALU.subtract
                                            ).then_inc(S("y_lo_done"), 1)

            def rope_angles(part):
                C1, C2 = 6.28125, 0.0019350051879882812
                C3 = 6.283185307179586 - C1 - C2
                ROUND = 12582912.0
                PI = 3.14159274101257
                if part == 0:
                    dve.wait_ge(S("pos_loaded"), 16)
                    link(nc.vector.tensor_copy(posf[:, :], posi[:, :]))
                    link(nc.vector.tensor_scalar(posf[:, :], posf[:, :], pc("inv_freq"), None, ALU.mult))
                    for which, name in enumerate(("q_norm", "k_norm")):
                        nc.vector.tensor_scalar(swap[:, which, :], cc("rope_swap"), pc(name), None, ALU.mult
                                                ).then_inc(S("swap_made"), 1)
                elif part < 3:
                    dst, quarter = ((sinT, 0.0), (cosT, 0.25))[part - 1]
                    turns = posi[:, :].bitcast(F32)
                    link(nc.vector.tensor_scalar(turns, posf[:, :], 1.0 / 6.283185307179586, quarter, ALU.mult, ALU.add))
                    link(nc.vector.tensor_scalar(turns, turns, ROUND, -ROUND, ALU.add, ALU.add))
                    for first, c in enumerate((C1, C2, C3)):
                        link(nc.vector.scalar_tensor_tensor(out=dst[:, :], in0=turns, scalar=-c,
                                                            in1=(dst if first else posf)[:, :],
                                                            op0=ALU.mult, op1=ALU.add))
                    if quarter:
                        link(nc.vector.tensor_scalar(dst[:, :], dst[:, :], PI / 2, None, ALU.add))
                    link(nc.vector.tensor_scalar(dst[:, :], dst[:, :], PI, -PI, ALU.min, ALU.max))
                else:
                    nc.vector.tensor_scalar(nsink[:, :], pc("sinks", 0, QH), -1.0, None, ALU.mult
                                            ).then_inc(S("angles"), 1)

            def rope(k):
                j = (0, 2, 3, 4, 5)[k]
                f = 2 * j
                dst = qr[:, (8 if j == 0 else f - 4):(8 if j == 0 else f - 4) + 2, :]
                dve.wait_ge(S("rot_t"), k + 1)
                nc.vector.tensor_tensor(trot[:, k % 2, :, :], ROT_BANK[k][:, :].rearrange("p (a t) -> p a t", a=2),
                                        sinT[:, :].unsqueeze(1).to_broadcast([P, 2, T]), ALU.mult
                                        ).then_inc(S("rot_used"), 1)
                dve.wait_ge(S("rot_used"), k + 1)
                dve.wait_ge(S("q_cosined"), k + 1)
                nc.vector.tensor_tensor(dst, dst, trot[:, k % 2, :, :], ALU.add).then_inc(S("roped"), 1)

            def during_qkv(j):
                if j == 2:
                    dve.wait_ge(S("rope_tables"), 2)
                    for which, name in enumerate(("q_norm", "k_norm")):
                        nc.vector.tensor_scalar(cosg[:, which, :], cosT[:, :], pc(name), None, ALU.mult
                                                ).then_inc(S("gains_in"), 1)
                if j == 5:
                    dve.wait_ge(S("v_t"), 1)
                    nc.vector.tensor_copy(v_tok[:, :, :], mix[3][:, :].rearrange("p (m f) -> p m f", m=2)
                                          ).then_inc(S("v_tok_made"), 1)
                    rope(0)
                    dve.wait_ge(S("rk_root"), 1)
                    nc.vector.reciprocal(rk[0:64, 1, :], rk[0:64, 0, :]).then_inc(S("rk_made"), 1)

            def attention():
                dve.wait_ge(S("rk_spread"), 1)
                nc.vector.tensor_tensor(qr[:, 8:10, :], mix[3][:, :].rearrange("p (a t) -> p a t", a=2), qr[:, 8:10, :],
                                        ALU.mult).then_inc(S("k_scaled"), 1)
                for k in range(2, 5):
                    rope(k)

                def maxima(g):
                    (n, c), s4 = round_of(g), g % NSC
                    W = P * (n + 1)
                    mask = cc("window")[:, 2 * P - W:2 * P].unsqueeze(1).to_broadcast([P, 2, W])
                    if g >= NSC:
                        dve.wait_ge(S("p_t"), 2 * (g - NSC) + 2)
                    for p in range(2):
                        dve.wait_ge(S("scores_t"), 2 * g + p + 1)
                        nc.vector.tensor_tensor(sc[:, s4, :, p, 0:W],
                                                mix[2 - 2 * (g % 2) + p][:, :].rearrange("p (i t) -> p i t", i=2)[:, :, 0:W],
                                                mask, ALU.add).then_inc(S("masked"), 1)
                    dve.wait_ge(S("masked"), 2 * g + 2)
                    link(nc.vector.tensor_reduce(sm[:, s4, 0, :].rearrange("p (i h) -> p i h", i=2), sc[:, s4, :, :, 0:W],
                                                 AX, ALU.max, negate=True))
                    if g == 0:
                        dve.wait_ge(S("rq_root"), 1)
                        link(nc.vector.reciprocal(rq[:, :, :], rq[:, :, :]))
                        nc.vector.tensor_scalar(rq[:, :, :], rq[:, :, :], HD ** -0.5, None, ALU.mult
                                                ).then_inc(S("rq_made"), 1)
                        dve.wait_ge(S("rq_made"), 1)
                    link(nc.vector.tensor_tensor(sm[:, s4, 1, :], sm[:, s4, 0, :], rq[:, n, 2 * c:2 * c + 4], ALU.mult))
                    link(nc.vector.tensor_tensor(sm[:, s4, 2, :], sm[:, s4, 1, :], nsink[:, 2 * c:2 * c + 4], ALU.min))
                    nc.vector.tensor_tensor(sm[:, s4, 3, :], sm[:, s4, 2, :], pc("sinks", 2 * c, 4), ALU.add
                                            ).then_inc(S("max_made"), 1)

                def normalise(g):
                    (n, _), s4 = round_of(g), g % NSC
                    W = P * (n + 1)
                    dve.wait_ge(S("exp_made"), 5 * g + 5)
                    link(nc.vector.tensor_tensor(sm[:, s4, 6, :], sm[:, s4, 4, :], sm[:, s4, 5, :], ALU.add))
                    link(nc.vector.reciprocal(sm[:, s4, 7, :], sm[:, s4, 6, :]))
                    for i in range(2):
                        nc.vector.tensor_tensor(sc[:, s4, i, :, 0:W], sc[:, s4, i, :, 0:W],
                                                sm[:, s4, 7, 2 * i:2 * i + 2].unsqueeze(2).to_broadcast([P, 2, W]),
                                                ALU.mult).then_inc(S("p_made"), 1)

                def heads_lo(g):
                    n, c = round_of(g)
                    dve.wait_ge(S("o_hi_done"), g + 1)
                    nc.vector.tensor_tensor(y_lo[:, c:c + 2, n * P:(n + 1) * P],
                                            lin[2 + g % 2][:, 0:T].rearrange("p (i q) -> p i q", i=2),
                                            y_hi[:, c:c + 2, n * P:(n + 1) * P].bitcast(F32), ALU.subtract
                                            ).then_inc(S("o_lo_done"), 1)

                maxima(0)
                for g in range(ROUNDS):
                    if g + 1 < ROUNDS:
                        maxima(g + 1)
                    if g in (1, ROUNDS - 2):
                        split_lo(9, int(g > 1), int(g > 1))
                    normalise(g)
                    if g >= 1:
                        heads_lo(g - 1)
                heads_lo(ROUNDS - 1)

            for i, e in enumerate((RMS_EPS, LN_EPS, GN_EPS, 0.0)):
                link(nc.vector.memset(eps[:, i:i + 1], e))
            nc.vector.memset(ones[:, :], 1.0).then_inc(S("setup"), 1)
            nc.vector.memset(root[:, :], 1.0).then_inc(S("evacuated"), 4)
            dve.wait_ge(S("params_loaded"), 16)
            dve.wait_ge(S("x_first"), 16)
            for k in range(KD):
                if k == 2:
                    dve.wait_ge(S("x_loaded"), 16)
                new_h_lo(-1, k)
            for n, (name, steps, tiles, inst) in enumerate(LINEARS):
                if name not in ("w_out", "w_o"):
                    for j in range(2):
                        if n:
                            pn = LINEARS[n - 1][1] - 2 + j
                            late(n - 1, pn, pn)
                        split_lo(n, j, j)
                if n - 1 in NORM_NO:
                    norm_factor(NORM_NO[n - 1])
                if name == "gu":
                    def step(j, q, i):
                        split_lo(n, j, q, i)
                        scale_gu(n, j - 2, q - 2)
                    rounds(dve, 2, steps, step)
                elif n in PART:
                    for j in range(2, steps):
                        split_lo(n, j, j)
                    for j in range(2, steps):
                        late(n, j - 2, j - 2)
                else:
                    for j in range(2, steps):
                        split_lo(n, j, j)
                        late(n, j - 2, j - 2)
                        if name == "qkv":
                            during_qkv(j)
                        if n == 7 and 2 < j < 7:
                            rope_angles(j - 3)
                if name in ("w_in", "qkv"):
                    late(n, steps - 2, steps - 2)
                    if name == "qkv":
                        rope(1)
                    late(n, steps - 1, steps - 1)
                    if name == "w_in":
                        rwkv_gmlp()
                    else:
                        attention()
            for j in range(2):
                late(11, LINEARS[11][1] - 2 + j, LINEARS[11][1] - 2 + j)

        @block.gpsimd
        def _(pool):
            nc.gpsimd.memset(zz[:, :, 0:1], 0.0).then_inc(S("zz_zeroed"), 1)
            nc.gpsimd.memset(sil[:, :, :], 0.0).then_inc(S("act_made"), 2)

            def add_square(n, k):
                m = HBASE[n] + k
                pool.wait_ge(S("sq_done"), m + 1)
                if k == 0:
                    if NORM_NO[n] > 1:
                        pool.wait_ge(S("stats_done"), NORM_NO[n] - 1)
                    nc.gpsimd.tensor_copy(ssq[:, 0, :], sq[:, 0, :]).then_inc(S("sq_added"), 1)
                else:
                    pool.wait_ge(S("sq_added"), m)
                    nc.gpsimd.tensor_tensor(ssq[:, 0, :], ssq[:, 0, :], sq[:, k % 2, :], ALU.add
                                            ).then_inc(S("sq_added"), 1)

            def hidden(n, j, q):
                m = KF * LINEARS[n][3] + j
                pool.wait_ge(S("silu_done"), m + 1)
                nc.gpsimd.tensor_tensor(act_f[:, q % 2, :], sil[:, q % 2, :], pre[:, q % 2, 1, :], ALU.mult
                                        ).then_inc(S("act_made"), 1)
                pool.wait_ge(S("act_made"), m + 3)
                if LINEARS[n][3] and isinstance(q, int) and q < 2:
                    pool.wait_ge(S("sub_done"), 2 * FIRST[n])
                nc.gpsimd.tensor_copy(a_hi[:, bass.ds(j, 1), :].rearrange("p a t -> p (a t)"), act_f[:, q % 2, :]
                                      ).then_inc(S("a_hi_done"), 1)
                pool.wait_ge(S("a_hi_done"), m + 1)
                nc.gpsimd.tensor_tensor(a_lo[:, bass.ds(j, 1), :].rearrange("p a t -> p (a t)"), act_f[:, q % 2, :],
                                        a_hi[:, bass.ds(j, 1), :].rearrange("p a t -> p (a t)").bitcast(F32),
                                        ALU.subtract).then_inc(S("a_ready"), 1)

            def rwkv_gmlp():
                pool.wait_ge(S("consts_loaded"), 16)
                for m in range(2):
                    for h in range(2):
                        pool.wait_ge(S("AM_made"), 8 * m + 4 * h + 4)
                        nc.gpsimd.tensor_tensor(DmT[h][:, :, :], AM[h][:, :, 0:P],
                                                cc("mask16T").unsqueeze(1).to_broadcast([P, 4, P]), ALU.mult
                                                ).then_inc(S("DmT_made"), 1)
                        pool.wait_ge(S("DmT_made"), of_half(m + 1, h))
                        nc.gpsimd.tensor_tensor(Zt[h][:, :, :], DmT[h][:, :, :],
                                                ident.unsqueeze(1).to_broadcast([P, 4, P]), ALU.add
                                                ).then_inc(S("Z_first"), 1)

            for k in range(KD):
                add_square(-1, k)
            for n, (name, steps, tiles, inst) in enumerate(LINEARS):
                if name == "gu":
                    rounds(pool, 0, steps, lambda j, q, i: hidden(n, j, q))
                elif n in GAIN_AFTER:
                    for k in range(KD):
                        add_square(n, k)
                elif name == "qkv":
                    pool.wait_ge(S("gains_in"), 2)
                    for j in (0, 2, 3, 4, 5):
                        pool.wait_ge(S("qkv_biased"), 2 * j + 2)
                        f = 8 if j == 0 else 2 * j - 4
                        nc.gpsimd.tensor_tensor(qr[:, f:f + 2, :], qz[:, 2 * j:2 * j + 2, :],
                                                cosg[:, 1 if j == 0 else 0, :].unsqueeze(1).to_broadcast([P, 2, T]),
                                                ALU.mult).then_inc(S("q_cosined"), 1)
                elif name == "w_in":
                    pool.wait_ge(S("zz_zeroed"), 1)
                    for j in range(7):
                        pool.wait_ge(S("evacuated"), steps_to(n) + j + 1)
                        f = W_IN_TILE[j]
                        nc.gpsimd.tensor_tensor(zs[:, f:f + 2, :], zz[:, f:f + 2, 0:T], zz[:, f:f + 2, 1:T + 1],
                                                ALU.subtract).then_inc(S("shifted"), 1)
                    pool.wait_ge(S("cs_made"), 1)
                    nc.gpsimd.tensor_tensor(sd[:, :, :], cs[:, :, :], sd[:, :, :], ALU.subtract).then_inc(S("csm_made"), 1)
                    pool.wait_ge(S("kf_made"), CT)
                    nc.gpsimd.tensor_tensor(zs[:, 4:8, :], zs[:, 4:8, :], kf[:, :, :], ALU.mult
                                            ).then_inc(S("k_factored"), 1)
                    pool.wait_ge(S("en_made"), 1)
                    nc.gpsimd.tensor_tensor(ic[:, :, :], ic[:, :, :], cs[:, :, :], ALU.mult).then_inc(S("ic_scaled"), 1)
                    rwkv_gmlp()

        @block.tensor
        def _(pe):
            mm = nc.tensor.matmul

            def products(out, sub, w0, tiles, in_hi, in_lo, k0, last_k, first, done, signal=True):
                for k in range(tiles):
                    wa = w_hi[:, sub, (w0 + k) * P:(w0 + k + 1) * P]
                    wb = w_lo[:, sub, (w0 + k) * P:(w0 + k + 1) * P]
                    a, b = in_hi[:, k0 + k, :], in_lo[:, k0 + k, :]
                    if done is not None:
                        done(k0 + k)
                    mm(out, wa, a, start=first and k == 0, stop=False)
                    mm(out, wa, b, start=False, stop=False)
                    ins = mm(out, wb, a, start=False, stop=last_k and k == tiles - 1)
                if signal:
                    ins.then_inc(S("sub_done"), 1)

            def part(n, j, s, k0, k1):
                sub = (2 * (FIRST[n] + j) + s) % 4
                if k0 == PART[n][0]:
                    pe.wait_ge(S("lo_done"), 2 * (FIRST[n] + j) + s + 1)
                products((W_OUT_BANK if n == 3 else W_O_BANK)[j][s][:, s * T:(s + 1) * T], sub, k0, k1 - k0, y_hi, y_lo,
                         k0, k0 != PART[n][0], k0 == PART[n][0], None, signal=k0 != PART[n][0])

            def early_part(n, j, s):
                part(n, j, s, *PART[n])

            def step(n, j, q, i=0):
                name, _, tiles, inst = LINEARS[n]
                g0 = FIRST[n]
                b = W_OUT_BANK[q][0] if name == "w_out" else lin[(g0 + q) % 4]
                pe.wait_ge(S("evacuated"), g0 + j + 1)
                for s in range(2):
                    pe.wait_ge(S("lo_done"), 2 * (g0 + j) + s + 1)
                    sub = (2 * (g0 + q) + s) % 4
                    if name == "down":
                        ready = (lambda k: pe.wait_ge(S("a_ready"), KF * inst + k + 1)) if q == 0 else None
                        products(b[:, 0:T], sub, 0, tiles, a_hi, a_lo, s * tiles, s == 1, s == 0, ready)
                    elif name in ("w_out", "w_o"):
                        products(b[:, s * T:(s + 1) * T], sub, 0, tiles, y_hi, y_lo, 0, True, True, None)
                    else:
                        ready = (lambda k: pe.wait_ge(S("h_ready"), HBASE[n - 1] + k + 1)) if q == 0 and s == 0 else None
                        products(b[:, s * T:(s + 1) * T], sub, 0, tiles, h_hi, h_lo, 0, True, True, ready)

            def stats(no):
                pe.wait_ge(S("sq_added"), 8 * no)
                pe.wait_ge(S("setup"), 1)
                mm(mix[0][:, 0:T], ones[:, :], ssq[:, 0, :], start=True, stop=True).then_inc(S("stats_done"), 1)

            def during_w_in(j):
                if j == 5:
                    pe.wait_ge(S("consts_loaded"), 16)
                    pe.wait_ge(S("norm_ready"), 2)
                    pe.wait_ge(S("lora_loaded"), 32)
                    pe.wait_ge(S("tanh_done"), 1)
                    for c in range(CT):
                        ins = mm(mix[2 + c // 2][:, (c % 2) * T:(c % 2 + 1) * T], lora[0:64, c * P:(c + 1) * P], th[0:64, :],
                                 start=True, stop=True)
                    ins.then_inc(S("decay_up"), 1)
                    for c in range(CT):
                        ins = mm(mix[c // 2][:, (c % 2) * T:(c % 2 + 1) * T], lora[64:128, c * P:(c + 1) * P],
                                 zs[64:128, 12, :], start=True, stop=True)
                    ins.then_inc(S("iclr_up"), 1)
                if j == 7:
                    pe.wait_ge(S("kq_squared"), 1)
                    pe.wait_ge(S("sd_made"), CT)
                    for c in range(CT):
                        ins = mm(mix[2][32 * c:32 * c + 32, 0:T], cc("pick"), ksq[:, c, :], start=True, stop=True)
                    ins.then_inc(S("kk_sums"), 1)
                if j == 9:
                    pe.wait_ge(S("kk_inv"), 1)
                    pe.wait_ge(S("ic_made"), CT)
                    for c in range(CT):
                        ins = mm(mix[c // 2][:, (c % 2) * T:(c % 2 + 1) * T], cc("spread")[:, c * P:(c + 1) * P],
                                 kinv, start=True, stop=True)
                        if c % 2:
                            ins.then_inc(S("kk_spread"), 1)
                if j == 10:
                    pe.wait_ge(S("bonus_in"), CT)
                    for c in range(2):
                        mm(mix[2 + c][:, :], cc("head_ones"), bonus_in[:, 2 * c:2 * c + 2, :], start=True, stop=True
                           ).then_inc(S("bonus_sums"), 1)

            def rwkv_gmlp():
                pe.wait_ge(S("evacuated"), steps_to(3))
                pe.wait_ge(S("s_gelu"), 1)
                for f in range(4):
                    ins = mm(lin[0][:, 0:T], ones[:, :], zz[:, 18 + f, 1:T + 1], start=f == 0, stop=f == 3)
                ins.then_inc(S("s_mean"), 1)
                for i in range(8):
                    m, kind = i % 2, i // 2
                    if kind and m == 0:
                        pe.wait_ge(S(("", "A_made", "K_made", "B_made")[kind]), 1)
                    if i >= 4:
                        pe.wait_ge(S("tok_made"), i - 3)
                    for c in range(CT):
                        tk = slice(m * P, (m + 1) * P)
                        src = (zs[:, 8 + c, tk], AR[:, c, m, 0, :], KT[:, c, tk], BT[:, c, tk])[kind]
                        ins = nc.tensor.transpose((lin[2], lin[3], mix[0], mix[1])[i % 4][:, c * P:(c + 1) * P], src, ident)
                    ins.then_inc(S("tok_t"), 1)
                pe.wait_ge(S("R_made"), 1)
                pe.wait_ge(S("bonus_done"), 2)
                pe.wait_ge(S("mean_made"), 1)
                pe.wait_ge(S("tok_made"), 8)

                def heads_of(h):
                    return [(u, 2 * h + u // 2, 64 * (u % 2), 4 * h + u) for u in range(4)]

                def state_part(n, b):
                    pe.wait_ge(S("S_made"), n)
                    for po in range(2):
                        r = slice(64 * po, 64 * po + 64)
                        for c in range(CT):
                            ins = mm(b[po][r, c * CH:(c + 1) * CH], ETs[r, n, c, :], St[r, n - 1, c, :],
                                     start=True, stop=True)
                    ins.then_inc(S("s_t"), 1)

                def four(bank_, a, b_, sem):
                    for u in range(4):
                        ins = mm(bank_[:, u * P:(u + 1) * P], a[:, u, :], b_[:, u, :], start=True, stop=True)
                    ins.then_inc(S(sem), 1)

                for m in range(2):
                    tk = slice(m * P, (m + 1) * P)
                    for h in range(2):
                        if m:
                            pe.wait_ge(S(f"EF_made{h}"), 4)
                            pe.wait_ge(S("Q_made"), of_half(1, h))
                            pe.wait_ge(S("y_done"), of_half(1, h))
                        for u, c, po, _ in heads_of(h):
                            r = slice(po, po + 64)
                            mm(banks[4 * h + u][:, 0:2 * P], BT[r, c, tk], AR[r, c, m, :, :], start=True, stop=True)
                            mm(banks[4 * h + u][:, 2 * P:4 * P], KT[r, c, tk], AR[r, c, m, :, :], start=True, stop=True
                               ).then_inc(S("pairs_t"), 1)
                    for h in range(2):
                        pe.wait_ge(S("AM_made"), 8 * m + 4 * h + 2)
                        for u, c, po, _ in heads_of(h):
                            r = slice(po, po + 64)
                            ins = mm(banks[4 * h + u % 2][:, (u // 2) * P:(u // 2 + 1) * P], AR[r, c, m, 0, :], BT[r, c, tk],
                                     start=True, stop=True)
                        ins.then_inc(S("ab_t"), 1)
                    for h in range(2):
                        pe.wait_ge(S("AM_made"), 8 * m + 4 * h + 4)
                        for u, c, po, hd in heads_of(h):
                            ins = mm(banks[4 * h + 2][:, u * CH:(u + 1) * CH], AM[h][:, u, 2 * P:3 * P],
                                     TM[m][:, 0, hd * HD:(hd + 1) * HD], start=True, stop=True)
                        ins.then_inc(S("akv_t"), 1)
                    if m:
                        pe.wait_ge(S("ws_masked"), 1)
                        for i in range(2):
                            pe.wait_ge(S("s_tok_made"), i + 1)
                            for f in range(4):
                                ins = mm(banks[4 * i + 3][:, f * P:(f + 1) * P], s_tok[:, i, f * P:(f + 1) * P],
                                         wsT[:, f, :], start=True, stop=True)
                            ins.then_inc(S("spatial_done"), 1)
                    for h in range(2):
                        b = banks[4 * h:4 * h + 4]
                        pe.wait_ge(S("ab_masked"), 12 * m + 6 * h + 6)
                        pe.wait_ge(S("DmT_made"), of_half(m + 1, h))
                        four(b[0], DmT[h], Dm[h], f"n_sq{h}")
                        four(b[1], Dm[h], DmT[h], f"n_sq{h}")
                    for h in range(2):
                        b = banks[4 * h:4 * h + 4]
                        pe.wait_ge(S(f"sq_made{h}"), 5 * m + 2)
                        pe.wait_ge(S("akv_made"), of_half(m + 1, h))
                        if m:
                            pe.wait_ge(S("s_mixed"), h + 1)
                        four(b[2], D2T[h], D2[h], f"n_sq{h}")
                        four(b[3], D2[h], D2T[h], f"n_sq{h}")
                        pe.wait_ge(S("Z_first"), of_half(m + 1, h))
                        four(b[0], D2[h], Zt[h], "z_t")
                    for h in range(2):
                        b = banks[4 * h:4 * h + 4]
                        pe.wait_ge(S(f"sq_made{h}"), 5 * m + 4)
                        four(b[1], D4T[h], D4[h], f"n_sq{h}")
                        pe.wait_ge(S("Z_made"), of_half(5 * m + 1, h))
                        four(b[2], D4[h], Zt[h], "z_t")
                    if m:
                        state_part(1, (banks[0], banks[4]))
                    for h in range(2):
                        b = banks[4 * h:4 * h + 4]
                        pe.wait_ge(S(f"sq_made{h}"), 5 * m + 5)
                        pe.wait_ge(S("Z_made"), of_half(5 * m + 2, h))
                        four(b[3], D2[h], Zt[h], "z_t")
                    if m == 0:
                        pe.wait_ge(S("s_squared"), 1)
                        for f in range(4):
                            ins = mm(banks[0][:, 0:T], ones[:, :], s_sq[:, f, :], start=f == 0, stop=f == 3)
                        ins.then_inc(S("s_var"), 1)
                    for r_, (mask, bt, bx, bz) in enumerate(((M32, 1, 0, 2), (M64, 0, 3, 1))):
                        for h in range(2):
                            b = banks[4 * h:4 * h + 4]
                            pe.wait_ge(S("Z_made"), of_half(5 * m + 3 + r_, h))
                            if m == 0 and h == 0:
                                pe.wait_ge(S("s_root"), 1)
                            if m and r_ == 0:
                                pe.wait_ge(S("S_made"), 2)
                            four(b[bx], mask[h], Zt[h], "x_t")
                            for u in range(4):
                                ins = nc.tensor.transpose(b[bt][:, u * P:(u + 1) * P], Zt[h][:, u, :], ident)
                            ins.then_inc(S("t_t"), 1)
                        for h in range(2):
                            b = banks[4 * h:4 * h + 4]
                            pe.wait_ge(S("t_made"), of_half(2 * m + r_ + 1, h))
                            pe.wait_ge(S("x_made"), of_half(2 * m + r_ + 1, h))
                            four(b[bz], Tt[h], Xa[h], "z_t")
                    if m == 0:
                        pe.wait_ge(S("s_normed"), 4)
                        for i in range(2):
                            pe.wait_ge(S("Z_made"), of_half(4, i))
                            for f in range(4):
                                ins = nc.tensor.transpose(banks[4 * i + 2][:, f * P:(f + 1) * P],
                                                          zz[:, 18 + f, 1 + i * P:1 + (i + 1) * P], ident)
                            ins.then_inc(S("s_tok_t"), 1)
                    for h in range(2):
                        b = banks[4 * h:4 * h + 4]
                        pe.wait_ge(S("Z_made"), of_half(5 * m + 5, h))
                        if m == 0:
                            pe.wait_ge(S("s_tok_made"), h + 1)
                        for u, c, po, hd in heads_of(h):
                            ins = mm(b[2][:, u * P:(u + 1) * P], Zt[h][:, u, :], TM[m][:, 3:5, hd * HD:(hd + 1) * HD],
                                     start=True, stop=True)
                        ins.then_inc(S("hg_t"), 1)
                    for h in range(2):
                        b = banks[4 * h:4 * h + 4]
                        pe.wait_ge(S("hg_made"), of_half(m + 1, h))
                        for u, c, po, hd in heads_of(h):
                            ins = mm(b[3][po:po + 64, (u // 2) * P:(u // 2 + 1) * P], HG[h][:, u, 0:CH],
                                     AM[h][:, u, P:2 * P], start=True, stop=True)
                        ins.then_inc(S("q_t"), 1)
                        for u, c, po, hd in heads_of(h):
                            o = b[0][po:po + 64, (u // 2) * P:(u // 2 + 1) * P]
                            mm(o, HG[h][:, u, CH:2 * CH], AM[h][:, u, P:2 * P], start=True, stop=False)
                            ins = mm(o, TM[m][:, 0, hd * HD:(hd + 1) * HD], AM[h][:, u, 3 * P:4 * P], start=False, stop=True)
                        ins.then_inc(S("y_t"), 1)
                        for c2 in range(2):
                            if 2 * m + c2 == NC - 1:
                                continue
                            r = slice(64 * c2, 64 * c2 + 64)
                            for u, c, po, hd in heads_of(h):
                                col = (u // 2) * CH
                                hc = slice(hd * HD, (hd + 1) * HD)
                                mm(b[1 + c2][po:po + 64, col:col + CH], HG[h][r, u, 0:CH], TM[m][r, 1, hc],
                                   start=True, stop=True)
                                o = b[1 + c2][po:po + 64, P + col:P + col + CH]
                                mm(o, TM[m][r, 1, hc], HG[h][r, u, CH:2 * CH], start=True, stop=False)
                                ins = mm(o, TM[m][r, 2, hc], TM[m][r, 0, hc], start=False, stop=True)
                            ins.then_inc(S(f"e_t{h}"), 1)
                for h in range(2):
                    pe.wait_ge(S(f"EF_made{h}"), 6)
                    pe.wait_ge(S("Q_made"), of_half(2, h))
                    pe.wait_ge(S("y_done"), of_half(2, h))
                state_part(2, mix[0:2])
                for n in range(3):
                    pe.wait_ge(S("S_made"), n + 1)
                    for po in range(2):
                        r = slice(64 * po, 64 * po + 64)
                        t0 = (n + 1) * CH
                        for c in range(CT):
                            ins = mm(YSB[n][po][r, c * CH:(c + 1) * CH], St[r, n, c, :],
                                     AR[r, c, t0 // P, 1, t0 % P:t0 % P + CH], start=True, stop=True)
                    ins.then_inc(S("ys_t"), 1)
                pe.wait_ge(S("y_complete"), 1)
                for c in range(2):
                    mm(mix[3 * c][:, :], cc("head_ones"), Yc[:, 2 * c:2 * c + 2, :], start=True, stop=True
                       ).then_inc(S("y_mean"), 1)
                pe.wait_ge(S("u_used"), 1)
                early_part(3, 0, 0)
                pe.wait_ge(S("y_squared"), 1)
                for c in range(CT):
                    ins = mm(mix[0][32 * c:32 * c + 32, 0:T], cc("pick"), ysq[:, c, :], start=True, stop=True)
                ins.then_inc(S("y_var"), 1)
                early_part(3, 0, 1)
                pe.wait_ge(S("y_inv"), 1)
                for c in range(2):
                    for a in range(2):
                        ins = mm(mix[3 * c][:, a * T:(a + 1) * T], cc("spread")[:, (2 * c + a) * P:(2 * c + a + 1) * P],
                                 yst[:, 1, :], start=True, stop=True)
                    ins.then_inc(S("y_spread"), 1)
                pe.wait_ge(S("gate_in"), 1)
                for c in range(2):
                    for a in range(2):
                        ins = mm(mix[1 + c][:, a * T:(a + 1) * T], wgate[:, (2 * c + a) * P:(2 * c + a + 1) * P], sgx[:, :],
                                 start=True, stop=True)
                    ins.then_inc(S("gate_up"), 1)
                early_part(3, 1, 0)
                early_part(3, 1, 1)
                pe.wait_ge(S("y_lo_done"), 2)
                pe.wait_ge(S("u_used"), 1)

            def rot(k):
                f = 2 * (0, 2, 3, 4, 5)[k]
                pe.wait_ge(S("swap_made"), 2)
                pe.wait_ge(S("qkv_biased"), f + 2)
                if k == 4:
                    pe.wait_ge(S("rot_used"), 1)
                elif k >= 2:
                    pe.wait_ge(S("evacuated"), steps_to(8) + k + 1)
                mm(ROT_BANK[k][:, :], swap[:, 1 if k == 0 else 0, :], qz[:, f:f + 2, :], start=True, stop=True
                   ).then_inc(S("rot_t"), 1)

            def q_sums(c):
                for m in range(2):
                    ins = mm(mix[0][:, m * QH + 2 * c:m * QH + 2 * c + 2], qsq[:, 2 + c, m * P:(m + 1) * P],
                             cc("pick")[:, 0:2], start=True, stop=True)
                return ins

            def during_qkv(j):
                if j == 3:
                    pe.wait_ge(S("qkv_biased"), 4)
                    for m in range(2):
                        for c in range(2):
                            ins = nc.tensor.transpose(mix[3][:, (2 * m + c) * P:(2 * m + c + 1) * P],
                                                      qz[:, 2 + c, m * P:(m + 1) * P], ident)
                    ins.then_inc(S("v_t"), 1)
                    rot(0)
                    for c in range(2):
                        ins = mm(mix[0][32 * c:32 * c + 32, T:2 * T], cc("pick"), qsq[:, c, :], start=True, stop=True)
                    ins.then_inc(S("k_sums"), 1)
                if j == 5:
                    rot(1)

            def attention():
                pe.wait_ge(S("rk_made"), 1)
                pe.wait_ge(S("v_tok_made"), 1)
                for c in range(2):
                    ins = mm(mix[3][:, c * T:(c + 1) * T], cc("spread")[0:64, c * P:(c + 1) * P], rk[0:64, 1, :],
                             start=True, stop=True)
                ins.then_inc(S("rk_spread"), 1)
                for k in range(1, 5):
                    if k > 1:
                        rot(k)
                    pe.wait_ge(S("q_squared"), k + 1)
                    q_sums(2 * k - 2)
                    ins = q_sums(2 * k - 1)
                ins.then_inc(S("q_sums"), 1)
                pe.wait_ge(S("k_scaled"), 1)
                pe.wait_ge(S("roped"), 2)
                pe.wait_ge(S("evacuated"), steps_to(9))

                def scores(g):
                    n, c = round_of(g)
                    if g >= 2:
                        pe.wait_ge(S("masked"), 2 * g - 2)
                    for p in range(2):
                        r = slice(64 * p, 64 * p + 64)
                        for i in range(2):
                            ins = mm(mix[2 - 2 * (g % 2) + p][:, i * T:i * T + P * (n + 1)], qr[r, c + i, n * P:(n + 1) * P],
                                     qr[r, 8 + c // 4, 0:P * (n + 1)], start=True, stop=True)
                        ins.then_inc(S("scores_t"), 1)

                def transposes(g):
                    (n, _), s4 = round_of(g), g % NSC
                    for i in range(2):
                        pe.wait_ge(S("p_made"), 2 * g + i + 1)
                        for p in range(2):
                            for k in range(n + 1):
                                ins = nc.tensor.transpose(lin[i][:, (2 * p + k) * P:(2 * p + k + 1) * P],
                                                          sc[:, s4, i, p, k * P:(k + 1) * P], ident)
                        ins.then_inc(S("p_t"), 1)

                def values(g):
                    n, c = round_of(g)
                    if g >= 2:
                        pe.wait_ge(S("o_lo_done"), g - 1)
                    for i in range(2):
                        pe.wait_ge(S("pT_made"), 2 * g + i + 1)
                        for p in range(2):
                            kv = 2 * (c // 4) + p
                            for k in range(n + 1):
                                ins = mm(lin[2 + g % 2][64 * p:64 * p + 64, i * P:(i + 1) * P],
                                         v_tok[:, k, kv * HD:(kv + 1) * HD],
                                         pT[:, i, p, k, :], start=k == 0, stop=k == n)
                    ins.then_inc(S("pv"), 1)

                scores(0)
                pe.wait_ge(S("roped"), 5)
                pe.wait_ge(S("rot_used"), 5)
                pe.wait_ge(S("rq_root"), 1)
                scores(1)
                for g in range(ROUNDS):
                    if g + 2 < ROUNDS:
                        scores(g + 2)
                    if g == ROUNDS - 2:
                        pe.wait_ge(S("o_lo_done"), PART[9][1])
                        pe.wait_ge(S("masked"), 2 * ROUNDS)
                        early_part(9, 0, 0)
                        early_part(9, 0, 1)
                    transposes(g)
                    if g >= ROUNDS - 2:
                        early_part(9, 1, g - ROUNDS + 2)
                    values(g)
                pe.wait_ge(S("o_lo_done"), ROUNDS)

            pe.wait_ge(S("setup"), 1)
            for n, (name, steps, tiles, inst) in enumerate(LINEARS):
                if n in PART:
                    k0, k1 = PART[n]
                    for j in range(2):
                        for s in range(2):
                            part(n, j, s, *((0, k0) if k0 else (k1, KD)))
                        if n - 1 in NORM_NO and j == 0:
                            stats(NORM_NO[n - 1])
                else:
                    step(n, 0, 0)
                    if n - 1 in NORM_NO:
                        stats(NORM_NO[n - 1])
                    step(n, 1, 1)
                if name == "w_in":
                    for j in range(2, steps):
                        step(n, j, j)
                        during_w_in(j)
                    rwkv_gmlp()
                elif name == "down":
                    rounds(pe, 2, steps, lambda j, q, i: step(n, j, q, i))
                elif name == "qkv":
                    for j in range(2, steps):
                        step(n, j, j)
                        during_qkv(j)
                    attention()
                else:
                    rounds(pe, 2, steps, lambda j, q, i: step(n, j, q, i))


def v3(bank):
    return bank[:, :].rearrange("p (u t) -> p u t", u=4)


def of_half(v, h):
    return 2 * v - 1 + h


def tok4(AR, which):
    return AR[:, :, :, which, :]


def constants():
    import numpy as np
    c = np.zeros((P, NCON), np.float32)

    def put(name, a):
        c[:, CCOLS[name][0]:CCOLS[name][0] + CCOLS[name][1]] = a

    i, j = np.arange(P)[:, None], np.arange(P)[None, :]
    put("ident", i == j)
    put("head_ones", i // HD == j // HD)
    swap = np.zeros((P, P))
    for f in range(P):
        if f % HD < HD // 2:
            swap[f + HD // 2, f] = -1
        else:
            swap[f - HD // 2, f] = 1
    put("rope_swap", swap)
    same = i // CH == j // CH
    put("mask_pair", np.concatenate([same & (i < j), same & (i <= j)] * 2, 1))
    put("mask16", (i // 16 == j // 16) & (i > j))
    put("mask16T", (i // 16 == j // 16) & (i < j))
    put("mask32", (i // 32 == j // 32) & (i // 16 > j // 16))
    put("mask64", (i // 64 == j // 64) & (i // 32 > j // 32))
    put("causal", i <= j)
    put("window", np.where(np.concatenate([j > i, j <= i], 1), 0.0, -1e30))
    put("restart", (np.arange(T)[None, :] % CH != 0) * np.ones((P, 1)))
    put("ident64", i % CH == np.arange(CH)[None, :])
    pick = np.zeros((P, 32))
    pick[:HD, 0] = 1
    pick[HD:, 1] = 1
    put("pick", pick)
    spread = np.zeros((P, CT, P))
    for t in range(CT):
        spread[32 * t, t, :HD] = 1
        spread[32 * t + 1, t, HD:] = 1
    put("spread", spread.reshape(P, CT * P))
    return c


def kernel(x, positions, ffn1_norm, ffn1_w_gate, ffn1_w_up, ffn1_w_down, mix_norm,
           ffn2_norm, ffn2_w_gate, ffn2_w_up, ffn2_w_down,
           ab_w_in, ab_mu_shift, rwkv_w0, rwkv_w_decay_up, rwkv_a0, rwkv_w_aaa_up, rwkv_w_gate_up,
           rwkv_k_k, rwkv_k_a, rwkv_r_k, rwkv_gn_gain, rwkv_gn_bias,
           sg_ln_gain, sg_ln_bias, sg_w_spatial, sg_b_spatial, ab_w_out,
           attn_w_qkv, attn_b_qkv, attn_q_norm, attn_k_norm, attn_sinks, attn_w_o, attn_b_o):
    import numpy as np
    import concourse.bacc as bacc
    from concourse.bass_utils import run_bass_kernel_spmd

    A = np.asarray

    def tiles(w, n_tile):
        w = A(w)
        K, N = w.shape
        return w.reshape(K // P, P, N // n_tile, n_tile).transpose(2, 1, 0, 3)

    def pairs(w):
        t = tiles(w, P)
        n = t.shape[0]
        return t.reshape(n // 2, 2, P, KD, P).transpose(0, 2, 1, 3, 4).reshape(n // 2, P, 2 * KD * P)

    def feature(v):
        return A(v).reshape(-1, P).T

    gu = []
    for wg, wu in ((ffn1_w_gate[0], ffn1_w_up[0]), (ffn2_w_gate[0], ffn2_w_up[0]),
                   (ffn1_w_gate[1], ffn1_w_up[1]), (ffn2_w_gate[1], ffn2_w_up[1])):
        g, u = tiles(wg, P), tiles(wu, P)
        gu.append(np.stack([g, u], 2).reshape(KF, P, 2 * KD * P))
    down = [tiles(w, P).reshape(KD, P, KF * P)
            for w in (ffn1_w_down[0], ffn2_w_down[0], ffn1_w_down[1], ffn2_w_down[1])]
    w_in = A(ab_w_in[0])
    w_in = np.concatenate([w_in[:, f * P:(f + 2) * P] for f in W_IN_TILE], 1)
    order = [h for half in range(2) for i in range(4) for h in (8 * half + i, 8 * half + 4 + i)]
    cols = np.concatenate([np.arange(h * HD, (h + 1) * HD) for h in order])
    qcols = np.concatenate([np.arange(QH * HD, 12 * P), cols])

    par = np.zeros((P, NPAR), np.float32)

    def put(name, a):
        par[:, PCOLS[name][0]:PCOLS[name][0] + PCOLS[name][1]] = a

    for layer in range(2):
        put(f"ffn1_norm{layer}", feature(ffn1_norm[layer]))
        put(f"mix_norm{layer}", feature(mix_norm[layer]))
        put(f"ffn2_norm{layer}", feature(ffn2_norm[layer]))
    for name, v in (("mu", ab_mu_shift), ("w0", rwkv_w0), ("a0", rwkv_a0), ("k_k", rwkv_k_k), ("k_a", rwkv_k_a),
                    ("r_k", rwkv_r_k), ("gn_gain", rwkv_gn_gain), ("gn_bias", rwkv_gn_bias), ("ln_gain", sg_ln_gain),
                    ("ln_bias", sg_ln_bias), ("b_o", attn_b_o)):
        put(name, feature(A(v)[0]))
    put("b_qkv", feature(A(attn_b_qkv)[0][qcols]))
    put("q_norm", np.tile(A(attn_q_norm)[0], 2)[:, None])
    put("k_norm", np.tile(A(attn_k_norm)[0], 2)[:, None])
    put("inv_freq", np.tile((10000.0 ** (-np.arange(0, HD, 2, dtype=np.float32) / np.float32(HD))
                             ).astype(np.float32), 4)[:, None])
    put("sinks", np.broadcast_to(A(attn_sinks)[0][order], (P, QH)))

    arrays = {
        "xT": A(x)[0].T.reshape(KD, P, T).transpose(1, 0, 2),
        "gu_w": np.concatenate(gu, 0),
        "down_w": np.concatenate(down, 0),
        "w_in": pairs(w_in),
        "w_out": pairs(ab_w_out[0]),
        "w_qkv": pairs(A(attn_w_qkv[0])[:, qcols]),
        "w_o": pairs(A(attn_w_o[0])[cols, :]),
        "params": par,
        "consts": constants(),
        "positions": np.broadcast_to(A(positions), (P, T)),
        "w_lora": np.concatenate([A(rwkv_w_decay_up)[0], A(rwkv_w_aaa_up)[0]], 0),
        "w_gate": A(rwkv_w_gate_up)[0],
        "w_spatialT": A(sg_w_spatial)[0].transpose(2, 0, 1),
        "b_spatial": np.broadcast_to(A(sg_b_spatial)[0], (P, 4, P)),
    }
    nc = bacc.Bacc("TRN2", target_bir_lowering=False, num_devices=1)
    args, ins = {}, {}
    for name, a in arrays.items():
        a = np.ascontiguousarray(a)
        ins[f"in_{name}"] = a
        args[name] = nc.dram_tensor(f"in_{name}", a.shape, mybir.dt.from_np(a.dtype), kind="ExternalInput").ap()
    args["out"] = nc.dram_tensor("out_x", (P, KD, T), F32, kind="ExternalOutput").ap()
    build(nc, **args)
    r = run_bass_kernel_spmd(nc, [ins], core_ids=[0])
    got = r.results[0]["out_x"]
    return got.transpose(1, 0, 2).reshape(D, T).T.reshape(1, T, D)
```
